# Optimizing a Trainium2 kernel written in Bass

```python
import math
import jax, jax.numpy as jnp
from jax import lax
import numpy as np

D_MODEL = 1024
BATCH = 1
SEQ = 1024
DEPTH = 2
DEC_BATCH = 8
DEC_SEQ = 1
PAST_LEN = 2048
PAGE_SIZE = 128

N_A = DEPTH // 2
N_B = DEPTH - N_A
GLA_HEADS = 4
GLA_DK = D_MODEL // 2 // GLA_HEADS
GLA_DV = (3 * D_MODEL // 4) // GLA_HEADS
GLA_QK = GLA_HEADS * GLA_DK
GLA_V = GLA_HEADS * GLA_DV
GLA_RANK = 16
GLA_TAU = 16.0
GLA_CHUNK = 64
HEAD_DIM = 64
DIL_KV_HEADS = 4
DIL_PAIRS = ((128, 1), (512, 4), (2048, 16))
N_GROUPS = len(DIL_PAIRS)
WIN_MAX = max(w for w, _ in DIL_PAIRS)
B_Q = N_GROUPS * DIL_KV_HEADS * HEAD_DIM
B_KV = DIL_KV_HEADS * HEAD_DIM
MEM_TOKENS = 256
MEM_HEADS = 4
MEM_Q = MEM_HEADS * HEAD_DIM
A_SPLITS = [GLA_QK, 2 * GLA_QK, 2 * GLA_QK + GLA_V, 2 * GLA_QK + 2 * GLA_V,
            2 * GLA_QK + 2 * GLA_V + GLA_RANK]
A_IN = 2 * GLA_QK + 2 * GLA_V + GLA_RANK + MEM_Q
A_OUT = GLA_V + MEM_Q
B_IN = B_Q + MEM_Q
B_OUT = B_KV + MEM_Q
D_FF = -(-8 * D_MODEL // (3 * 256)) * 256
ROPE_THETA = 10000.0
EPS = 1e-6
ATTN_SCALE = HEAD_DIM ** -0.5

kernel_name = "yoco_gla_dilated_window_decoder_step"

def rms_norm(x, g):
    xf = x.astype(jnp.float32)
    y = xf * lax.rsqrt(jnp.mean(xf * xf, axis=-1, keepdims=True) + EPS)
    return (y * g.astype(jnp.float32)).astype(x.dtype)

def rope(x, pos):
    half = x.shape[-1] // 2
    inv = ROPE_THETA ** (-jnp.arange(half, dtype=jnp.float32) / half)
    ang = pos.astype(jnp.float32)[:, None] * inv[None, :]
    cos = jnp.cos(ang)[None, :, None, :]
    sin = jnp.sin(ang)[None, :, None, :]
    xf = x.astype(jnp.float32)
    x1, x2 = xf[..., :half], xf[..., half:]
    return jnp.concatenate([x1 * cos - x2 * sin, x2 * cos + x1 * sin], axis=-1).astype(x.dtype)

def swiglu(x, w_gu, w_down):
    g, u = jnp.split(x @ w_gu, 2, axis=-1)
    return (jax.nn.silu(g) * u) @ w_down

def gla_chunked(q, k, v, log_a, h0):
    Bn, T, H, DK = q.shape
    DV = v.shape[-1]
    C = GLA_CHUNK if T >= GLA_CHUNK else T
    pad = (-T) % C
    q, k, v, log_a = [t.astype(jnp.float32) for t in (q, k, v, log_a)]
    if pad:
        pw = ((0, 0), (0, pad), (0, 0), (0, 0))
        q, k, v, log_a = [jnp.pad(t, pw) for t in (q, k, v, log_a)]
    nc = (T + pad) // C

    def to_chunks(t):
        return jnp.moveaxis(t.reshape(Bn, nc, C, *t.shape[2:]), 1, 0)

    causal = jnp.asarray(np.tril(np.ones((C, C), dtype=bool)))[None, :, :, None, None]

    def step(h, inp):
        qc, kc, vc, ac = inp
        b = jnp.cumsum(ac, axis=1)
        diff = b[:, :, None] - b[:, None, :]
        decay = jnp.exp(jnp.where(causal, diff, -jnp.inf))
        scores = jnp.einsum('bihd,bjhd,bijhd->bhij', qc, kc, decay)
        o = (jnp.einsum('bhij,bjhe->bihe', scores, vc)
             + jnp.einsum('bihd,bhde->bihe', qc * jnp.exp(b), h))
        b_last = b[:, -1]
        k_dec = kc * jnp.exp(b_last[:, None] - b)
        h_new = jnp.exp(b_last)[..., None] * h + jnp.einsum('bjhd,bjhe->bhde', k_dec, vc)
        return h_new, o

    h_T, o = lax.scan(step, h0.astype(jnp.float32), tuple(to_chunks(t) for t in (q, k, v, log_a)))
    o = jnp.moveaxis(o, 0, 1).reshape(Bn, nc * C, H, DV)[:, :T]
    return o, h_T.astype(h0.dtype)

def dilated_band_attn(q, k, v, dil, n_keys):
    Bn, S, H, Dh = q.shape
    n = n_keys
    L = S // dil
    nb = -(-L // n)
    Lp = nb * n

    def resid(t):
        t = jnp.swapaxes(t.reshape(Bn, L, dil, H, Dh), 1, 2)
        t = jnp.pad(t, ((0, 0), (0, 0), (0, Lp - L), (0, 0), (0, 0)))
        return t.reshape(Bn, dil, nb, n, H, Dh)

    qb, kb, vb = resid(q), resid(k), resid(v)

    def with_prev(t):
        prev = jnp.pad(t, ((0, 0), (0, 0), (1, 0), (0, 0), (0, 0), (0, 0)))[:, :, :-1]
        return jnp.concatenate([prev, t], axis=3)

    kk, vv = with_prev(kb), with_prev(vb)
    i = np.arange(n)[:, None]
    j = np.arange(2 * n)[None, :]
    dist = i + n - j
    local = (dist >= 0) & (dist <= n)
    blk = np.arange(nb)[:, None, None]
    valid = jnp.asarray(local[None] & ~((blk == 0) & (j[None] < n)))
    s = jnp.einsum('brnqhd,brnkhd->brnhqk', qb, kk, preferred_element_type=jnp.float32) * ATTN_SCALE
    s = jnp.where(valid[None, None, :, None], s, -jnp.inf)
    m = jnp.max(s, axis=-1, keepdims=True)
    p = jnp.exp(s - m)
    l = jnp.sum(p, axis=-1)
    o = jnp.einsum('brnhqk,brnkhd->brnqhd', p, vv.astype(jnp.float32))
    o = o / jnp.swapaxes(l, 3, 4)[..., None]
    lse = jnp.swapaxes(m[..., 0] + jnp.log(l), 3, 4)

    def back(t):
        t = t.reshape(Bn, dil, Lp, *t.shape[4:])[:, :, :L]
        t = jnp.swapaxes(t, 1, 2)
        return t.reshape(Bn, S, *t.shape[3:])

    return back(o), back(lse)

def dilated_gather_attn(q, kbuf, vbuf, dil, n_keys):
    T = q.shape[1]
    Lb = kbuf.shape[1] - T
    idx = Lb + np.arange(T)[:, None] - dil * np.arange(n_keys + 1)[None, :]
    valid = jnp.asarray(idx >= 0)
    idx = np.maximum(idx, 0)
    kg = kbuf[:, idx]
    vg = vbuf[:, idx]
    s = jnp.einsum('bthd,btjhd->bthj', q, kg, preferred_element_type=jnp.float32) * ATTN_SCALE
    s = jnp.where(valid[None, :, None, :], s, -jnp.inf)
    m = jnp.max(s, axis=-1, keepdims=True)
    p = jnp.exp(s - m)
    l = jnp.sum(p, axis=-1)
    o = jnp.einsum('bthj,btjhd->bthd', p, vg.astype(jnp.float32)) / l[..., None]
    return o, m[..., 0] + jnp.log(l)

def mem_kv(mem, g_norm, w_mem_kv, g_mk):
    Bn, M, _ = mem.shape
    mk, mv = jnp.split(rms_norm(mem, g_norm) @ w_mem_kv, 2, axis=-1)
    mk = rms_norm(mk.reshape(Bn, M, MEM_HEADS, HEAD_DIM), g_mk)
    return mk, mv.reshape(Bn, M, MEM_HEADS, HEAD_DIM)

def mem_attend(mq, g_mq, mk, mv):
    Bn, T, _ = mq.shape
    q = rms_norm(mq.reshape(Bn, T, MEM_HEADS, HEAD_DIM), g_mq)
    s = jnp.einsum('bthd,bmhd->bhtm', q, mk, preferred_element_type=jnp.float32) * ATTN_SCALE
    p = jax.nn.softmax(s, axis=-1)
    o = jnp.einsum('bhtm,bmhd->bthd', p, mv.astype(jnp.float32))
    return o.reshape(Bn, T, MEM_Q)

def shared_kv(h, kv_norm, w_kv, g_k, pos):
    Bn, T, _ = h.shape
    k, v = jnp.split(rms_norm(h, kv_norm) @ w_kv, 2, axis=-1)
    k = rope(rms_norm(k.reshape(Bn, T, DIL_KV_HEADS, HEAD_DIM), g_k), pos)
    return k, v.reshape(Bn, T, DIL_KV_HEADS, HEAD_DIM)

def trunk(x, pos, gla_h0, mem_k, mem_v, win_k, win_v,
          norm1, norm2, a_w_in, a_w_gate2, a_b_gate, a_g_onorm, a_w_out,
          kv_norm, w_kv, g_k, b_w_in, b_g_q, b_w_out, g_mem_q, w_ffn_gu, w_ffn_down):
    Bn, T, _ = x.shape
    h = x
    gla_states = []
    k_sh = v_sh = kbuf = vbuf = None
    for li in range(DEPTH):
        hn = rms_norm(h, norm1[li])
        if li < N_A:
            q, k, v, g, glr, mq = jnp.split(hn @ a_w_in[li], A_SPLITS, axis=-1)
            log_a = jax.nn.log_sigmoid((glr @ a_w_gate2[li] + a_b_gate[li]).astype(jnp.float32)) / GLA_TAU
            o, h_T = gla_chunked(
                (q * GLA_DK ** -0.5).reshape(Bn, T, GLA_HEADS, GLA_DK),
                k.reshape(Bn, T, GLA_HEADS, GLA_DK),
                v.reshape(Bn, T, GLA_HEADS, GLA_DV),
                log_a.reshape(Bn, T, GLA_HEADS, GLA_DK),
                gla_h0[li])
            gla_states.append(h_T)
            o = rms_norm(o, a_g_onorm[li]).astype(h.dtype) * jax.nn.silu(g.reshape(Bn, T, GLA_HEADS, GLA_DV))
            tok = o.reshape(Bn, T, GLA_V)
            w_out = a_w_out[li]
        else:
            bi = li - N_A
            qd, mq = jnp.split(hn @ b_w_in[bi], [B_Q], axis=-1)
            qd = rope(rms_norm(qd.reshape(Bn, T, N_GROUPS * DIL_KV_HEADS, HEAD_DIM), b_g_q[bi]), pos)
            qd = qd.reshape(Bn, T, N_GROUPS, DIL_KV_HEADS, HEAD_DIM)
            outs, lses = [], []
            for gi, (win, dil) in enumerate(DIL_PAIRS):
                if win_k is None:
                    o_g, l_g = dilated_band_attn(qd[:, :, gi], k_sh, v_sh, dil, win // dil)
                else:
                    o_g, l_g = dilated_gather_attn(qd[:, :, gi], kbuf, vbuf, dil, win // dil)
                outs.append(o_g)
                lses.append(l_g)
            wts = jax.nn.softmax(jnp.stack(lses, 0), axis=0)
            o = jnp.einsum('gbth,gbthd->bthd', wts, jnp.stack(outs, 0))
            tok = o.reshape(Bn, T, B_KV).astype(h.dtype)
            w_out = b_w_out[bi]
        mem_o = mem_attend(mq, g_mem_q[li], mem_k[li], mem_v[li]).astype(h.dtype)
        h = h + jnp.concatenate([tok, mem_o], axis=-1) @ w_out
        h = h + swiglu(rms_norm(h, norm2[li]), w_ffn_gu[li], w_ffn_down[li])
        if li == N_A - 1:
            k_sh, v_sh = shared_kv(h, kv_norm, w_kv, g_k, pos)
            if win_k is not None:
                kbuf = jnp.concatenate([win_k, k_sh.astype(win_k.dtype)], axis=1)
                vbuf = jnp.concatenate([win_v, v_sh.astype(win_v.dtype)], axis=1)
    return h, jnp.stack(gla_states, 0), k_sh, v_sh

def setup_inputs(seed: int = 0) -> dict:
    key = jax.random.key(seed)
    ks = iter(jax.random.split(key, 32))

    def nrm(shape, scale):
        return jax.random.normal(next(ks), shape, jnp.float32) * scale

    def gain(shape):
        return 1.0 + nrm(shape, 0.05)

    win_rows = min(WIN_MAX, PAST_LEN)
    return {
        "x_prompt": nrm((BATCH, SEQ, D_MODEL), 1.0),
        "x_sample": nrm((DEC_BATCH, DEC_SEQ, D_MODEL), 1.0),
        "state_gla": nrm((N_A, DEC_BATCH, GLA_HEADS, GLA_DK, GLA_DV), 0.5),
        "cache_win_k": nrm((DEC_BATCH, win_rows, DIL_KV_HEADS, HEAD_DIM), 1.0),
        "cache_win_v": nrm((DEC_BATCH, win_rows, DIL_KV_HEADS, HEAD_DIM), 1.0),
        "cache_mem_k": nrm((DEPTH, DEC_BATCH, MEM_TOKENS, MEM_HEADS, HEAD_DIM), 1.0),
        "cache_mem_v": nrm((DEPTH, DEC_BATCH, MEM_TOKENS, MEM_HEADS, HEAD_DIM), 1.0),
        "mem_prompt": nrm((BATCH, MEM_TOKENS, D_MODEL), 1.0),
        "norm1": gain((DEPTH, D_MODEL)),
        "norm2": gain((DEPTH, D_MODEL)),
        "a_w_in": nrm((N_A, D_MODEL, A_IN), D_MODEL ** -0.5),
        "a_w_gate2": nrm((N_A, GLA_RANK, GLA_QK), GLA_RANK ** -0.5),
        "a_b_gate": nrm((N_A, GLA_QK), 0.1),
        "a_g_onorm": gain((N_A, GLA_DV)),
        "a_w_out": nrm((N_A, A_OUT, D_MODEL), A_OUT ** -0.5),
        "kv_norm": gain((D_MODEL,)),
        "w_kv": nrm((D_MODEL, 2 * B_KV), D_MODEL ** -0.5),
        "g_k": gain((HEAD_DIM,)),
        "b_w_in": nrm((N_B, D_MODEL, B_IN), D_MODEL ** -0.5),
        "b_g_q": gain((N_B, HEAD_DIM)),
        "b_w_out": nrm((N_B, B_OUT, D_MODEL), B_OUT ** -0.5),
        "mem_norm": gain((DEPTH, D_MODEL)),
        "w_mem_kv": nrm((DEPTH, D_MODEL, 2 * MEM_Q), D_MODEL ** -0.5),
        "g_mem_q": gain((DEPTH, HEAD_DIM)),
        "g_mem_k": gain((DEPTH, HEAD_DIM)),
        "w_ffn_gu": nrm((DEPTH, D_MODEL, 2 * D_FF), D_MODEL ** -0.5),
        "w_ffn_down": nrm((DEPTH, D_FF, D_MODEL), D_FF ** -0.5),
    }

def reference(x_prompt, x_sample, state_gla, cache_win_k, cache_win_v, cache_mem_k, cache_mem_v,
              mem_prompt, norm1, norm2, a_w_in, a_w_gate2, a_b_gate, a_g_onorm, a_w_out,
              kv_norm, w_kv, g_k, b_w_in, b_g_q, b_w_out, mem_norm, w_mem_kv, g_mem_q, g_mem_k,
              w_ffn_gu, w_ffn_down):
    weights = (norm1, norm2, a_w_in, a_w_gate2, a_b_gate, a_g_onorm, a_w_out,
               kv_norm, w_kv, g_k, b_w_in, b_g_q, b_w_out, g_mem_q, w_ffn_gu, w_ffn_down)

    mks, mvs = [], []
    for li in range(DEPTH):
        mk, mv = mem_kv(mem_prompt, mem_norm[li], w_mem_kv[li], g_mem_k[li])
        mks.append(mk)
        mvs.append(mv)
    mem_k_p = jnp.stack(mks, 0)
    mem_v_p = jnp.stack(mvs, 0)
    h0_p = jnp.zeros((N_A, x_prompt.shape[0], GLA_HEADS, GLA_DK, GLA_DV), x_prompt.dtype)
    pos_p = jnp.arange(x_prompt.shape[1], dtype=jnp.int32)
    y_prompt, gla_p, k_p, v_p = trunk(x_prompt, pos_p, h0_p, mem_k_p, mem_v_p, None, None, *weights)
    keep = min(WIN_MAX, x_prompt.shape[1])
    win_k_p = k_p[:, -keep:]
    win_v_p = v_p[:, -keep:]

    pos_s = PAST_LEN + jnp.arange(x_sample.shape[1], dtype=jnp.int32)
    y_sample, gla_s, k_s, v_s = trunk(x_sample, pos_s, state_gla, cache_mem_k, cache_mem_v,
                                      cache_win_k, cache_win_v, *weights)
    return (y_prompt, y_sample, gla_p, gla_s, win_k_p, win_v_p, k_s, v_s, mem_k_p, mem_v_p)


_drawn_inputs = setup_inputs


def setup_inputs(seed=0):
    import zlib

    import numpy as np

    out = dict(_drawn_inputs(seed))
    spreads = {}
    factors = {'b_g_q': 8.0, 'g_mem_q': 8.0}
    for name, (base, spread) in spreads.items():
        noise = np.random.default_rng([zlib.crc32(name.encode()), seed]).standard_normal(out[name].shape)
        drawn = base * np.exp(spread * noise) if base else spread * noise
        out[name] = __import__('jax').numpy.asarray(drawn.astype(out[name].dtype))
    for name, factor in factors.items():
        out[name] = (out[name] * factor).astype(out[name].dtype)
    return out
```

```python
from contextlib import ExitStack

import numpy as np

import concourse.bass as bass
from concourse import mybir

F32 = mybir.dt.float32
F32R = mybir.dt.float32r
BF16 = mybir.dt.bfloat16
U8 = mybir.dt.uint8
ACT = mybir.ActivationFunctionType
ALU = mybir.AluOpType
AX = mybir.AxisListType

P = 128
D = 1024
KT = D // P
SEQ, NB = 1024, 8
T = SEQ + NB
CH = T // 3
NCH = 3
MEM = 256
HD = 64
H = 4
DV = 192
NBLK = SEQ // P
FF = 2816
JFF = FF // (2 * P)
EPS = 1e-6
WSLOT = 3
NWIN = 129
GROUPS = ((P, 1), (512, 4), (2048, 16))

A_Q, A_K, A_V, A_G, A_R, A_M = range(0, 4), range(4, 8), range(8, 14), range(14, 20), (20,), (21, 22)
NA_IN = 23
B_Q, B_M = range(0, 6), (6, 7)

U_MEM = 0
U_AIN = U_MEM + 8
U_AOUT = U_AIN + NA_IN
U_FFA = U_AOUT + KT
U_KV = U_FFA + 6 * JFF
U_BIN = U_KV + 4
U_BOUT = U_BIN + 8
U_FFB = U_BOUT + 4
NUNIT = U_FFB + 6 * JFF

G_N1, G_N2, G_KV, G_MN = 0, 16, 32, 40
G_MQ, G_MK, G_Q, G_K, G_ON, G_BIAS = 56, 58, 60, 61, 62, 64
NG = 68


def chunk(c):
    return slice(c * CH, (c + 1) * CH)

NCST = 1032


def tokens_of(view, g, blk):
    if g == 0:
        return view[:, blk * P:(blk + 1) * P]
    if g == 1:
        r, nb = blk % 4, blk // 4
        return view[:, r + 512 * nb:r + 512 * nb + 509:4]
    return view[:, blk:blk + SEQ - 7:8]


def tokens_of4(view, g, b):
    if g == 0:
        return view[:, 512 * b:512 * b + 512].rearrange("p (n m) -> p n m", n=4)
    if g == 1:
        return view[:, 512 * b:512 * b + 512].rearrange("p (m r) -> p r m", r=4)
    return view[:, 0:SEQ].rearrange("p (m c) -> p c m", c=8)[:, 4 * b:4 * b + 4]


def key_blocks(g, blk):
    before = {0: blk - 1 if blk >= 1 else None, 1: blk - 4 if blk >= 4 else None, 2: None}[g]
    return ([(before, True)] if before is not None else []) + [(blk, False)]


W_STEPS = [(0, range(0, 4), 0, False), (0, range(4, 8), 0, False), (0, range(1, 4), 1, True), (0, range(4, 8), 1, True),
           (1, range(0, 4), 0, False), (1, range(4, 8), 0, False), (1, range(4, 8), 4, True),
           (2, range(0, 4), 0, False), (2, range(4, 8), 0, False)]
NW = len(W_STEPS)


def trunk_program(nc, x_d, mem_d, w_d, cst_d, lvl_d, tri_d, gain_d, gate2_d, sel_d, rope_d, state_d,
                  cmk_d, cmv_d, wink_d, winv_d,
                  y_d, gstate_d, sstate_d, kwin_d, vwin_d, mk_d, mv_d):
    ctx = ExitStack()
    with ctx:
        def at(name, shape, offset, dt=F32):
            return nc.alloc_sbuf_tensor_at(name, shape, dt, offset=offset)

        def bank(i):
            return ctx.enter_context(nc.psum_tensor(f"bank{i}", [P, 512], F32))

        def sem(name):
            return ctx.enter_context(nc.semaphore(name))

        ROW = T * 4
        O_W = 16512
        w_raw = at("w_raw", [P, WSLOT, 1024], O_W)
        w_hi = at("w_hi", [P, WSLOT, 1024], O_W + 12288, F32R)
        w_lo = at("w_lo", [P, WSLOT, 1024], O_W + 24576, F32R)
        O_X = O_W + 36864
        x_hi = at("x_hi", [P, KT, T], O_X, F32R)
        x_lo = at("x_lo", [P, KT, T], O_X + KT * ROW, F32R)
        O_H = O_X + 2 * KT * ROW
        h = at("h", [P, KT, T], O_H)
        O_C = O_H + KT * ROW
        cst = at("cst", [P, NCST], O_C)
        ident, ones, head_ones = cst[:, 0:128], cst[:, 128:256], cst[:, 256:384]
        low_ones, high_ones = cst[:, 384:512], cst[:, 512:640]
        swap = cst[:, 640:768]
        smp_col = cst[0:32, 768:776]
        smp_head = cst[0:32, 776:1032].rearrange("p (t m) -> p t m", t=2)
        gain = at("gain", [P, NG], O_C + 4128)
        mk_t = at("mk_t", [P, 2, 2, MEM], O_C + 4416)
        mv_t = at("mv_t", [P, 2, 2, MEM], O_C + 8512)
        hsq = at("hsq", [P, 2, CH], O_C + 12608)
        rstd = at("rstd", [P, 2, CH], O_C + 15360)
        zero = at("zero", [P, 1], O_C + 18112)
        O_L = O_C + 18144
        sq = at("sq", [P, KT, CH], O_L)
        xt = at("xt", [P, KT, CH], O_L + 11008)
        mt = at("mt", [P, KT, MEM], O_L + 22016)
        mk_raw = at("mk_raw", [P, 2, 2, MEM], O_L + 30208)
        mv_raw = at("mv_raw", [P, 2, 2, MEM], O_L + 34304)
        mem_xt = at("mem_xt", [P, 2, KT, MEM], O_L + 38400)
        q_a = at("q_a", [P, H, T], O_L)
        k_a = at("k_a", [P, H, T], O_L + 4 * ROW)
        v_tok = at("v_tok", [P, NBLK, H * DV], O_L + 8 * ROW)
        tok_a = at("tok_a", [P, 6, T], O_L)
        g_a = at("g_a", [P, 6, T], O_L + 8 * ROW)
        mq_a = at("mq_a", [P, 2, T], O_H)
        glr = at("glr", [16, T], O_H + 2 * ROW)
        ring = at("ring", [P, 2, T], O_H + 3 * ROW)
        vs_a = at("vs_a", [NB, H * DV], O_H + 5 * ROW)
        gate2 = at("gate2", [16, 512], O_H + 5 * ROW + 3072)
        lvl = at("lvl", [P, 8, P], O_H + 5 * ROW + 9376, U8)
        lvl_raw = at("lvl_raw", [P, 8, P], O_C + 12608)
        q_b = at("q_b", [P, 6, T], O_L)
        mq_b = at("mq_b", [P, 2, T], O_L + 6 * ROW)
        tok_b = at("tok_b", [P, 2, T], O_L + 8 * ROW)
        k_b = at("k_b", [P, 2, T], O_L + 10 * ROW)
        v_b = at("v_b", [P, 2, T], O_L + 12 * ROW)
        v3 = at("v3", [P, 3, NBLK, 6 * HD], O_X)
        pw = at("pw", [P, 2, 4, P], O_C + 4416)
        m_col = at("m_col", [P, 3, H, NBLK], O_X + 36864)
        m_row = at("m_row", [H, SEQ], O_C + 8512)
        nm_row = at("nm_row", [H, SEQ], O_X + 39296, F32R)
        sel_raw = at("sel_raw", [H, H, P], O_X + 43392)
        sel = at("sel", [H, H, P], O_X + 45440, F32R)
        o_sb = at("o_sb", [P, SEQ], O_X + 47488)
        o_rl = at("o_rl", [P, SEQ], O_X + 51584)
        tri_raw = at("tri_raw", [P, 5, P], O_X + 55680)
        tri = at("tri", [P, 5, P], O_X + 58240, BF16)
        rope = at("rope", [P, 2, T], O_X + 52640)
        r_cos = at("r_cos", [P, CH], O_X + 60896)
        r_sin = at("r_sin", [P, CH], O_X + 62272)
        wk = at("wk", [P, 2, 3, NB, 130], O_X)
        wv = at("wv", [P, 3, NB, 256], O_X + 24960)
        qw_blk = at("qw_blk", [P, 3, 2, NB, 32], O_X + 49536)
        pd = at("pd", [32, 3, NWIN], O_X + 55680)
        pdt = at("pdt", [P, 3, 32], O_X + 57248)
        wst = at("wst", [32, 16], O_X + 57632)
        v_new = at("v_new", [P, 2, NB], O_X + 57696)
        hid_hi = at("hid_hi", [P, 2, T], O_L + 22016, F32R)
        hid_lo = at("hid_lo", [P, 2, T], O_L + 22016 + 2 * ROW, F32R)
        sil = at("sil", [P, NCH, CH], O_L + 22016 + 4 * ROW)
        hid = at("hid", [P, NCH, CH], O_L + 22016 + 5 * ROW)

        reset = at("reset", [P, SEQ], O_H + 5 * ROW + 5120)
        k_smp = at("k_smp", [NB, H, P], O_H + 5 * ROW + 5120)
        a_smp = at("a_smp", [P, H, NB], O_H + 5 * ROW + 9216)
        b_end = at("b_end", [P, NBLK], O_H + 5 * ROW + 9344)
        o_a = at("o_a", [P, 6, T], O_X)
        O_G = O_X + 6 * ROW
        dec = at("dec", [P, 2, SEQ], O_G)
        dqk = at("dqk", [P, 2, SEQ], O_G + 8192)
        s_acc = at("s_acc", [P, NBLK, P], O_G + 16384)
        q_dec = at("q_dec", [P, SEQ], O_G + 20480)
        k_tok = at("k_tok", [P, NBLK, P], O_G + 24576)
        st = at("st", [P, NBLK, DV], O_G + 28672)
        b_cum = at("b_cum", [P, SEQ], O_G + 34816)
        st_smp = at("st_smp", [P, H, NB, DV], O_G)
        k_one = at("k_one", [NB, H, NB, P], O_G + 24576)
        o_sq = at("o_sq", [P, 6, CH], O_G)
        o_rs = at("o_rs", [P, 6, CH], O_G + 8256)
        o_nm = at("o_nm", [P, 6, CH], O_G + 16512)
        ck = at("ck", [P, 2, NB, MEM], O_X)
        cv = at("cv", [P, 2, NB, MEM], O_X + 16384)
        q_blk = at("q_blk", [P, 2, NB, 32], O_X + 32768)
        pr = at("pr", [P, 2, H, MEM], O_X + 34816)
        pt = at("pt", [P, 2, 2 * H, P], O_X + 43008)
        dp = at("dp", [32, MEM], O_X + 51200)
        dpt = at("dpt", [P, 2, 32], O_X + 52224)
        nmax = at("nmax", [P, 2, H], O_X + 52480)
        nbias = at("nbias", [P, 2, H], O_X + 52512)
        psums = at("psums", [P, 2, H], O_X + 52544)
        rsums = at("rsums", [P, 2, H], O_X + 52576)
        dst4 = at("dst4", [32, 4], O_X + 52608)

        banks = [bank(i) for i in range(8)]
        g_spill = nc.dram_tensor("g_spill", [P, 6, T], F32, kind="Internal").ap()

        s_w = [sem(f"w_landed{i}") for i in range(WSLOT)]
        s_whi, s_wlo, s_wused = sem("w_hi_made"), sem("w_split"), sem("w_used")
        s_cst, s_gain, s_lvl_in, s_lvl, s_mem = sem("constants_landed"), sem("gains_landed"), sem("level_masks_landed"), sem("level_masks_cast"), sem("mem_landed")
        s_x = [sem(f"x_landed{c}") for c in range(NCH)]
        s_zero = sem("zero_set")
        s_sq, s_sum, s_ln, s_rs = sem("squares"), sem("square_sums"), sem("logs"), sem("rstds")
        s_xt, s_hi, s_lo = sem("normed"), sem("hi_made"), sem("split")
        s_mm = sem("products")
        s_ev = sem("evacuated")
        s_hsq, s_hsum, s_hln, s_hrs, s_hn = (sem("head_" + n) for n in ("squares", "sums", "logs", "rstds", "normed"))
        s_mvT, s_mvt = sem("mem_v_turned"), sem("mem_v_kept")
        s_vT, s_vt = sem("v_turned"), sem("v_kept")
        s_out = sem("outputs_written")
        s_spill = [sem("gate_spilled0"), sem("gate_spilled1")]
        s_res = sem("residual_added")
        s_sil, s_hid, s_hhi, s_hlo, s_up, s_down = (sem(n) for n in ("silu", "hidden", "hidden_hi", "hidden_split", "up_read", "down_added"))
        s_gate2 = sem("gate2_landed")

        s_z, s_zb, s_zt, s_la, s_rst, s_rst2, s_bc, s_as, s_be = (sem("gla_" + n) for n in (
            "gates", "gates_kept", "gate_terms", "log_decays", "ones", "resets", "cumulated", "sample_decays", "block_decays"))
        s_df, s_ex, s_mu, s_ss, s_cp, s_sz, s_kt, s_kv, s_st, s_go, s_oe = (sem("gla_" + n) for n in (
            "exponents", "decays", "decayed", "level_scores", "scores_kept", "scores_cleared", "keys_kept", "updates", "states", "outs", "outs_kept"))
        s_gst, s_sin, s_sout = sem("gla_state_written"), sem("sample_states_landed"), sem("sample_states_written")
        s_skt, s_skk, s_sk1, s_su, s_sn, s_so, s_soe = (sem("sample_" + n) for n in (
            "keys_turned", "keys_kept", "keys_apart", "updates", "states", "outs", "outs_kept"))
        s_gland, s_gsil, s_osq, s_osum, s_oln, s_ors, s_onm, s_tok, s_chi, s_clo = (sem(n) for n in (
            "gate_landed", "gate_silu", "out_squares", "out_sums", "out_logs", "out_rstds", "out_normed", "tokens_mixed", "mix_hi", "mix_split"))
        s_rope, s_rsw, s_rc, s_rs_, s_rok = (sem("rope_" + n) for n in ("landed", "swapped", "cos", "sin", "done"))
        s_tri_in, s_sel_in, s_tri, s_sel, s_ones3 = (sem(n) for n in (
            "masks_landed", "head_rows_landed", "masks_cast", "head_rows_cast", "ones_set"))
        s_v3t, s_v3 = sem("window_values_turned"), sem("window_values_kept")
        s_w1, s_m1, s_mt, s_mr, s_nm = (sem("window_" + n) for n in ("scores", "max", "max_turned", "max_rows", "max_negated"))
        s_w2, s_we, s_wo, s_woc, s_wok, s_wor, s_wod = (sem("window_" + n) for n in (
            "key_scores", "exps", "outs", "outs_copied", "outs_joined", "sums_inverted", "outs_scaled"))
        s_wc, s_wqz, s_wqb, s_wkn, s_d1, s_dm, s_db, s_de, s_dr, s_dp, s_dpn_, s_dpt_, s_dptk_, s_dn, s_dnb_, s_dvn, s_do, s_dok = (
            sem("step_window_" + n) for n in ("cache_landed", "cleared", "queries", "new_keys", "scores", "max", "bias", "exps", "sums_inverted",
                                              "probs", "new_probs", "probs_turned", "probs_kept", "new_apart", "new_spread", "new_values", "outs", "outs_kept"))
        s_h = sem("residual_landed")
        s_cache = sem("cache_landed")
        s_sc, s_mx, s_nb, s_pe, s_ra, s_pn, s_pt, s_ptk, s_po, s_pok = (sem("mem_" + n) for n in (
            "scores", "max", "bias", "exps", "sums_inverted", "probs", "probs_turned", "probs_kept", "outs", "outs_kept"))
        s_qz, s_qb, s_dsc, s_dmx, s_dnb, s_dpe, s_dra, s_dpn, s_dpt, s_dptk, s_dpo, s_dpok = (sem("step_mem_" + n) for n in (
            "cleared", "queries", "scores", "max", "bias", "exps", "sums_inverted", "probs", "probs_turned", "probs_kept", "outs", "outs_kept"))

        NORM_A1, NORM_A2, NORM_KV, NORM_B1, NORM_B2 = (1 + 3 * i for i in range(5))
        HN_MK, HN_MQA = 0, 4
        HN_K, HN_Q, HN_MQB = 10, 16, 34

        MM_AIN = 0
        MM_AOUT = MM_AIN + 2 * NA_IN
        MM_FFA = MM_AOUT + 2 * KT
        MM_FF = 4 * 2 + 23
        MM_KV = MM_FFA + MM_FF * JFF
        MM_BIN = MM_KV + 8
        MM_BOUT = MM_BIN + 16
        MM_FFB = MM_BOUT + 20
        EV_KV = 8 + 3 * NA_IN
        EV_BIN = EV_KV + 12
        EV_END = EV_BIN + 24
        NLEV = 7
        TAU = 16.0

        def tile_ready(eng, mm0, u0, t, c):
            if c < NCH - 1:
                eng.wait_ge(s_mm, mm0 + 2 * t + c + 1)
            else:
                eng.wait_ge(s_wused, u0 + t + 1)

        block = ctx.enter_context(nc.Block())

        @block.sync
        def _(sp):
            for s in range(WSLOT):
                sp.dma_start(w_raw[:, s], w_d[s]).then_inc(s_w[s], 16)
            with sp.Fori(1, NUNIT // WSLOT) as g:
                for s in range(WSLOT):
                    sp.wait_ge(s_wlo, WSLOT * g + (s + 1 - WSLOT))
                    sp.dma_start(w_raw[:, s], w_d[bass.ds(WSLOT * g + s, 1)].rearrange("a p n -> p (a n)")).then_inc(s_w[s], 16)
            for u in range(NUNIT // WSLOT * WSLOT, NUNIT):
                sp.wait_ge(s_wlo, u + 1 - WSLOT)
                sp.dma_start(w_raw[:, u % WSLOT], w_d[u]).then_inc(s_w[u % WSLOT], 16)

        @block.gpsimd
        def _(pool):
            def split(s, landed, made, used):
                pool.wait_ge(s_w[s], landed)
                if used is not None:
                    pool.wait_ge(s_wused, used)
                nc.gpsimd.tensor_tensor(w_hi[:, s], w_raw[:, s], zero[:].broadcast_to([P, 1024]), ALU.add).then_inc(s_whi, 1)
                pool.wait_ge(s_whi, made)
                nc.gpsimd.tensor_tensor(w_lo[:, s], w_raw[:, s], w_hi[:, s].bitcast(F32), ALU.subtract).then_inc(s_wlo, 1)

            nc.gpsimd.memset(zero[:], 0.0).then_inc(s_zero, 1)
            pool.wait_ge(s_zero, 1)
            for s in range(WSLOT):
                split(s, 16, s + 1, None)
            with pool.Fori(1, NUNIT // WSLOT) as g:
                for s in range(WSLOT):
                    split(s, 16 * g + 16, WSLOT * g + (s + 1), WSLOT * g + (s + 1 - WSLOT))
            for u in range(NUNIT // WSLOT * WSLOT, NUNIT):
                split(u % WSLOT, 16 * (u // WSLOT + 1), u + 1, u + 1 - WSLOT)

        @block.tensor
        def _(pe):
            def product(out, parts, last=None):
                n = len(parts)
                for i, (wh, wl, xh, xl) in enumerate(parts):
                    pe.matmul(out, wh, xh, start=(i == 0), stop=False)
                    pe.matmul(out, wh, xl, start=False, stop=False)
                    mm = pe.matmul(out, wl, xh, start=False, stop=(i == n - 1))
                return mm

            def tile_parts(s, cols, nk=KT, base=0, row=0):
                def w(t, k):
                    return t[:, s, base + k * P:base + (k + 1) * P]
                return [(w(w_hi, k), w(w_lo, k), x_hi[:, row + k, cols], x_lo[:, row + k, cols]) for k in range(nk)]

            def norm_sum(n, src, width):
                pe.wait_ge(s_sq, n + 1)
                if n >= 2:
                    pe.wait_ge(s_ln, n - 1)
                for k in range(KT):
                    mm = pe.matmul(banks[6 + n % 2][:, 0:width], ones, src[:, k, 0:width], start=(k == 0), stop=(k == KT - 1))
                mm.then_inc(s_sum, 1)

            def head_sum(i, width, free=None):
                pe.wait_ge(s_hsq, i + 1)
                if i >= 2:
                    pe.wait_ge(s_hln, i - 1)
                if free:
                    pe.wait_ge(*free)
                pe.matmul(banks[6 + i % 2][:, 0:width], head_ones, hsq[:, i % 2, 0:width], start=True, stop=True).then_inc(s_hsum, 1)

            pe.wait_ge(s_cst, 16)
            norm_sum(0, sq, MEM)
            for t in range(8):
                pe.wait_ge(s_wlo, U_MEM + t + 1)
                if t == 0:
                    pe.wait_ge(s_lo, 1)
                if t >= 6:
                    pe.wait_ge(s_ev, t - 5)
                li = t // 4
                s = (U_MEM + t) % WSLOT
                mm = product(banks[t % 6][:, 0:MEM], tile_parts(s, slice(li * MEM, (li + 1) * MEM)))
                mm.then_inc(s_wused, 1)
            for li in range(2):
                pe.wait_ge(s_ev, 4 * li + 4)
                for kt in range(2):
                    i = 2 * li + kt
                    if i == 0:
                        pe.wait_ge(s_ln, 1)
                    if i >= 2:
                        pe.wait_ge(s_mvt, i - 1)
                    for t in range(2):
                        mm = pe.transpose(banks[6 + i % 2][:, t * P:(t + 1) * P], mv_raw[:, li, t, kt * P:(kt + 1) * P], ident)
                    mm.then_inc(s_mvT, 1)
            pe.wait_ge(s_mvt, 4)
            for i in range(4):
                head_sum(HN_MK + i, MEM)

            pe.wait_ge(s_hln, 4)
            for c in range(NCH):
                norm_sum(NORM_A1 + c, sq, CH)

            def v_turn(i):
                pe.wait_ge(s_ev, 8 + 3 * (A_V[i] + 1))
                if i == 0:
                    pe.wait_ge(s_ln, NORM_A1 + NCH)
                for b in range(2):
                    n = 3 * i + b
                    if n >= 2:
                        pe.wait_ge(s_vt, n - 1)
                    for j in range(4):
                        blk = 4 * b + j
                        mm = pe.transpose(banks[6 + n % 2][:, j * P:(j + 1) * P], ring[:, i % 2, blk * P:(blk + 1) * P], ident)
                    mm.then_inc(s_vT, 1)
                n = 3 * i + 2
                pe.wait_ge(s_vt, n - 1)
                pe.transpose(banks[6 + n % 2][0:NB, 0:P], ring[:, i % 2, SEQ:T], ident).then_inc(s_vT, 1)

            for t in range(NA_IN):
                u = U_AIN + t
                pe.wait_ge(s_wlo, u + 1)
                for c in range(NCH):
                    n = 3 * t + c
                    if t == 0:
                        pe.wait_ge(s_lo, NORM_A1 + c + 1)
                    pe.wait_ge(s_ev, 8 + max(n - 5, 0))
                    mm = product(banks[n % 6][:, 0:CH], tile_parts(u % WSLOT, chunk(c)))
                    mm.then_inc(s_mm if c < NCH - 1 else s_wused, 1)
                if t - 1 in A_V:
                    v_turn(t - 1 - A_V[0])
            for i in range(2 * NCH):
                head_sum(HN_MQA + i, CH, (s_vt, 18) if i == 0 else None)

            def mem_attention(L, mq):
                a0 = NBLK * L
                sel = (slice(0, HD), slice(HD, P))
                for i in range(NBLK + 2):
                    if i < NBLK:
                        a = a0 + i
                        if i == 0:
                            pe.wait_ge(s_hn, (HN_MQA, HN_MQB)[L] + 2 * NCH)
                        if a >= 2:
                            pe.wait_ge(s_pe, a - 1)
                        for par in range(2):
                            for r in range(2):
                                mm = pe.matmul(banks[2 * (i % 2) + par][:, r * MEM:(r + 1) * MEM], mq[sel[par], r, i * P:(i + 1) * P],
                                               mk_t[sel[par], L, r], start=True, stop=True)
                        mm.then_inc(s_sc, 1)
                    if 1 <= i <= NBLK:
                        a = a0 + i - 1
                        pe.wait_ge(s_pn, a + 1)
                        if a >= 1:
                            pe.wait_ge(s_ptk, 2 * a)
                        for j in range(H):
                            for kt in range(2):
                                mm = pe.transpose(banks[4 + j // 2][:, (2 * (j % 2) + kt) * P:][:, 0:P], pr[:, (i - 1) % 2, j, kt * P:(kt + 1) * P], ident)
                        mm.then_inc(s_pt, 1)
                    if i >= 2:
                        a = a0 + i - 2
                        pe.wait_ge(s_ptk, 2 * a + 2)
                        if a >= 2:
                            pe.wait_ge(s_pok, a - 1)
                        for par in range(2):
                            for r in range(2):
                                j, head = 2 * par + r, 2 * r + par
                                for kt in range(2):
                                    mm = pe.matmul(banks[6 + i % 2][sel[par], r * P:(r + 1) * P], mv_t[:, L, kt, head * HD:(head + 1) * HD],
                                                   pt[:, i % 2, 2 * j + kt], start=(kt == 0), stop=(kt == 1))
                        mm.then_inc(s_po, 1)
                pe.wait_ge(s_qb, 4 * L + 4)
                pe.wait_ge(s_cache, 32 * (L + 1))
                pe.wait_ge(s_pe, a0 + NBLK)
                for t in range(2):
                    for b in range(NB):
                        mm = pe.matmul(banks[0][0:32, 0:MEM], q_blk[:, t, b], ck[:, t, b], start=(t + b == 0), stop=(t == 1 and b == NB - 1))
                mm.then_inc(s_dsc, 1)
                pe.wait_ge(s_dpn, L + 1)
                for kt in range(2):
                    mm = pe.transpose(banks[2][:, kt * 32:(kt + 1) * 32], dp[:, kt * P:(kt + 1) * P], ident[0:32, 0:32])
                mm.then_inc(s_dpt, 1)
                pe.wait_ge(s_dptk, L + 1)
                for b in range(NB):
                    for t in range(2):
                        for kt in range(2):
                            c0 = (t * NB + b) * 2
                            mm = pe.matmul(banks[3][:, c0:c0 + 2], cv[:, kt, b, t * P:(t + 1) * P], dpt[:, kt, 4 * b + 2 * t:4 * b + 2 * t + 2],
                                           start=(kt == 0), stop=(kt == 1))
                mm.then_inc(s_dpo, 1)

            mem_attention(0, mq_a)

            NSTEP = NLEV + 2
            for hh in range(H):
                par = hh % 2
                half = slice(HD * par, HD * par + HD)
                if hh == 0:
                    pe.wait_ge(s_gate2, 16)
                    pe.wait_ge(s_ptk, 2 * NBLK)
                    pe.wait_ge(s_pok, NBLK)
                    pe.wait_ge(s_dpok, 2)
                else:
                    pe.wait_ge(s_st, 8 * hh)
                for c in range(NCH):
                    pe.matmul(banks[4 + c][:, 0:CH], gate2[:, hh * P:(hh + 1) * P], glr[:, chunk(c)], start=True, stop=True).then_inc(s_z, 1)
                for l in range(NSTEP):
                    n = NSTEP * hh + l
                    pair = banks[2 * (n % 2)], banks[2 * (n % 2) + 1]
                    if l >= 2:
                        pe.wait_ge(s_cp, 8 * hh + l - 1)
                    elif hh >= 1:
                        pe.wait_ge(s_oe, 4 * hh)
                    if l < NLEV:
                        pe.wait_ge(s_mu, NSTEP * hh + l + 1)
                    elif l == NLEV + 1:
                        pe.wait_ge(s_mu, NSTEP * hh + l + 1)
                    for b in range(NBLK):
                        cols = slice(b * P, (b + 1) * P)
                        out = pair[b // 4][:, (b % 4) * P:(b % 4 + 1) * P]
                        if l < NLEV:
                            mm = pe.matmul(out, dqk[:, l % 2, cols], dqk[:, l % 2, cols], start=True, stop=True)
                        elif l == NLEV:
                            mm = pe.matmul(out, k_a[:, hh, cols], q_a[:, hh, cols], start=True, stop=True)
                        else:
                            mm = pe.transpose(out, dqk[:, 0, cols], ident)
                    mm.then_inc(s_ss, 1)
                pe.wait_ge(s_kt, 2 * hh + 2)
                pe.wait_ge(s_zb, 3 * hh + 3)
                for b in range(NBLK):
                    pe.matmul(banks[4 + b // 2][:, (b % 2) * DV:(b % 2 + 1) * DV], k_tok[:, b], v_tok[:, b, hh * DV:(hh + 1) * DV],
                              start=True, stop=True).then_inc(s_kv, 1)
                pe.wait_ge(s_cp, 8 * (hh + 1))
                for b in range(NBLK):
                    if b >= 1:
                        pe.wait_ge(s_st, 8 * hh + b)
                    cols = slice((b % 4) * P, (b % 4 + 1) * P)
                    for e0, e1, out in ((0, P, banks[b // 4][:, cols]), (P, DV, banks[2 + b // 4][half, cols])):
                        pe.matmul(out, v_tok[:, b, hh * DV + e0:hh * DV + e1], s_acc[:, b], start=True, stop=(b == 0))
                        if b >= 1:
                            mm = pe.matmul(out, st[:, b - 1, e0:e1], q_dec[:, b * P:(b + 1) * P], start=False, stop=True)
                mm.then_inc(s_go, 1)

            pe.wait_ge(s_st, 8 * H)
            for hh in range(H):
                mm = pe.transpose(banks[4][0:NB, hh * P:(hh + 1) * P], k_a[:, hh, SEQ:T], ident)
            mm.then_inc(s_skt, 1)

            def sample_updates(hh):
                pe.wait_ge(s_sk1, hh + 1)
                if hh == 0:
                    pe.wait_ge(s_oe, 4 * H)
                if hh >= 2:
                    pe.wait_ge(s_soe, 2 * (hh - 1))
                for b in range(NB):
                    mm = pe.matmul(banks[4 * (hh % 2) + b // 2][:, (b % 2) * DV:(b % 2 + 1) * DV], k_one[:, hh, b],
                                   vs_a[:, hh * DV:(hh + 1) * DV], start=True, stop=True)
                mm.then_inc(s_su, 1)

            def sample_outs(hh):
                half = slice(HD * (hh % 2), HD * (hh % 2) + HD)
                pe.wait_ge(s_sn, 8 * (hh + 1))
                for b in range(NB):
                    pe.matmul(banks[4 * (hh % 2)][:, b:b + 1], st_smp[:, hh, b, 0:P], q_a[:, hh, SEQ + b:SEQ + b + 1], start=True, stop=True)
                    mm = pe.matmul(banks[4 * (hh % 2) + 1][half, b:b + 1], st_smp[:, hh, b, P:DV], q_a[:, hh, SEQ + b:SEQ + b + 1],
                                   start=True, stop=True)
                mm.then_inc(s_so, 1)

            for hh in range(H + 1):
                if hh < H:
                    sample_updates(hh)
                if hh >= 1:
                    sample_outs(hh - 1)

            for c in range(NCH):
                pe.wait_ge(s_osq, c + 1)
                if c == 0:
                    pe.wait_ge(s_soe, 2 * H)
                else:
                    pe.wait_ge(s_oln, 6 * c)
                for r in range(6):
                    out = banks[r][:, 0:CH]
                    if r < H:
                        half = slice(HD * (r % 2), HD * (r % 2) + HD)
                        pe.matmul(out, ones, o_sq[:, r], start=True, stop=False)
                        pe.matmul(out, ones[half], o_sq[half, 4 + r // 2], start=False, stop=True).then_inc(s_osum, 1)
                    else:
                        pe.matmul(out, low_ones, o_sq[:, 2 * (r - 4)], start=True, stop=False)
                        pe.matmul(out, high_ones, o_sq[:, 2 * (r - 4) + 1], start=False, stop=False)
                        pe.matmul(out, head_ones, o_sq[:, r], start=False, stop=True).then_inc(s_osum, 1)

            def tiles_product(nt, u0, ready, free_sem, free0, nk=KT, per_unit=1):
                for t in range(nt):
                    u = u0 + t // per_unit
                    pe.wait_ge(s_wlo, u + 1)
                    for c in range(NCH):
                        n = 3 * t + c
                        if t == 0:
                            ready(c)
                        if n >= 6:
                            pe.wait_ge(free_sem, free0 + n - 5)
                        mm = product(banks[n % 6][:, 0:CH], tile_parts(u % WSLOT, chunk(c), nk, (t % per_unit) * nk * P))
                        last = c == NCH - 1 and t % per_unit == per_unit - 1
                        mm.then_inc(s_wused if last else s_mm, 1)

            def after_outs(c):
                pe.wait_ge(s_clo, 2 * (c + 1))
                pe.wait_ge(s_oln, 18)
            tiles_product(KT, U_AOUT, after_outs, s_res, 0)

            def swiglu(L, norm, u0, ev0):
                for c in range(NCH):
                    if c == 0:
                        pe.wait_ge(*ev0)
                    pe.wait_ge(*resid(L, c))
                    norm_sum(norm + c, sq, CH)

                def step(j, first):
                    for q in range(4):
                        s = (u0 + q) % WSLOT
                        pe.wait_ge(s_wlo, u0 + q + 1 if first else 6 * j + (u0 + q + 1))
                        for c in range(NCH):
                            if first and q == 0:
                                pe.wait_ge(s_lo, norm + c + 1)
                            if q >= 2:
                                sem_, at_ = ((s_sil, s_hid)[q % 2], 6 * JFF * L + c + 1)
                                pe.wait_ge(sem_, at_ if first else 6 * j + at_)
                            elif not first:
                                pe.wait_ge(s_down, 24 * j + (24 * JFF * L - 6 + 3 * q + c + 1))
                            mm = product(banks[3 * (q % 2) + c][:, 0:CH], tile_parts(s, chunk(c)))
                            mm.then_inc(s_mm if c < NCH - 1 else s_wused, 1)
                    sd = [(u0 + 4) % WSLOT, (u0 + 5) % WSLOT]
                    pe.wait_ge(s_wlo, u0 + 6 if first else 6 * j + (u0 + 6))
                    for c in range(NCH):
                        at_ = 6 * JFF * L + 3 + c + 1
                        pe.wait_ge(s_hlo, at_ if first else 6 * j + at_)
                        for m in range(KT):
                            n = KT * c + m
                            if n < 6:
                                sem_, at_ = (s_sil if n < 3 else s_hid, 6 * JFF * L + 3 + n % 3 + 1)
                                pe.wait_ge(sem_, at_ if first else 6 * j + at_)
                            else:
                                at_ = 24 * JFF * L + n - 5
                                pe.wait_ge(s_down, at_ if first else 24 * j + at_)
                            cols = slice(m * P, (m + 1) * P)
                            mm = product(banks[n % 6][:, 0:CH], [(w_hi[:, sd[f], cols], w_lo[:, sd[f], cols], hid_hi[:, f, chunk(c)],
                                                                  hid_lo[:, f, chunk(c)]) for f in range(2)])
                            if n < 23:
                                mm.then_inc(s_mm, 1)
                            else:
                                mm.then_inc(s_wused, 2)

                step(0, True)
                with pe.Fori(1, JFF) as j:
                    step(j, False)

            def resid(L, c):
                return s_sq, (NORM_A2, NORM_B2)[L] + c + 1

            swiglu(0, NORM_A2, U_FFA, (s_res, 24))

            for c in range(NCH):
                norm_sum(NORM_KV + c, sq, CH)

            def after_norm(norm):
                return lambda c: pe.wait_ge(s_lo, norm + c + 1)
            pe.wait_ge(s_down, 24 * JFF)
            tiles_product(4, U_KV, after_norm(NORM_KV), s_ev, EV_KV)
            for c in range(NCH):
                norm_sum(NORM_B1 + c, sq, CH)
            pe.wait_ge(s_ev, EV_BIN)
            tiles_product(8, U_BIN, after_norm(NORM_B1), s_ev, EV_BIN)
            for i in range(30):
                head_sum(HN_K + i, CH, (s_ln, NORM_B1 + NCH) if i == 0 else None)
            pe.wait_ge(s_ev, EV_END)
            mem_attention(1, mq_b)

            rows = [k_b[:, t] for t in range(2)] + [q_b[:, t] for t in range(6)]
            for i in range(3 * len(rows)):
                if i == 0:
                    pe.wait_ge(s_po, 2 * NBLK)
                    pe.wait_ge(s_pok, 2 * NBLK)
                    pe.wait_ge(s_hn, HN_MQB)
                if i >= 2:
                    pe.wait_ge(s_rs_, i - 1)
                pe.matmul(banks[6 + i % 2][:, 0:CH], swap, rows[i // 3][:, chunk(i % 3)], start=True, stop=True).then_inc(s_rsw, 1)

            for i in range(12):
                g, b = i // 4, i % 4
                if i == 0:
                    pe.wait_ge(s_dpok, 4)
                if i >= 4:
                    pe.wait_ge(s_v3, i - 3)
                for m in range(2):
                    for t in range(2):
                        c0 = (2 * m + t) * P
                        mm = pe.transpose(banks[i % 4][:, c0:c0 + P], tokens_of(v_b[:, t], g, 2 * b + m), ident)
                mm.then_inc(s_v3t, 1)

            pe.wait_ge(s_v3, 12)
            pe.wait_ge(s_tri, 1)
            pe.wait_ge(s_rok, 3 * len(rows))
            i = 0
            for hh in range(H):
                par = slice(HD * (hh % 2), HD * (hh % 2) + HD)
                for g in range(3):
                    per = 4 if g == 2 else 2
                    for b in range(NBLK // per):
                        bk = banks[i % 4]
                        if i >= 4:
                            pe.wait_ge(s_m1, i - 3)
                        if g < 2:
                            late = [blk for blk in range(2 * b, 2 * b + 2)]
                            for m, blk in enumerate(late):
                                kbs = key_blocks(g, blk)
                                if len(kbs) == 1:
                                    kbs = kbs * 2
                                for x, (kb, before) in enumerate(kbs):
                                    out = bk[:, (2 * m + x) * P:(2 * m + x + 1) * P]
                                    pe.matmul(out, tri[:, 0], tri[:, 1 if before else 2], start=True, stop=False)
                                    mm = pe.matmul(out, tokens_of(q_b[par, 2 * g + hh // 2], g, blk), tokens_of(k_b[par, hh // 2], g, kb),
                                                   start=False, stop=True)
                        else:
                            for m in range(4):
                                blk = 4 * b + m
                                out = bk[:, m * P:(m + 1) * P]
                                pe.matmul(out, tri[:, 0], tri[:, 4], start=True, stop=False)
                                mm = pe.matmul(out, tokens_of(q_b[par, 2 * g + hh // 2], g, blk), tokens_of(k_b[par, hh // 2], g, blk),
                                               start=False, stop=True)
                        mm.then_inc(s_w1, 1)
                        i += 1
            pe.wait_ge(s_m1, 40)
            for g in range(3):
                for b in range(2):
                    n = 2 * g + b
                    if n >= 4:
                        pe.wait_ge(s_mr, n - 3)
                    for m in range(4):
                        mm = pe.transpose(banks[n % 4][0:H, m * P:(m + 1) * P], m_col[:, g, :, 4 * b + m], ident)
                    mm.then_inc(s_mt, 1)
            pe.wait_ge(s_nm, 1)
            pe.wait_ge(s_sel, 1)

            def key_scores(hh, w):
                i = NW * hh + w
                g, qs, back, before = W_STEPS[w]
                par = slice(HD * (hh % 2), HD * (hh % 2) + HD)
                if i >= 4:
                    pe.wait_ge(s_we, i - 3)
                bk = banks[i % 4]
                n = len(qs)
                mask = tri[:, (2 if before else 1) if g < 2 else 3].unsqueeze(1).broadcast_to([P, n, P])
                pe.matmul(bk[:, 0:n * P], tri[:, 0], mask, start=True, stop=False, skip_group_check=True)
                at_ = tokens_of4(nm_row[:], g, qs[0] // 4)
                if n < 4:
                    at_ = at_[:, 4 - n:4]
                pe.matmul(bk[:, 0:n * P], sel[:, hh], at_, start=False, stop=False, skip_group_check=True)
                for m, blk in enumerate(qs):
                    mm = pe.matmul(bk[:, m * P:(m + 1) * P], tokens_of(k_b[par, hh // 2], g, blk - back),
                                   tokens_of(q_b[par, 2 * g + hh // 2], g, blk), start=False, stop=(m == n - 1), skip_group_check=True)
                mm.then_inc(s_w2, 1)

            def value_products(hh, w):
                i = NW * hh + w
                g, qs, back, before = W_STEPS[w]
                pe.wait_ge(s_we, i + 1)
                if w == 0 and hh >= 1:
                    pe.wait_ge(s_woc, 2 * hh)
                    pe.wait_ge(s_wok, 2 * hh)
                if w == 0 and hh == 0:
                    pe.wait_ge(s_rs_, 24)
                for m, blk in enumerate(qs):
                    e0 = 192 * (hh // 2) + HD * (hh % 2)
                    lhs = v3[:, g, blk - back, e0:e0 + P]
                    rhs = pw[:, i % 2, m]
                    bk = banks[(6 if g == 2 else 4) + blk // 4]
                    if g == 1:
                        out = tokens_of(bk[:], 1, blk % 4)
                    else:
                        out = bk[:, (blk % 4) * P:(blk % 4 + 1) * P]
                    mm = pe.matmul(out, lhs, rhs, start=((w in (0, 1, 7, 8)) and m == 0), stop=False, skip_group_check=True)
                mm.then_inc(s_wo, 1)

            for i in range(NW * H + 2):
                if i < NW * H:
                    key_scores(i // NW, i % NW)
                if i >= 2:
                    value_products((i - 2) // NW, (i - 2) % NW)

            pe.wait_ge(s_wqb, 12)
            pe.wait_ge(s_wkn, 3)
            for g in range(3):
                for t in range(2):
                    for b in range(NB):
                        mm = pe.matmul(banks[0][0:32, g * NWIN:(g + 1) * NWIN], qw_blk[:, g, t, b], wk[:, t, g, b, 0:NWIN],
                                       start=(t + b == 0), stop=(t == 1 and b == NB - 1))
            mm.then_inc(s_d1, 1)
            pe.wait_ge(s_dp, 1)
            for g in range(3):
                mm = pe.transpose(banks[1][:, g * 32:(g + 1) * 32], pd[:, g, 0:P], ident[0:32, 0:32])
            mm.then_inc(s_dpt_, 1)
            pe.wait_ge(s_dn, 1)
            for t in range(2):
                mm = pe.matmul(banks[2][:, t * NB:(t + 1) * NB], smp_head[:, t], wst[:, 8:16], start=True, stop=True)
            mm.then_inc(s_dnb_, 1)
            pe.wait_ge(s_dptk_, 1)
            for b in range(NB):
                for t in range(2):
                    c0 = (t * NB + b) * 2
                    for g in range(3):
                        mm = pe.matmul(banks[3][:, c0:c0 + 2], wv[:, g, b, t * P:(t + 1) * P], pdt[:, g, 4 * b + 2 * t:4 * b + 2 * t + 2],
                                       start=(g == 0), stop=(g == 2))
            mm.then_inc(s_do, 1)

            def after_mix(c):
                if c == 0:
                    pe.wait_ge(s_dok, 2)
                    pe.wait_ge(s_wok, 2 * H)
                    pe.wait_ge(s_woc, 2 * H)
                pe.wait_ge(s_clo, 2 * NCH + 2 * (c + 1))
            tiles_product(KT, U_BOUT, after_mix, s_res, 24, nk=4, per_unit=2)
            swiglu(1, NORM_B2, U_FFB, (s_res, 48))

        @block.scalar
        def _(act):
            act.dma_start(cst[:], cst_d).then_inc(s_cst, 16)
            act.dma_start(mt[:], mem_d).then_inc(s_mem, 16)
            act.dma_start(gain[:], gain_d).then_inc(s_gain, 16)
            for c in range(NCH):
                act.dma_start(h[:, :, chunk(c)], x_d[:, :, chunk(c)]).then_inc(s_x[c], 16)
            nc.scalar.preload_act_table_set("natural_log_exp_and_others")

            def rstd_of(bank_, out, scale, log_sem, exp_sem, n):
                nc.scalar.activation(out, bank_, ACT.Ln, scale=scale, bias=EPS).then_inc(log_sem, 1)
                act.wait_ge(log_sem, n + 1)
                nc.scalar.activation(out, out, ACT.Exp, scale=-0.5).then_inc(exp_sem, 1)

            def norm_rstd(n, src, width):
                if n >= 1:
                    act.wait_ge(s_sum, n)
                nc.scalar.activation(sq[:, :, 0:width], src, ACT.Square).then_inc(s_sq, 1)
                act.wait_ge(s_sum, n + 1)
                if n >= 2:
                    act.wait_ge(s_xt, n - 1)
                rstd_of(banks[6 + n % 2][:, 0:width], rstd[:, n % 2, 0:width], 1.0 / D, s_ln, s_rs, n)

            def norm_hi(n, dst):
                act.wait_ge(s_xt, n + 1)
                nc.scalar.activation(dst, xt[:], ACT.Copy).then_inc(s_hi, 1)

            def head_norms(first, srcs):
                def square(j):
                    i = first + j
                    src, wait = srcs[j]
                    if wait:
                        act.wait_ge(*wait)
                    if i >= 2:
                        act.wait_ge(s_hsum, i - 1)
                    nc.scalar.activation(hsq[:, i % 2, 0:src.shape[1]], src, ACT.Square).then_inc(s_hsq, 1)
                square(0)
                for j in range(len(srcs)):
                    i = first + j
                    if j + 1 < len(srcs):
                        square(j + 1)
                    act.wait_ge(s_hsum, i + 1)
                    if i >= 2:
                        act.wait_ge(s_hn, i - 1)
                    w = srcs[j][0].shape[1]
                    rstd_of(banks[6 + i % 2][:, 0:w], rstd[:, i % 2, 0:w], 1.0 / HD, s_hln, s_hrs, i)

            act.wait_ge(s_mem, 16)
            norm_rstd(0, mt[:], MEM)
            act.wait_ge(s_xt, 1)
            nc.scalar.activation(x_hi[:, :, 0:2 * MEM].rearrange("p k (l m) -> p l k m", l=2), mem_xt[:], ACT.Copy).then_inc(s_hi, 1)
            for t in range(8):
                li, j = t // 4, t % 4
                dst = mk_raw[:, li, j] if j < 2 else mv_raw[:, li, j - 2]
                act.wait_ge(s_wused, U_MEM + t + 1)
                nc.scalar.activation(dst, banks[t % 6][:, 0:MEM], ACT.Copy).then_inc(s_ev, 1)
            act.wait_ge(s_ev, 8)
            act.dma_start(mv_d, mv_raw[:]).then_inc(s_out, 16)
            head_norms(HN_MK, [(mk_raw[:, i // 2, i % 2], None) for i in range(4)])
            act.wait_ge(s_hn, 4)
            act.dma_start(mk_d, mk_t[:]).then_inc(s_out, 16)

            for c in range(NCH):
                act.wait_ge(s_x[c], 16)
                norm_rstd(NORM_A1 + c, h[:, :, chunk(c)], CH)
                norm_hi(NORM_A1 + c, x_hi[:, :, chunk(c)])
            act.wait_ge(s_lo, NORM_A1 + NCH)
            act.wait_ge(s_out, 32)
            act.dma_start(gate2[:], gate2_d).then_inc(s_gate2, 16)
            for t in range(NA_IN):
                for c in range(NCH):
                    rows, scale = P, 1.0
                    if t in A_Q:
                        dst, scale = q_a[:, t - A_Q[0], chunk(c)], float(P) ** -0.5
                    elif t in A_K:
                        dst = k_a[:, t - A_K[0], chunk(c)]
                    elif t in A_V or t in A_G:
                        i = t - A_V[0]
                        dst = ring[:, i % 2, chunk(c)]
                        if c == 0 and 2 <= i < 8:
                            act.wait_ge(s_vT, 3 * (i - 1))
                        if c == 0 and i >= 8:
                            act.wait_ge(s_spill[i % 2], 16 * (i // 2 - 3))
                    elif t in A_R:
                        dst, rows = glr[:, chunk(c)], 16
                    else:
                        dst = mq_a[:, t - A_M[0], chunk(c)]
                    n = 3 * t + c
                    tile_ready(act, MM_AIN, U_AIN, t, c)
                    nc.scalar.activation(dst, banks[n % 6][0:rows, 0:CH], ACT.Copy, scale=scale).then_inc(s_ev, 1)
                if t in A_G:
                    act.wait_ge(s_ev, 8 + 3 * (t + 1))
                    i = t - A_V[0]
                    act.dma_start(g_spill[:, t - A_G[0]], ring[:, i % 2]).then_inc(s_spill[i % 2], 16)
            act.wait_ge(s_wused, U_AIN + NA_IN)
            act.wait_ge(s_ev, 8 + 3 * NA_IN)
            act.dma_start(ck[:], cmk_d[0]).then_inc(s_cache, 16)
            act.dma_start(cv[:], cmv_d[0]).then_inc(s_cache, 16)
            head_norms(HN_MQA, [(mq_a[:, i // NCH, chunk(i % NCH)], None) for i in range(2 * NCH)])

            def mem_attention(L):
                a0 = NBLK * L
                for i in range(NBLK + 1):
                    if i < NBLK:
                        a = a0 + i
                        act.wait_ge(s_nb, a + 1)
                        if a >= 2:
                            act.wait_ge(s_pt, a - 1)
                        for par in range(2):
                            for r in range(2):
                                j = 2 * par + r
                                op = nc.scalar.activation(pr[:, i % 2, j], banks[2 * (i % 2) + par][:, r * MEM:(r + 1) * MEM], ACT.Exp,
                                                          scale=HD ** -0.5, bias=nbias[:, i % 2, j:j + 1], accum_out=psums[:, i % 2, j:j + 1])
                        op.then_inc(s_pe, 1)
                    if i >= 1:
                        a = a0 + i - 1
                        act.wait_ge(s_pt, a + 1)
                        if a >= 2:
                            act.wait_ge(s_po, a - 1)
                        for b in range(2):
                            op = nc.scalar.activation(pt[:, (i - 1) % 2, 4 * b:4 * b + 4], banks[4 + b][:].rearrange("p (j m) -> p j m", j=4), ACT.Copy)
                            op.then_inc(s_ptk, 1)
                act.wait_ge(s_dnb, L + 1)
                nc.scalar.activation(dp[:], banks[0][0:32, 0:MEM], ACT.Exp, scale=HD ** -0.5, bias=dst4[:, 1:2], accum_out=dst4[:, 2:3]).then_inc(s_dpe, 1)
                act.wait_ge(s_dpt, L + 1)
                nc.scalar.activation(dpt[:], banks[2][:, 0:64].rearrange("p (k m) -> p k m", k=2), ACT.Copy).then_inc(s_dptk, 1)

            act.wait_ge(s_hn, HN_MQA + 2 * NCH)
            act.dma_start(lvl_raw[:], lvl_d).then_inc(s_lvl_in, 16)
            mem_attention(0)

            for hh in range(H):
                half = slice(HD * (hh % 2), HD * (hh % 2) + HD)
                for c in range(NCH):
                    act.wait_ge(s_z, 3 * hh + c + 1)
                    if hh == 0 and c == 0:
                        act.wait_ge(s_spill[0], 48)
                        act.wait_ge(s_spill[1], 48)
                    elif c == 0:
                        act.wait_ge(s_bc, hh)
                        act.wait_ge(s_as, hh)
                    nc.scalar.activation(ring[:, 0, chunk(c)], banks[4 + c][:, 0:CH], ACT.Identity,
                                         bias=gain[:, G_BIAS + hh:G_BIAS + hh + 1]).then_inc(s_zb, 1)
                act.wait_ge(s_zb, 3 * hh + 3)
                nc.scalar.activation(ring[:, 1], ring[:, 0], ACT.Abs).then_inc(s_zt, 1)
                act.wait_ge(s_zt, 3 * hh + 1)
                nc.scalar.activation(ring[:, 1], ring[:, 1], ACT.Exp, scale=-1.0).then_inc(s_zt, 1)
                act.wait_ge(s_zt, 3 * hh + 2)
                nc.scalar.activation(ring[:, 1], ring[:, 1], ACT.Ln, bias=1.0).then_inc(s_zt, 1)
                act.wait_ge(s_la, hh + 1)
                nc.scalar.activation(a_smp[:, hh], ring[:, 0, SEQ:T], ACT.Exp, scale=1.0 / TAU).then_inc(s_as, 1)
                act.wait_ge(s_bc, hh + 1)
                if hh >= 1:
                    act.wait_ge(s_st, 8 * hh)
                nc.scalar.activation(b_end[:], b_cum[:, P - 1::P], ACT.Exp, scale=1.0 / TAU).then_inc(s_be, 1)
                for l in range(NLEV + 2):
                    n = (NLEV + 2) * hh + l
                    src = dec[:, l % 2]
                    if l == NLEV:
                        act.wait_ge(s_mu, n - 1)
                        src = b_cum[:]
                    else:
                        act.wait_ge(s_df, (NLEV + 1) * hh + min(l, NLEV) + 1)
                    nc.scalar.activation(dec[:, l % 2], src, ACT.Exp, scale=1.0 / TAU).then_inc(s_ex, 1)
                act.wait_ge(s_ss, (NLEV + 2) * (hh + 1))
                if hh >= 1:
                    act.wait_ge(s_kv, 8 * hh)
                n = (NLEV + 2) * hh + NLEV + 1
                for b in range(2):
                    nc.scalar.activation(k_tok[:, 4 * b:4 * b + 4], banks[2 * (n % 2) + b][:].rearrange("p (j m) -> p j m", j=4), ACT.Copy).then_inc(s_kt, 1)
                act.wait_ge(s_go, hh + 1)
                for b in range(2):
                    nc.scalar.activation(o_a[:, hh, b * 512:(b + 1) * 512], banks[b][:], ACT.Copy).then_inc(s_oe, 1)
                    nc.scalar.activation(o_a[half, 4 + hh // 2, b * 512:(b + 1) * 512], banks[2 + b][half], ACT.Copy).then_inc(s_oe, 1)
                act.wait_ge(s_st, 8 * (hh + 1))
                act.dma_start(gstate_d[hh], st[:, NBLK - 1]).then_inc(s_gst, 16)
            act.wait_ge(s_cp, 8 * H)
            act.dma_start(st_smp[:], state_d.rearrange("h p b e -> p h b e")).then_inc(s_sin, 16)
            act.wait_ge(s_spill[0], 48)
            act.wait_ge(s_spill[1], 48)
            act.dma_start(g_a[:], g_spill).then_inc(s_gland, 16)
            for hh in range(H):
                half = slice(HD * (hh % 2), HD * (hh % 2) + HD)
                act.wait_ge(s_sn, 8 * (hh + 1))
                act.dma_start(sstate_d[hh], st_smp[:, hh]).then_inc(s_sout, 16)
                act.wait_ge(s_so, hh + 1)
                nc.scalar.activation(o_a[:, hh, SEQ:T], banks[4 * (hh % 2)][:, 0:NB], ACT.Copy).then_inc(s_soe, 1)
                nc.scalar.activation(o_a[half, 4 + hh // 2, SEQ:T], banks[4 * (hh % 2) + 1][half, 0:NB], ACT.Copy).then_inc(s_soe, 1)
            act.wait_ge(s_gland, 16)
            nc.scalar.activation(g_a[:], g_a[:], ACT.Silu).then_inc(s_gsil, 1)
            act.wait_ge(s_sout, 16 * H)
            act.wait_ge(s_soe, 2 * H)
            for c in range(NCH):
                if c >= 1:
                    act.wait_ge(s_osum, 6 * c)
                nc.scalar.activation(o_sq[:], o_a[:, :, chunk(c)], ACT.Square).then_inc(s_osq, 1)
                if c >= 1:
                    act.wait_ge(s_onm, c)
                for r in range(6):
                    act.wait_ge(s_osum, 6 * c + r + 1)
                    nc.scalar.activation(o_rs[:, r], banks[r][:, 0:CH], ACT.Ln, scale=1.0 / DV, bias=EPS).then_inc(s_oln, 1)
                act.wait_ge(s_oln, 6 * (c + 1))
                nc.scalar.activation(o_rs[:], o_rs[:], ACT.Exp, scale=-0.5).then_inc(s_ors, 1)
            act.wait_ge(s_tok, NCH)
            for c in range(NCH):
                nc.scalar.activation(x_hi[:, 0:6, chunk(c)], tok_a[:, :, chunk(c)], ACT.Copy).then_inc(s_chi, 1)
                nc.scalar.activation(x_hi[:, 6:8, chunk(c)], mq_a[:, :, chunk(c)], ACT.Copy).then_inc(s_chi, 1)
            act.wait_ge(s_clo, 2 * NCH)
            act.dma_start(h[:], x_d).then_inc(s_h, 16)

            def swiglu(L, norm, u0, mm0, first_res):
                for c in range(NCH):
                    act.wait_ge(*first_res)
                    norm_rstd(norm + c, h[:, :, chunk(c)], CH)
                    norm_hi(norm + c, x_hi[:, :, chunk(c)])

                def step(j, first):
                    def at_(base, k):
                        return base if first else k * j + base
                    for f in range(2):
                        for c in range(NCH):
                            if c < NCH - 1:
                                act.wait_ge(s_mm, at_(mm0 + 4 * f + c + 1, MM_FF))
                            else:
                                act.wait_ge(s_wused, at_(u0 + 2 * f + 1, 6))
                            done = 6 * JFF * L + 3 * f + c - 2
                            if done > 0 or not first:
                                act.wait_ge(s_hid, at_(done, 6))
                            nc.scalar.activation(sil[:, c], banks[c][:, 0:CH], ACT.Silu).then_inc(s_sil, 1)
                        for c in range(NCH):
                            act.wait_ge(s_hid, at_(6 * JFF * L + 3 * f + c + 1, 6))
                            nc.scalar.activation(hid_hi[:, f, chunk(c)], hid[:, c], ACT.Copy).then_inc(s_hhi, 1)

                step(0, True)
                with act.Fori(1, JFF) as j:
                    step(j, False)

            swiglu(0, NORM_A2, U_FFA, MM_FFA, (s_res, 24))

            for norm in (NORM_KV, NORM_B1):
                for c in range(NCH):
                    if c == 0:
                        act.wait_ge(s_down, 24 * JFF)
                    norm_rstd(norm + c, h[:, :, chunk(c)], CH)
                    norm_hi(norm + c, x_hi[:, :, chunk(c)])
                act.wait_ge(s_lo, norm + NCH)
                nt, mm0, u0, ev = (4, MM_KV, U_KV, EV_KV) if norm == NORM_KV else (8, MM_BIN, U_BIN, EV_BIN)
                for t in range(nt):
                    if norm == NORM_KV:
                        dst = (k_b, v_b)[t // 2][:, t % 2]
                    else:
                        dst = q_b[:, t] if t < 6 else mq_b[:, t - 6]
                    for c in range(NCH):
                        tile_ready(act, mm0, u0, t, c)
                        nc.scalar.activation(dst[:, chunk(c)], banks[(3 * t + c) % 6][:, 0:CH], ACT.Copy).then_inc(s_ev, 1)
                if norm == NORM_KV:
                    act.wait_ge(s_ev, EV_BIN)
                    act.dma_start(vwin_d, v_b[:]).then_inc(s_out, 16)
            act.wait_ge(s_wused, U_BIN + 8)
            act.wait_ge(s_ev, EV_END)
            act.dma_start(ck[:], cmk_d[1]).then_inc(s_cache, 16)
            act.dma_start(cv[:], cmv_d[1]).then_inc(s_cache, 16)
            act.dma_start(rope[:], rope_d).then_inc(s_rope, 16)
            act.wait_ge(s_xt, NORM_B1 + NCH)
            rows = [k_b[:, t] for t in range(2)] + [q_b[:, t] for t in range(6)] + [mq_b[:, t] for t in range(2)]
            head_norms(HN_K, [(rows[i // 3][:, chunk(i % 3)], None) for i in range(30)])
            mem_attention(1)

            act.wait_ge(s_rok, 24)
            act.dma_start(kwin_d, k_b[:]).then_inc(s_out, 16)
            act.dma_start(tri_raw[:], tri_d).then_inc(s_tri_in, 16)
            act.dma_start(sel_raw[:], sel_d).then_inc(s_sel_in, 16)
            for i in range(NW * H):
                hh, w = i // NW, i % NW
                act.wait_ge(s_w2, i + 1)
                if i >= 2:
                    act.wait_ge(s_wo, i - 1)
                n = len(W_STEPS[w][1])
                nc.scalar.activation(pw[:, i % 2, 0:n], banks[i % 4][:, 0:n * P].rearrange("p (n m) -> p n m", n=n), ACT.Exp,
                                     scale=HD ** -0.5).then_inc(s_we, 1)
                if w == 1 and hh >= 1 or i == NW * H - 1:
                    done = hh if w == 1 else hh + 1
                    act.wait_ge(s_wo, NW * done)
                    if done >= 2:
                        act.wait_ge(s_wod, done - 1)
                    for b in range(2):
                        nc.scalar.activation(o_sb[:, 512 * b:512 * b + 512], banks[4 + b][:], ACT.Copy).then_inc(s_woc, 1)
            act.wait_ge(s_wod, H)
            act.dma_start(wk[:, :, :, :, 0:P], wink_d).then_inc(s_wc, 16)
            act.dma_start(wv[:], winv_d).then_inc(s_wc, 16)
            act.wait_ge(s_db, 1)
            nc.scalar.activation(pd[:], banks[0][0:32, 0:3 * NWIN].rearrange("p (g m) -> p g m", g=3), ACT.Exp, scale=HD ** -0.5,
                                 bias=wst[:, 1:2], accum_out=wst[:, 2:3]).then_inc(s_de, 1)
            act.wait_ge(s_dpt_, 1)
            nc.scalar.activation(pdt[:], banks[1][:, 0:96].rearrange("p (g m) -> p g m", g=3), ACT.Copy).then_inc(s_dptk_, 1)
            act.wait_ge(s_dok, 2)
            for c in range(NCH):
                nc.scalar.activation(x_hi[:, 0:2, chunk(c)], tok_b[:, :, chunk(c)], ACT.Copy).then_inc(s_chi, 1)
                nc.scalar.activation(x_hi[:, 2:4, chunk(c)], mq_b[:, :, chunk(c)], ACT.Copy).then_inc(s_chi, 1)
            swiglu(1, NORM_B2, U_FFB, MM_FFB, (s_res, 48))
            act.wait_ge(s_down, 48 * JFF)
            act.dma_start(y_d, h[:]).then_inc(s_out, 16)
            act.wait_ge(s_out, 16 * 5)

        @block.vector
        def _(dve):
            def norm_apply(n, src, g0, dst=None, inc=True):
                w = src.shape[2]
                dve.wait_ge(s_rs, n + 1)
                for k in range(KT):
                    op = nc.vector.scalar_tensor_tensor(out=dst[:, k], in0=src[:, k], scalar=gain[:, g0 + k:g0 + k + 1],
                                                        in1=rstd[:, n % 2, 0:w], op0=ALU.mult, op1=ALU.mult)
                if inc:
                    op.then_inc(s_xt, 1)

            def norm_lo(n, dst, hi, src):
                dve.wait_ge(s_hi, n + 1)
                nc.vector.tensor_tensor(dst, src, hi.bitcast(F32), ALU.subtract).then_inc(s_lo, 1)

            def norm_chunk(n, c, g0):
                if n >= 2:
                    dve.wait_ge(s_lo, n)
                norm_apply(n, h[:, :, chunk(c)], g0, xt)
                norm_lo(n, x_lo[:, :, chunk(c)], x_hi[:, :, chunk(c)], xt[:])

            def head_apply(first, items):
                for j, (src, g, dst) in enumerate(items):
                    i = first + j
                    dve.wait_ge(s_hrs, i + 1)
                    nc.vector.scalar_tensor_tensor(out=dst, in0=src, scalar=gain[:, g:g + 1], in1=rstd[:, i % 2, 0:src.shape[1]],
                                                   op0=ALU.mult, op1=ALU.mult).then_inc(s_hn, 1)

            dve.wait_ge(s_gain, 16)
            dve.wait_ge(s_mem, 16)
            norm_apply(0, mt, G_MN, mem_xt[:, 0], inc=False)
            norm_apply(0, mt, G_MN + KT, mem_xt[:, 1])
            norm_lo(0, x_lo[:, :, 0:2 * MEM].rearrange("p k (l m) -> p l k m", l=2),
                    x_hi[:, :, 0:2 * MEM].rearrange("p k (l m) -> p l k m", l=2), mem_xt[:])
            for li in range(2):
                for kt in range(2):
                    i = 2 * li + kt
                    dve.wait_ge(s_mvT, i + 1)
                    nc.vector.tensor_copy(mv_t[:, li, kt], banks[6 + i % 2][:, 0:MEM]).then_inc(s_mvt, 1)
            head_apply(HN_MK, [(mk_raw[:, i // 2, i % 2], G_MK + i // 2, mk_t[:, i // 2, i % 2]) for i in range(4)])

            for c in range(NCH):
                dve.wait_ge(s_x[c], 16)
                norm_chunk(NORM_A1 + c, c, G_N1)
            for n in range(18):
                i, b = n // 3, n % 3
                dve.wait_ge(s_vT, n + 1)
                if b < 2:
                    nc.vector.tensor_copy(v_tok[:, 4 * b:4 * b + 4, i * P:(i + 1) * P],
                                          banks[6 + n % 2][:].rearrange("p (j m) -> p j m", j=4)).then_inc(s_vt, 1)
                else:
                    nc.vector.tensor_copy(vs_a[:, i * P:(i + 1) * P], banks[6 + n % 2][0:NB, 0:P]).then_inc(s_vt, 1)
            head_apply(HN_MQA, [(mq_a[:, i // NCH, chunk(i % NCH)], G_MQ, mq_a[:, i // NCH, chunk(i % NCH)]) for i in range(2 * NCH)])

            def mem_attention(L, mq):
                a0 = NBLK * L
                sel = (slice(0, HD), slice(HD, P))
                nc.vector.memset(q_blk[:], 0.0).then_inc(s_qz, 1)
                dve.wait_ge(s_qz, L + 1)
                dve.wait_ge(s_hn, (HN_MQA, HN_MQB)[L] + 2 * NCH)
                for t in range(2):
                    for par in range(2):
                        diag = bass.AP(q_blk[sel[par], t].tensor, q_blk[sel[par], t].offset + 2 * t + par, [[2 * NB * 32, HD], [36, NB]])
                        nc.vector.tensor_copy(diag, mq[sel[par], t, SEQ:T]).then_inc(s_qb, 1)
                for i in range(NBLK + 3):
                    if i < NBLK:
                        a = a0 + i
                        dve.wait_ge(s_sc, a + 1)
                        if a >= 2:
                            dve.wait_ge(s_pe, a - 1)
                            dve.wait_ge(s_nb, a - 1)
                        for par in range(2):
                            nc.vector.tensor_reduce(nmax[:, i % 2, 2 * par:2 * par + 2], banks[2 * (i % 2) + par][:].rearrange("p (r m) -> p r m", r=2),
                                                    AX.X, ALU.max, negate=True).then_inc(s_mx, 1)
                        dve.wait_ge(s_mx, 2 * a + 2)
                        nc.vector.tensor_scalar(nbias[:, i % 2], nmax[:, i % 2], HD ** -0.5, None, ALU.mult).then_inc(s_nb, 1)
                    if 1 <= i <= NBLK:
                        a, s = a0 + i - 1, (i - 1) % 2
                        dve.wait_ge(s_pe, a + 1)
                        if a >= 2:
                            dve.wait_ge(s_pn, a - 1)
                        nc.vector.reciprocal(rsums[:, s], psums[:, s]).then_inc(s_ra, 1)
                        dve.wait_ge(s_ra, a + 1)
                        for j in range(H):
                            op = nc.vector.tensor_scalar(pr[:, s, j], pr[:, s, j], rsums[:, s, j:j + 1], None, ALU.mult)
                        op.then_inc(s_pn, 1)
                    if i >= 3:
                        c = i - 3
                        dve.wait_ge(s_po, a0 + c + 1)
                        nc.vector.tensor_copy(mq[:, :, c * P:(c + 1) * P], banks[6 + c % 2][:, 0:2 * P].rearrange("p (r m) -> p r m", r=2)).then_inc(s_pok, 1)
                dve.wait_ge(s_dsc, L + 1)
                nc.vector.tensor_reduce(dst4[:, 0:1], banks[0][0:32, 0:MEM], AX.X, ALU.max, negate=True).then_inc(s_dmx, 1)
                dve.wait_ge(s_dmx, L + 1)
                nc.vector.tensor_scalar(dst4[:, 1:2], dst4[:, 0:1], HD ** -0.5, None, ALU.mult).then_inc(s_dnb, 1)
                dve.wait_ge(s_dpe, L + 1)
                nc.vector.reciprocal(dst4[:, 3:4], dst4[:, 2:3]).then_inc(s_dra, 1)
                dve.wait_ge(s_dra, L + 1)
                nc.vector.tensor_scalar(dp[:], dp[:], dst4[:, 3:4], None, ALU.mult).then_inc(s_dpn, 1)
                dve.wait_ge(s_dpo, L + 1)
                for par in range(2):
                    nc.vector.tensor_copy(mq[sel[par], :, SEQ:T],
                                          banks[3][sel[par], 0:32].rearrange("p (t b r) -> p t b r", t=2, b=NB)[:, :, :, par]).then_inc(s_dpok, 1)

            mem_attention(0, mq_a)

            dve.wait_ge(s_lvl_in, 16)
            nc.vector.tensor_copy(lvl[:], lvl_raw[:]).then_inc(s_lvl, 1)
            nc.vector.memset(reset[:], 1.0).then_inc(s_rst, 1)
            dve.wait_ge(s_rst, 1)
            nc.vector.memset(reset[:, 0::P], 0.0).then_inc(s_rst2, 1)
            dve.wait_ge(s_ptk, 2 * NBLK)
            dve.wait_ge(s_po, NBLK)
            dve.wait_ge(s_dpo, 1)
            nc.vector.memset(s_acc[:], 0.0).then_inc(s_sz, 1)
            for hh in range(H):
                dve.wait_ge(s_zt, 3 * hh + 3)
                nc.vector.scalar_tensor_tensor(out=ring[:, 0], in0=ring[:, 0], scalar=0.0, in1=ring[:, 1], op0=ALU.min, op1=ALU.subtract).then_inc(s_la, 1)
                dve.wait_ge(s_la, hh + 1)
                dve.wait_ge(s_rst2, 1)
                nc.vector.tensor_tensor_scan(b_cum[:], reset[:], ring[:, 0, 0:SEQ], 0.0, ALU.mult, ALU.add).then_inc(s_bc, 1)
                dve.wait_ge(s_bc, hh + 1)
                N9 = NLEV + 2

                def halves(t2d, s):
                    v = t2d.rearrange("p (n h s) -> p n h s", h=2, s=s)
                    return v[:, :, 0], v[:, :, 1]

                def exponents(l):
                    n = N9 * hh + l
                    if n >= 2:
                        dve.wait_ge(s_mu, n - 1)
                    if l < NLEV:
                        s = 2 ** l
                        lo_, hi_ = halves(b_cum[:], s)
                        dlo, dhi = halves(dec[:, l % 2], s)
                        ref = lo_[:, :, s - 1:s].broadcast_to(list(lo_.shape))
                        nc.vector.tensor_tensor(dlo, ref, lo_, ALU.subtract)
                        nc.vector.tensor_tensor(dhi, hi_, ref, ALU.subtract).then_inc(s_df, 1)
                    elif l == NLEV + 1:
                        v = b_cum[:].rearrange("p (n s) -> p n s", s=P)
                        nc.vector.tensor_tensor(dec[:, l % 2].rearrange("p (n s) -> p n s", s=P), v[:, :, P - 1:P].broadcast_to([P, NBLK, P]), v,
                                                ALU.subtract).then_inc(s_df, 1)

                def decayed(l):
                    n = N9 * hh + l
                    dve.wait_ge(s_ex, n + 1)
                    if l == NLEV:
                        if hh >= 1:
                            dve.wait_ge(s_go, hh)
                        nc.vector.tensor_tensor(q_dec[:], q_a[:, hh, 0:SEQ], dec[:, l % 2], ALU.mult).then_inc(s_mu, 1)
                        return
                    slot = 0 if l == NLEV + 1 else l % 2
                    if l == 0 and hh >= 1:
                        dve.wait_ge(s_ss, N9 * hh)
                    if l >= 2:
                        dve.wait_ge(s_ss, N9 * hh + min(l, NLEV) - 1)
                    if l == NLEV + 1:
                        dve.wait_ge(s_ss, N9 * hh + NLEV)
                        nc.vector.tensor_tensor(dqk[:, 0], k_a[:, hh, 0:SEQ], dec[:, l % 2], ALU.mult).then_inc(s_mu, 1)
                        return
                    s = 2 ** l
                    elo, ehi = halves(dec[:, l % 2], s)
                    xlo, xhi = halves(dqk[:, l % 2], s)
                    nc.vector.tensor_tensor(xlo, halves(k_a[:, hh, 0:SEQ], s)[0], elo, ALU.mult)
                    nc.vector.tensor_tensor(xhi, halves(q_a[:, hh, 0:SEQ], s)[1], ehi, ALU.mult).then_inc(s_mu, 1)

                def keep(l):
                    n = N9 * hh + l
                    dve.wait_ge(s_ss, n + 1)
                    if l == 0 and hh >= 1:
                        dve.wait_ge(s_go, hh)
                    if hh == 0 and l == 0:
                        dve.wait_ge(s_sz, 1)
                        dve.wait_ge(s_lvl, 1)
                    if 8 * hh + l >= 1:
                        dve.wait_ge(s_cp, 8 * hh + l)
                    for b in range(2):
                        op = nc.vector.copy_predicated(s_acc[:, 4 * b:4 * b + 4], lvl[:, l:l + 1].broadcast_to([P, 4, P]),
                                                       banks[2 * (n % 2) + b][:].rearrange("p (j m) -> p j m", j=4))
                    op.then_inc(s_cp, 1)

                exponents(0)
                for l in range(N9):
                    if l + 1 < N9:
                        exponents(l + 1)
                    decayed(l)
                    if 1 <= l <= NLEV:
                        keep(l - 1)
                keep(NLEV)
                dve.wait_ge(s_be, hh + 1)
                for b in range(NBLK):
                    dve.wait_ge(s_kv, 8 * hh + 2 * (b // 2) + 2)
                    up = banks[4 + b // 2][:, (b % 2) * DV:(b % 2 + 1) * DV]
                    if b == 0:
                        if hh >= 1:
                            dve.wait_ge(s_gst, 16 * hh)
                            dve.wait_ge(s_go, hh)
                        nc.vector.tensor_copy(st[:, 0], up).then_inc(s_st, 1)
                    else:
                        dve.wait_ge(s_st, 8 * hh + b)
                        nc.vector.scalar_tensor_tensor(out=st[:, b], in0=st[:, b - 1], scalar=b_end[:, b:b + 1], in1=up,
                                                       op0=ALU.mult, op1=ALU.add).then_inc(s_st, 1)

            dve.wait_ge(s_skt, 1)
            nc.vector.tensor_copy(k_smp[:], banks[4][0:NB, :].rearrange("p (h m) -> p h m", h=H)).then_inc(s_skk, 1)
            dve.wait_ge(s_skk, 1)
            dve.wait_ge(s_go, H)
            dve.wait_ge(s_gst, 16 * H)
            for hh in range(H):
                nc.vector.tensor_tensor(k_one[:, hh], k_smp[:, hh:hh + 1].broadcast_to([NB, NB, P]),
                                        ident[0:NB, 0:NB].unsqueeze(2).broadcast_to([NB, NB, P]), ALU.mult).then_inc(s_sk1, 1)
            dve.wait_ge(s_sin, 16)
            dve.wait_ge(s_as, H)
            for hh in range(H):
                dve.wait_ge(s_su, hh + 1)
                for b in range(NB):
                    nc.vector.scalar_tensor_tensor(out=st_smp[:, hh, b], in0=st_smp[:, hh, b], scalar=a_smp[:, hh, b:b + 1],
                                                   in1=banks[4 * (hh % 2) + b // 2][:, (b % 2) * DV:(b % 2 + 1) * DV],
                                                   op0=ALU.mult, op1=ALU.add).then_inc(s_sn, 1)

            for c in range(NCH):
                dve.wait_ge(s_ors, c + 1)
                if c >= 1:
                    dve.wait_ge(s_tok, c)
                for r in range(6):
                    g = G_ON if r < H else G_ON + 1
                    op = nc.vector.scalar_tensor_tensor(out=o_nm[:, r], in0=o_a[:, r, chunk(c)], scalar=gain[:, g:g + 1], in1=o_rs[:, r],
                                                        op0=ALU.mult, op1=ALU.mult)
                op.then_inc(s_onm, 1)
                dve.wait_ge(s_onm, c + 1)
                dve.wait_ge(s_gsil, 1)
                nc.vector.tensor_tensor(tok_a[:, :, chunk(c)], o_nm[:], g_a[:, :, chunk(c)], ALU.mult).then_inc(s_tok, 1)
            for c in range(NCH):
                dve.wait_ge(s_chi, 2 * c + 2)
                nc.vector.tensor_tensor(x_lo[:, 0:6, chunk(c)], tok_a[:, :, chunk(c)], x_hi[:, 0:6, chunk(c)].bitcast(F32), ALU.subtract).then_inc(s_clo, 1)
                nc.vector.tensor_tensor(x_lo[:, 6:8, chunk(c)], mq_a[:, :, chunk(c)], x_hi[:, 6:8, chunk(c)].bitcast(F32), ALU.subtract).then_inc(s_clo, 1)

            def add_residual(nt, mm0, u0, per_unit, n0):
                for t in range(nt):
                    for c in range(NCH):
                        n = 3 * t + c
                        if c < NCH - 1 or t % per_unit < per_unit - 1:
                            dve.wait_ge(s_mm, mm0 + (3 * per_unit - 1) * (t // per_unit) + 3 * (t % per_unit) + c + 1)
                        else:
                            dve.wait_ge(s_wused, u0 + t // per_unit + 1)
                        nc.vector.tensor_tensor(h[:, t, chunk(c)], h[:, t, chunk(c)], banks[n % 6][:, 0:CH], ALU.add).then_inc(s_res, 1)

            dve.wait_ge(s_h, 16)
            add_residual(KT, MM_AOUT, U_AOUT, 1, 0)

            def swiglu(L, norm, g0, u0, mm0, first_res):
                for c in range(NCH):
                    dve.wait_ge(*first_res)
                    norm_chunk(norm + c, c, g0)

                def step(j, first):
                    def at_(base, k):
                        return base if first else k * j + base
                    for f in range(2):
                        for c in range(NCH + 1):
                            if c < NCH:
                                i = 6 * JFF * L + 3 * f + c
                                dve.wait_ge(s_sil, at_(i + 1, 6))
                                if c < NCH - 1:
                                    dve.wait_ge(s_mm, at_(mm0 + 4 * f + 2 + c + 1, MM_FF))
                                else:
                                    dve.wait_ge(s_wused, at_(u0 + 2 * f + 2, 6))
                                if i >= 3 or not first:
                                    dve.wait_ge(s_hlo, at_(i - 2, 6))
                                nc.vector.tensor_tensor(hid[:, c], sil[:, c], banks[3 + c][:, 0:CH], ALU.mult).then_inc(s_hid, 1)
                            if c >= 1:
                                i = 6 * JFF * L + 3 * f + c - 1
                                dve.wait_ge(s_hhi, at_(i + 1, 6))
                                nc.vector.tensor_tensor(hid_lo[:, f, chunk(c - 1)], hid[:, c - 1], hid_hi[:, f, chunk(c - 1)].bitcast(F32),
                                                        ALU.subtract).then_inc(s_hlo, 1)
                    for c in range(NCH):
                        for m in range(KT):
                            n = KT * c + m
                            if n < 23:
                                dve.wait_ge(s_mm, at_(mm0 + 8 + n + 1, MM_FF))
                            else:
                                dve.wait_ge(s_wused, at_(u0 + 6, 6))
                            i = 24 * JFF * L + n
                            if not first:
                                dve.wait_ge(s_down, at_(i - 23, 24))
                            nc.vector.tensor_tensor(h[:, m, chunk(c)], h[:, m, chunk(c)], banks[n % 6][:, 0:CH], ALU.add).then_inc(s_down, 1)

                step(0, True)
                with dve.Fori(1, JFF) as j:
                    step(j, False)

            swiglu(0, NORM_A2, G_N2, U_FFA, MM_FFA, (s_res, 24))

            for norm, g0 in ((NORM_KV, G_KV), (NORM_B1, G_N1 + KT)):
                for c in range(NCH):
                    if c == 0:
                        dve.wait_ge(s_down, 24 * JFF)
                    norm_chunk(norm + c, c, g0)
            rows = [(k_b[:, t], G_K) for t in range(2)] + [(q_b[:, t], G_Q) for t in range(6)] + [(mq_b[:, t], G_MQ + 1) for t in range(2)]
            head_apply(HN_K, [(rows[i // 3][0][:, chunk(i % 3)], rows[i // 3][1], rows[i // 3][0][:, chunk(i % 3)]) for i in range(30)])
            mem_attention(1, mq_b)

            dve.wait_ge(s_rope, 16)
            for i in range(24):
                x = rows[i // 3][0][:, chunk(i % 3)]
                if i >= 1:
                    dve.wait_ge(s_rok, i)
                nc.vector.tensor_tensor(r_cos[:], x, rope[:, 0, chunk(i % 3)], ALU.mult).then_inc(s_rc, 1)
                dve.wait_ge(s_rsw, i + 1)
                nc.vector.tensor_tensor(r_sin[:], banks[6 + i % 2][:, 0:CH], rope[:, 1, chunk(i % 3)], ALU.mult).then_inc(s_rs_, 1)
                dve.wait_ge(s_rc, i + 1)
                dve.wait_ge(s_rs_, i + 1)
                nc.vector.tensor_tensor(x, r_cos[:], r_sin[:], ALU.add).then_inc(s_rok, 1)

            sel2 = (slice(0, HD), slice(HD, P))
            dve.wait_ge(s_dpo, 2)
            nc.vector.memset(v3[:].rearrange("p g n (t x e) -> p (g n t) x e", t=2, e=HD)[:, :, 1], 1.0).then_inc(s_ones3, 1)
            for i in range(12):
                g, b = i // 4, i % 4
                dve.wait_ge(s_v3t, i + 1)
                nc.vector.tensor_copy(v3[:, g, 2 * b:2 * b + 2].rearrange("p n (t x e) -> p (n t) x e", t=2, e=HD)[:, :, 0::2],
                                      banks[i % 4][:].rearrange("p (n x e) -> p n x e", n=4, e=HD)).then_inc(s_v3, 1)
            dve.wait_ge(s_tri_in, 16)
            nc.vector.tensor_copy(tri[:], tri_raw[:]).then_inc(s_tri, 1)
            dve.wait_ge(s_sel_in, 16)
            nc.vector.tensor_copy(sel[:], sel_raw[:]).then_inc(s_sel, 1)
            i = 0
            for hh in range(H):
                for g in range(3):
                    per = 4 if g == 2 else 2
                    for b in range(NBLK // per):
                        dve.wait_ge(s_w1, i + 1)
                        nc.vector.tensor_reduce(m_col[:, g, hh, per * b:per * (b + 1)], banks[i % 4][:].rearrange("p (n m) -> p n m", n=per),
                                                AX.X, ALU.max).then_inc(s_m1, 1)
                        i += 1
            for g in range(3):
                for b in range(2):
                    n = 2 * g + b
                    dve.wait_ge(s_mt, n + 1)
                    src = banks[n % 4][0:H, :]
                    if g == 0:
                        nc.vector.tensor_copy(m_row[:, 512 * b:512 * b + 512], src).then_inc(s_mr, 1)
                        continue
                    dve.wait_ge(s_mr, n if g == 1 else 4 + b)
                    src = src.rearrange("p (n m) -> p n m", n=4)
                    nc.vector.tensor_tensor(tokens_of4(m_row[:], g, b), tokens_of4(m_row[:], g, b), src, ALU.max).then_inc(s_mr, 1)
            dve.wait_ge(s_mr, 6)
            nc.vector.tensor_scalar(nm_row[:], m_row[:], -1.0, None, ALU.mult).then_inc(s_nm, 1)
            for hh in range(H):
                dve.wait_ge(s_wo, NW * (hh + 1))
                for b in range(2):
                    dve.wait_ge(s_woc, 2 * hh + 2)
                    if b:
                        dve.wait_ge(s_wok, 2 * hh + 1)
                    v = tokens_of4(o_sb[:], 2, b)
                    nc.vector.tensor_tensor(v, v, banks[6 + b][:].rearrange("p (n m) -> p n m", n=4), ALU.add).then_inc(s_wok, 1)
                dve.wait_ge(s_wok, 2 * hh + 2)
                if hh >= 1:
                    dve.wait_ge(s_wod, hh)
                own, sums = sel2[hh % 2], sel2[1 - hh % 2]
                nc.vector.reciprocal(o_rl[own], o_sb[sums]).then_inc(s_wor, 1)
                dve.wait_ge(s_wor, hh + 1)
                nc.vector.tensor_tensor(tok_b[own, hh // 2, 0:SEQ], o_sb[own], o_rl[own], ALU.mult).then_inc(s_wod, 1)
            dve.wait_ge(s_wod, H)
            nc.vector.memset(qw_blk[:], 0.0).then_inc(s_wqz, 1)
            dve.wait_ge(s_wqz, 1)
            for g in range(3):
                for t in range(2):
                    for par in range(2):
                        v = qw_blk[sel2[par], g, t]
                        diag = bass.AP(v.tensor, v.offset + 2 * t + par, [[3 * 2 * NB * 32, HD], [36, NB]])
                        nc.vector.tensor_copy(diag, q_b[sel2[par], 2 * g + t, SEQ:T]).then_inc(s_wqb, 1)
            dve.wait_ge(s_wc, 32)
            for g in range(3):
                nc.vector.tensor_copy(wk[:, :, g, :, P], k_b[:, :, SEQ:T]).then_inc(s_wkn, 1)
            dve.wait_ge(s_d1, 1)
            nc.vector.tensor_reduce(wst[:, 0:1], banks[0][0:32, 0:3 * NWIN], AX.X, ALU.max, negate=True).then_inc(s_dm, 1)
            dve.wait_ge(s_dm, 1)
            nc.vector.tensor_scalar(wst[:, 1:2], wst[:, 0:1], HD ** -0.5, None, ALU.mult).then_inc(s_db, 1)
            dve.wait_ge(s_de, 1)
            nc.vector.reciprocal(wst[:, 3:4], wst[:, 2:3]).then_inc(s_dr, 1)
            dve.wait_ge(s_dr, 1)
            nc.vector.tensor_scalar(pd[:], pd[:], wst[:, 3:4], None, ALU.mult).then_inc(s_dp, 1)
            dve.wait_ge(s_dp, 1)
            nc.vector.tensor_reduce(wst[:, 4:5], pd[:, :, P], AX.X, ALU.add).then_inc(s_dpn_, 1)
            dve.wait_ge(s_dpn_, 1)
            nc.vector.tensor_scalar(wst[:, 8:16], smp_col, wst[:, 4:5], None, ALU.mult).then_inc(s_dn, 1)
            dve.wait_ge(s_dnb_, 1)
            nc.vector.tensor_tensor(v_new[:], banks[2][:, 0:2 * NB].rearrange("p (t b) -> p t b", t=2), v_b[:, :, SEQ:T], ALU.mult).then_inc(s_dvn, 1)
            dve.wait_ge(s_dvn, 1)
            dve.wait_ge(s_do, 1)
            for par in range(2):
                nc.vector.tensor_tensor(tok_b[sel2[par], :, SEQ:T], banks[3][sel2[par], 0:32].rearrange("p (t b r) -> p t b r", t=2, b=NB)[:, :, :, par],
                                        v_new[sel2[par]], ALU.add).then_inc(s_dok, 1)
            for c in range(NCH):
                dve.wait_ge(s_chi, 2 * NCH + 2 * c + 2)
                nc.vector.tensor_tensor(x_lo[:, 0:2, chunk(c)], tok_b[:, :, chunk(c)], x_hi[:, 0:2, chunk(c)].bitcast(F32), ALU.subtract).then_inc(s_clo, 1)
                nc.vector.tensor_tensor(x_lo[:, 2:4, chunk(c)], mq_b[:, :, chunk(c)], x_hi[:, 2:4, chunk(c)].bitcast(F32), ALU.subtract).then_inc(s_clo, 1)
            add_residual(KT, MM_BOUT, U_BOUT, 2, 24)
            swiglu(1, NORM_B2, G_N2 + KT, U_FFB, MM_FFB, (s_res, 48))



_OUTS = [("y", (P, KT, T)), ("gstate", (H, P, DV)), ("sstate", (H, P, NB, DV)), ("kwin", (P, 2, T)), ("vwin", (P, 2, T)),
         ("mk", (P, 2, 2, MEM)), ("mv", (P, 2, 2, MEM))]

_E_ORDER = np.concatenate([np.arange(hh * DV, hh * DV + P) for hh in range(H)]
                          + [np.arange(hh * DV + P, (hh + 1) * DV) for hh in range(H)])


def _constants():
    i = np.arange(P)
    half = i // 64
    ident = np.eye(P)
    head = (half[:, None] == half[None, :]) * 1.0
    low = np.tile((i[None, :] < 64) * 1.0, (P, 1))
    swap = (i[:, None] == (i[None, :] ^ 32)) * 1.0
    smp = (i[:, None] // H == np.arange(NB)[None, :]) * 1.0
    smp_head = (i[:, None, None] % H == 2 * np.arange(2)[None, :, None] + half[None, None, :]).reshape(P, 2 * P) * 1.0
    cst = np.concatenate([ident, np.ones((P, P)), head, low, 1.0 - low, swap, smp, smp_head], axis=1).astype(np.float32)
    lvl = []
    for s in (1, 2, 4, 8, 16, 32, 64):
        same = (i[:, None] // (2 * s)) == (i[None, :] // (2 * s))
        lvl.append(same & (i[:, None] % (2 * s) < s) & (i[None, :] % (2 * s) >= s))
    lvl.append(np.eye(P, dtype=bool))
    lvl = np.stack(lvl, 1).astype(np.float32)
    ge = i[None, :] >= i[:, None]
    no = -1e30
    turn = i[:, None] % 2 == i[None, :] % 2
    tri = np.stack([ident, np.where(ge, 0, no), np.where(ge.T, 0, no),
                    np.where(ge & turn, 0, no), np.where(ge.T & turn, 0, no)], 1).astype(np.float32)
    sel = np.zeros((H, H, P), np.float32)
    for hh in range(H):
        sel[hh, hh] = 1.0
    pos = np.concatenate([np.arange(SEQ), np.full(NB, 2048)]).astype(np.float32)
    half_n = HD // 2
    inv = (10000.0 ** (-np.arange(half_n) / half_n)).astype(np.float32)
    ang = (pos[None, :] * inv[:, None].astype(np.float32)).astype(np.float32)
    cos, sin = np.cos(ang), np.sin(ang)
    rope = np.stack([np.concatenate([cos] * 4), np.concatenate([-sin, sin] * 2)], 1).astype(np.float32)
    return cst, lvl, tri, sel, rope


def _tiles(w):
    k, n = w.shape
    if n % P:
        w = np.concatenate([w, np.zeros((k, P - n % P), w.dtype)], 1)
    return w.reshape(KT, P, -1, P).transpose(2, 1, 0, 3).reshape(-1, P, KT * P)


def _ffn_units(gu, down):
    g, u = _tiles(gu[:, :FF]), _tiles(gu[:, FF:])
    d = down.reshape(FF // P, P, D)
    order = [x for j in range(JFF) for x in (g[2 * j], u[2 * j], g[2 * j + 1], u[2 * j + 1], d[2 * j], d[2 * j + 1])]
    return np.stack(order)


def _rows(a):
    return a.T.reshape(-1, P, a.shape[0]).transpose(1, 0, 2)


def kernel(x_prompt, x_sample, state_gla, cache_win_k, cache_win_v, cache_mem_k, cache_mem_v, mem_prompt,
           norm1, norm2, a_w_in, a_w_gate2, a_b_gate, a_g_onorm, a_w_out, kv_norm, w_kv, g_k, b_w_in, b_g_q,
           b_w_out, mem_norm, w_mem_kv, g_mem_q, g_mem_k, w_ffn_gu, w_ffn_down):
    import concourse.bacc as bacc
    from concourse.bass_utils import run_bass_kernel_spmd

    f = np.ascontiguousarray
    a = lambda x: np.asarray(x)
    (x_prompt, x_sample, state_gla, cache_win_k, cache_win_v, cache_mem_k, cache_mem_v, mem_prompt,
     norm1, norm2, a_w_in, a_w_gate2, a_b_gate, a_g_onorm, a_w_out, kv_norm, w_kv, g_k, b_w_in, b_g_q,
     b_w_out, mem_norm, w_mem_kv, g_mem_q, g_mem_k, w_ffn_gu, w_ffn_down) = map(a, (
         x_prompt, x_sample, state_gla, cache_win_k, cache_win_v, cache_mem_k, cache_mem_v, mem_prompt,
         norm1, norm2, a_w_in, a_w_gate2, a_b_gate, a_g_onorm, a_w_out, kv_norm, w_kv, g_k, b_w_in, b_g_q,
         b_w_out, mem_norm, w_mem_kv, g_mem_q, g_mem_k, w_ffn_gu, w_ffn_down))
    cst, lvl, tri, sel, rope = _constants()
    x = _rows(np.concatenate([x_prompt[0], x_sample[:, 0]], 0))
    w = a_w_in[0]
    q, k, v, g, r, mq = np.split(w, [512, 1024, 1792, 2560, 2576], axis=1)
    w_in = np.concatenate([q, k, v, g[:, _E_ORDER], np.concatenate([r, np.zeros((D, 112), w.dtype)], 1), mq], 1)
    w_out = np.concatenate([a_w_out[0][:768][_E_ORDER], a_w_out[0][768:]], 0)
    b_out = b_w_out[0].reshape(4, P, 4, 2, P).transpose(2, 1, 3, 0, 4).reshape(4, P, 1024)
    weights = np.concatenate([_tiles(w_mem_kv[0]), _tiles(w_mem_kv[1]), _tiles(w_in), _tiles(w_out),
                              _ffn_units(w_ffn_gu[0], w_ffn_down[0]), _tiles(w_kv), _tiles(b_w_in[0]), b_out,
                              _ffn_units(w_ffn_gu[1], w_ffn_down[1])], 0)
    assert weights.shape == (NUNIT, P, 1024)
    col = lambda v: v.reshape(-1, P).T
    two = lambda v: np.tile(v, 2)[:, None]
    gains = np.concatenate([col(norm1.reshape(-1)), col(norm2.reshape(-1)), col(kv_norm), col(mem_norm.reshape(-1)),
                            two(g_mem_q[0]), two(g_mem_q[1]), two(g_mem_k[0]), two(g_mem_k[1]), two(b_g_q[0]), two(g_k),
                            a_g_onorm[0][:P, None], two(a_g_onorm[0][P:]), col(a_b_gate[0])], 1)
    ck = cache_mem_k.reshape(2, NB, MEM, 2, P).transpose(0, 4, 3, 1, 2)
    cv = cache_mem_v.reshape(2, NB, 2, P, 256).transpose(0, 3, 2, 1, 4)
    n_past = cache_win_k.shape[1]
    rows = [n_past - dil * np.arange(1, win // dil + 1) for win, dil in GROUPS]
    wk = np.stack([cache_win_k[:, ix] for ix in rows]).reshape(3, NB, P, 2, P).transpose(4, 3, 0, 1, 2)
    wv = np.stack([cache_win_v[:, ix] for ix in rows]).reshape(3, NB, P, 256).transpose(2, 0, 1, 3)
    arrays = dict(x=x, mem=_rows(mem_prompt[0]), w=weights, cst=cst, lvl=lvl, tri=tri, gain=gains, gate2=a_w_gate2[0],
                  sel=sel, rope=rope, state=state_gla[0].transpose(1, 2, 0, 3), cmk=ck, cmv=cv, wink=wk, winv=wv)
    arrays = {f"in_{n}": f(v) for n, v in arrays.items()}
    nc = bacc.Bacc("TRN2", target_bir_lowering=False, num_devices=1)
    args = [nc.dram_tensor(n, v.shape, mybir.dt.from_np(v.dtype), kind="ExternalInput").ap() for n, v in arrays.items()]
    args += [nc.dram_tensor(f"out_{n}", s, F32, kind="ExternalOutput").ap() for n, s in _OUTS]
    trunk_program(nc, *args)
    r = run_bass_kernel_spmd(nc, [arrays], core_ids=[0]).results[0]
    y = r["out_y"].transpose(2, 1, 0).reshape(T, D)
    rows_of = lambda name: r[name].transpose(2, 1, 0).reshape(T, H, HD)
    kw, vw = rows_of("out_kwin"), rows_of("out_vwin")
    mem_out = lambda name: r[name].transpose(1, 3, 2, 0).reshape(2, 1, MEM, H, HD)
    return (y[:SEQ].reshape(1, SEQ, D), y[SEQ:].reshape(NB, 1, D),
            r["out_gstate"].reshape(1, 1, H, P, DV), r["out_sstate"].transpose(2, 0, 1, 3).reshape(1, NB, H, P, DV),
            kw[:SEQ].reshape(1, SEQ, H, HD), vw[:SEQ].reshape(1, SEQ, H, HD),
            kw[SEQ:].reshape(NB, 1, H, HD), vw[SEQ:].reshape(NB, 1, H, HD),
            mem_out("out_mk"), mem_out("out_mv"))
```

```python
from contextlib import ExitStack

import numpy as np

import concourse.bass as bass
from concourse import mybir

F32 = mybir.dt.float32
F32R = mybir.dt.float32r
BF16 = mybir.dt.bfloat16
U8 = mybir.dt.uint8
ACT = mybir.ActivationFunctionType
ALU = mybir.AluOpType
AX = mybir.AxisListType

P = 128
D = 1024
KT = D // P
SEQ, NB = 1024, 8
T = SEQ + NB
CH = T // 3
NCH = 3
MEM = 256
HD = 64
H = 4
DV = 192
NBLK = SEQ // P
FF = 2816
JFF = FF // (2 * P)
EPS = 1e-6
WSLOT = 3
NWIN = 129
GROUPS = ((P, 1), (512, 4), (2048, 16))

A_M, A_R, A_Q, A_K, A_V, A_G = range(0, 2), (2,), range(3, 7), range(7, 11), range(11, 17), range(17, 23)
NA_IN = 23
B_M, B_K, B_Q, B_V = range(0, 2), range(2, 4), range(4, 10), range(10, 12)
NB_IN = 12
NB_NORM = 30

U_MEM = 0
U_AIN = U_MEM + 8
U_AOUT = U_AIN + NA_IN
U_FFA = U_AOUT + KT
U_KV = U_FFA + 6 * JFF
U_BOUT = U_KV + NB_IN
U_FFB = U_BOUT + 4
NUNIT = U_FFB + 6 * JFF

G_N1, G_N2, G_KV, G_MN = 0, 16, 32, 40
G_MQ, G_MK, G_Q, G_K, G_ON, G_BIAS = 56, 58, 60, 61, 62, 64
NG = 68


def chunk(c):
    return slice(c * CH, (c + 1) * CH)

NCST = 1032


def steps_of(nt):
    return [(t, c) for c in range(NCH) for t in range(3)] + [(t, c) for t in range(3, nt) for c in range(NCH)]


def tokens_of(view, g, blk):
    if g == 0:
        return view[:, blk * P:(blk + 1) * P]
    if g == 1:
        r, nb = blk % 4, blk // 4
        return view[:, r + 512 * nb:r + 512 * nb + 509:4]
    return view[:, blk:blk + SEQ - 7:8]


def tokens_of4(view, g, b):
    if g == 0:
        return view[:, 512 * b:512 * b + 512].rearrange("p (n m) -> p n m", n=4)
    if g == 1:
        return view[:, 512 * b:512 * b + 512].rearrange("p (m r) -> p r m", r=4)
    return view[:, 0:SEQ].rearrange("p (m c) -> p c m", c=8)[:, 4 * b:4 * b + 4]


def key_blocks(g, blk):
    before = {0: blk - 1 if blk >= 1 else None, 1: blk - 4 if blk >= 4 else None, 2: None}[g]
    return ([(before, True)] if before is not None else []) + [(blk, False)]


W_STEPS = [(0, range(0, 4), 0, False), (0, range(4, 8), 0, False), (0, range(1, 4), 1, True), (0, range(4, 8), 1, True),
           (1, range(0, 4), 0, False), (1, range(4, 8), 0, False), (1, range(4, 8), 4, True),
           (2, range(0, 4), 0, False), (2, range(4, 8), 0, False)]
NW = len(W_STEPS)


def trunk_program(nc, x_d, mem_d, w_d, cst_d, lvl_d, tri_d, gain_d, gate2_d, sel_d, rope_d, state_d,
                  cmk_d, cmv_d, wink_d, winv_d,
                  y_d, gstate_d, sstate_d, kwin_d, vwin_d, mk_d, mv_d):
    ctx = ExitStack()
    with ctx:
        def at(name, shape, offset, dt=F32):
            return nc.alloc_sbuf_tensor_at(name, shape, dt, offset=offset)

        def bank(i):
            return ctx.enter_context(nc.psum_tensor(f"bank{i}", [P, 512], F32))

        def sem(name):
            return ctx.enter_context(nc.semaphore(name))

        ROW = T * 4
        O_W = 16512
        w_raw = at("w_raw", [P, WSLOT, 1024], O_W)
        w_hi = at("w_hi", [P, WSLOT, 1024], O_W + 12288, F32R)
        w_lo = at("w_lo", [P, WSLOT, 1024], O_W + 24576, F32R)
        O_X = O_W + 36864
        x_hi = at("x_hi", [P, KT, T], O_X, F32R)
        x_lo = at("x_lo", [P, KT, T], O_X + KT * ROW, F32R)
        O_H = O_X + 2 * KT * ROW
        h = at("h", [P, KT, T], O_H)
        O_C = O_H + KT * ROW
        cst = at("cst", [P, NCST], O_C)
        ident, ones, head_ones = cst[:, 0:128], cst[:, 128:256], cst[:, 256:384]
        low_ones, high_ones = cst[:, 384:512], cst[:, 512:640]
        swap = cst[:, 640:768]
        smp_col = cst[0:32, 768:776]
        smp_head = cst[0:32, 776:1032].rearrange("p (t m) -> p t m", t=2)
        gain = at("gain", [P, NG], O_C + 4128)
        mk_t = at("mk_t", [P, 2, 2, MEM], O_C + 4416)
        mv_t = at("mv_t", [P, 2, 2, MEM], O_C + 8512)
        hsq = at("hsq", [P, 2, CH], O_C + 12608)
        rstd = at("rstd", [P, 2, CH], O_C + 15360)
        zero = at("zero", [P, 1], O_C + 18112)
        O_L = O_C + 18144
        sq = at("sq", [P, KT, CH], O_L)
        xt = at("xt", [P, KT, CH], O_L + 11008)
        mt = at("mt", [P, KT, MEM], O_L + 22016)
        mk_raw = at("mk_raw", [P, 2, 2, MEM], O_L + 30208)
        mv_raw = at("mv_raw", [P, 2, 2, MEM], O_L + 34304)
        mem_xt = at("mem_xt", [P, 2, KT, MEM], O_L + 38400)
        q_a = at("q_a", [P, H, T], O_L)
        k_a = at("k_a", [P, H, T], O_L + 4 * ROW)
        v_tok = at("v_tok", [P, NBLK, H * DV], O_L + 8 * ROW)
        tok_a = at("tok_a", [P, 6, T], O_L)
        g_a = at("g_a", [P, 6, T], O_L + 8 * ROW)
        mq_a = at("mq_a", [P, 2, T], O_H)
        glr = at("glr", [16, T], O_H + 2 * ROW)
        ring = at("ring", [P, 2, T], O_H + 3 * ROW)
        vs_a = at("vs_a", [NB, H * DV], O_H + 5 * ROW)
        gate2 = at("gate2", [16, 512], O_H + 5 * ROW + 3072)
        lvl = at("lvl", [P, 8, P], O_H + 5 * ROW + 9376, U8)
        lvl_raw = at("lvl_raw", [P, 8, P], O_C + 12608)
        q_b = at("q_b", [P, 6, T], O_L)
        mq_b = at("mq_b", [P, 2, T], O_L + 6 * ROW)
        tok_b = at("tok_b", [P, 2, T], O_L + 8 * ROW)
        k_b = at("k_b", [P, 2, T], O_L + 10 * ROW)
        v_b = at("v_b", [P, 2, T], O_L + 12 * ROW)
        v3 = at("v3", [P, 3, NBLK, 6 * HD], O_X)
        pw = at("pw", [P, 2, 4, P], O_C + 4416)
        m_col = at("m_col", [P, 3, H, NBLK], O_X + 36864)
        m_row = at("m_row", [H, SEQ], O_C + 8512)
        nm_row = at("nm_row", [H, SEQ], O_X + 39296, F32R)
        sel_raw = at("sel_raw", [H, H, P], O_X + 43392)
        sel = at("sel", [H, H, P], O_X + 45440, F32R)
        o_sb = at("o_sb", [P, SEQ], O_X + 47488)
        o_rl = at("o_rl", [P, SEQ], O_X + 51584)
        tri_raw = at("tri_raw", [P, 5, P], O_X + 55680)
        tri = at("tri", [P, 5, P], O_X + 58240, BF16)
        rope = at("rope", [P, 2, T], O_L + 8 * ROW)
        rstd_b = at("rstd_b", [P, 2, CH], O_L + 22016)
        mem_pr = [at("pr_a", [P, H, MEM], O_H + 5 * ROW + 5120), at("pr_b", [P, H, MEM], O_L + 12 * ROW)]
        mem_pt = [at("pt_a", [P, 2 * H, P], O_C + 12608), at("pt_b", [P, 2 * H, P], O_L + 13 * ROW)]
        mem_st = at("mem_st", [P, 4, H], O_L + 14 * ROW)
        nmax, nbias, psums, rsums = (mem_st[:, i] for i in range(4))
        wk = at("wk", [P, 2, 3, NB, 130], O_X)
        wv = at("wv", [P, 3, NB, 256], O_X + 24960)
        qw_blk = at("qw_blk", [P, 3, 2, NB, 32], O_X + 49536)
        pd = at("pd", [32, 3, NWIN], O_X + 55680)
        pdt = at("pdt", [P, 3, 32], O_X + 57248)
        wst = at("wst", [32, 16], O_X + 57632)
        v_new = at("v_new", [P, 2, NB], O_X + 57696)
        hid_hi = at("hid_hi", [P, 2, T], O_L + 22016, F32R)
        hid_lo = at("hid_lo", [P, 2, T], O_L + 22016 + 2 * ROW, F32R)
        sil = at("sil", [P, NCH, CH], O_L + 22016 + 4 * ROW)
        hid = at("hid", [P, NCH, CH], O_L + 22016 + 5 * ROW)

        reset = at("reset", [P, SEQ], O_H + 5 * ROW + 5120)
        k_smp = at("k_smp", [NB, H, P], O_H + 5 * ROW + 5120)
        a_smp = at("a_smp", [P, H, NB], O_H + 5 * ROW + 9216)
        b_end = at("b_end", [P, NBLK], O_H + 5 * ROW + 9344)
        o_a = at("o_a", [P, 6, T], O_X)
        O_G = O_X + 6 * ROW
        dec = at("dec", [P, 2, SEQ], O_G)
        dqk = at("dqk", [P, 2, SEQ], O_G + 8192)
        s_acc = at("s_acc", [P, NBLK, P], O_G + 16384)
        q_dec = at("q_dec", [P, SEQ], O_G + 20480)
        k_tok = at("k_tok", [P, NBLK, P], O_G + 24576)
        st = at("st", [P, NBLK, DV], O_G + 28672)
        b_cum = at("b_cum", [P, SEQ], O_G + 34816)
        st_smp = at("st_smp", [P, H, NB, DV], O_G)
        k_one = at("k_one", [NB, H, NB, P], O_G + 24576)
        o_sq = at("o_sq", [P, 6, CH], O_G)
        o_rs = at("o_rs", [P, 6, CH], O_G + 8256)
        o_nm = at("o_nm", [P, 6, CH], O_G + 16512)
        ck = at("ck", [P, 2, NB, MEM], O_X)
        cv = at("cv", [P, 2, NB, MEM], O_X + 16384)
        q_blk = at("q_blk", [P, 2, NB, 32], O_X + 32768)
        dp = at("dp", [32, MEM], O_X + 51200)
        dpt = at("dpt", [P, 2, 32], O_X + 52224)
        dst4 = at("dst4", [32, 4], O_X + 52608)

        banks = [bank(i) for i in range(8)]
        g_spill = nc.dram_tensor("g_spill", [P, 6, T], F32, kind="Internal").ap()

        s_wg = sem("w_scaled")
        s_w = [sem(f"w_landed{i}") for i in range(WSLOT)]
        s_whi, s_wlo, s_wused = sem("w_hi_made"), sem("w_split"), sem("w_used")
        s_cst, s_gain, s_lvl_in, s_lvl, s_mem = sem("constants_landed"), sem("gains_landed"), sem("level_masks_landed"), sem("level_masks_cast"), sem("mem_landed")
        s_x = [sem(f"x_landed{c}") for c in range(NCH)]
        s_zero = sem("zero_set")
        s_sq, s_f1, s_fold, s_sum, s_ln, s_rs = sem("squares"), sem("squares_halved"), sem("squares_folded"), sem("square_sums"), sem("logs"), sem("rstds")
        s_xt, s_hi, s_lo = sem("normed"), sem("hi_made"), sem("split")
        s_mm = sem("products")
        s_ev = sem("evacuated")
        s_hsq, s_hsum, s_hln, s_hrs, s_hn = (sem("head_" + n) for n in ("squares", "sums", "logs", "rstds", "normed"))
        s_mvT, s_mvt = sem("mem_v_turned"), sem("mem_v_kept")
        s_vT, s_vt = sem("v_turned"), sem("v_kept")
        s_out = sem("outputs_written")
        s_spill = [sem("gate_spilled0"), sem("gate_spilled1")]
        s_res = sem("residual_added")
        s_tsq, s_tacc = sem("tile_squares"), sem("tile_squares_added")
        s_sil, s_hid, s_hhi, s_hlo, s_up, s_down = (sem(n) for n in ("silu", "hidden", "hidden_hi", "hidden_split", "up_read", "down_added"))
        s_gate2 = sem("gate2_landed")

        s_z, s_zb, s_zt, s_la, s_rst, s_rst2, s_bc, s_as, s_be = (sem("gla_" + n) for n in (
            "gates", "gates_kept", "gate_terms", "log_decays", "ones", "resets", "cumulated", "sample_decays", "block_decays"))
        s_df, s_ex, s_mu, s_ss, s_cp, s_sz, s_kt, s_kv, s_st, s_go, s_oe = (sem("gla_" + n) for n in (
            "exponents", "decays", "decayed", "level_scores", "scores_kept", "scores_cleared", "keys_kept", "updates", "states", "outs", "outs_kept"))
        s_gst, s_sin, s_sout = sem("gla_state_written"), sem("sample_states_landed"), sem("sample_states_written")
        s_skt, s_skk, s_sk1, s_su, s_sn, s_so, s_soe = (sem("sample_" + n) for n in (
            "keys_turned", "keys_kept", "keys_apart", "updates", "states", "outs", "outs_kept"))
        s_gland, s_gsil, s_osq, s_osum, s_oln, s_ors, s_onm, s_tok, s_chi, s_clo = (sem(n) for n in (
            "gate_landed", "gate_silu", "out_squares", "out_sums", "out_logs", "out_rstds", "out_normed", "tokens_mixed", "mix_hi", "mix_split"))
        s_rope, s_rsw, s_rc, s_rs_, s_rok = (sem("rope_" + n) for n in ("landed", "swapped", "cos", "sin", "done"))
        s_tri_in, s_sel_in, s_tri, s_sel, s_ones3 = (sem(n) for n in (
            "masks_landed", "head_rows_landed", "masks_cast", "head_rows_cast", "ones_set"))
        s_v3t, s_v3 = sem("window_values_turned"), sem("window_values_kept")
        s_w1, s_m1, s_mt, s_mr, s_nm = (sem("window_" + n) for n in ("scores", "max", "max_turned", "max_rows", "max_negated"))
        s_w2, s_we, s_wo, s_woc, s_wok, s_wor, s_wod = (sem("window_" + n) for n in (
            "key_scores", "exps", "outs", "outs_copied", "outs_joined", "sums_inverted", "outs_scaled"))
        s_wc, s_wqz, s_wqb, s_wkn, s_d1, s_dm, s_db, s_de, s_dr, s_dp, s_dpn_, s_dpt_, s_dptk_, s_dn, s_dnb_, s_dvn, s_do, s_dok = (
            sem("step_window_" + n) for n in ("cache_landed", "cleared", "queries", "new_keys", "scores", "max", "bias", "exps", "sums_inverted",
                                              "probs", "new_probs", "probs_turned", "probs_kept", "new_apart", "new_spread", "new_values", "outs", "outs_kept"))
        s_h = sem("residual_landed")
        s_cache = sem("cache_landed")
        s_sc, s_mx, s_nb, s_pe, s_ra, s_pn, s_pt, s_ptk, s_po, s_pok = (sem("mem_" + n) for n in (
            "scores", "max", "bias", "exps", "sums_inverted", "probs", "probs_turned", "probs_kept", "outs", "outs_kept"))
        s_qz, s_qb, s_dsc, s_dmx, s_dnb, s_dpe, s_dra, s_dpn, s_dpt, s_dptk, s_dpo, s_dpok = (sem("step_mem_" + n) for n in (
            "cleared", "queries", "scores", "max", "bias", "exps", "sums_inverted", "probs", "probs_turned", "probs_kept", "outs", "outs_kept"))

        NORM_A1, NORM_A2, NORM_KV, NORM_B2 = (1 + 3 * i for i in range(4))
        SQ_A1, SQ_KV = 1, 4
        HN_MK, HN_MQA = 0, 4
        HEAD_A = ([(mk_raw[:, i // 2, i % 2], G_MK + i // 2, mk_t[:, i // 2, i % 2]) for i in range(4)]
                  + [(mq_a[:, i % 2, chunk(i // 2)], G_MQ, mq_a[:, i % 2, chunk(i // 2)]) for i in range(2 * NCH)])
        STEPS_A, STEPS_B = steps_of(NA_IN), steps_of(NB_IN)

        def dest_b(t):
            if t in B_M:
                return mq_b[:, t - B_M[0]], G_MQ + 1
            if t in B_K:
                return k_b[:, t - B_K[0]], G_K
            if t in B_Q:
                return q_b[:, t - B_Q[0]], G_Q
            return v_b[:, t - B_V[0]], None
        HEAD_B = [(dest_b(t)[0][:, chunk(c)], dest_b(t)[1], c) for t, c in STEPS_B[:NB_NORM]]
        ROPE_B = [i for i, (t, c) in enumerate(STEPS_B[:NB_NORM]) if t not in B_M]
        HN_B = 10
        MEM_AT = ([12 + 3 * i for i in range(NBLK)], [6 + 3 * i for i in range(NBLK)])

        MM_AIN = 0
        MM_AOUT = MM_AIN + 2 * NA_IN
        MM_FFA = MM_AOUT + 2 * KT
        MM_FF = 4 * 2 + 23
        MM_KV = MM_FFA + MM_FF * JFF
        MM_BOUT = MM_KV + 2 * NB_IN
        MM_FFB = MM_BOUT + 20
        EV_KV = 8 + 3 * NA_IN
        EV_END = EV_KV + 3 * NB_IN
        NLEV = 7
        TAU = 16.0

        def tile_ready(eng, mm0, u0, t, c):
            if c < NCH - 1:
                eng.wait_ge(s_mm, mm0 + (3 * c + t if t < 3 else 2 * t + c) + 1)
            else:
                eng.wait_ge(s_wused, u0 + t + 1)

        block = ctx.enter_context(nc.Block())

        @block.sync
        def _(sp):
            for s in range(WSLOT):
                sp.dma_start(w_raw[:, s], w_d[s]).then_inc(s_w[s], 16)
            with sp.Fori(1, NUNIT // WSLOT) as g:
                for s in range(WSLOT):
                    sp.wait_ge(s_wlo, WSLOT * g + (s + 1 - WSLOT))
                    sp.dma_start(w_raw[:, s], w_d[bass.ds(WSLOT * g + s, 1)].rearrange("a p n -> p (a n)")).then_inc(s_w[s], 16)
            for u in range(NUNIT // WSLOT * WSLOT, NUNIT):
                sp.wait_ge(s_wlo, u + 1 - WSLOT)
                sp.dma_start(w_raw[:, u % WSLOT], w_d[u]).then_inc(s_w[u % WSLOT], 16)

        @block.gpsimd
        def _(pool):
            def split(s, landed, made, used):
                pool.wait_ge(s_w[s], landed)
                if used is not None:
                    pool.wait_ge(s_wused, used)
                nc.gpsimd.tensor_tensor(w_hi[:, s], w_raw[:, s], zero[:].broadcast_to([P, 1024]), ALU.add).then_inc(s_whi, 1)
                pool.wait_ge(s_whi, made)
                nc.gpsimd.tensor_tensor(w_lo[:, s], w_raw[:, s], w_hi[:, s].bitcast(F32), ALU.subtract).then_inc(s_wlo, 1)

            pool.wait_ge(s_gain, 16)
            nc.gpsimd.memset(zero[:], 0.0).then_inc(s_zero, 1)
            pool.wait_ge(s_zero, 1)
            for s in range(WSLOT):
                split(s, 16, s + 1, None)
            with pool.Fori(1, U_KV // WSLOT) as g:
                for s in range(WSLOT):
                    split(s, 16 * g + 16, WSLOT * g + (s + 1), WSLOT * g + (s + 1 - WSLOT))
            for t in range(NB_IN):
                u = U_KV + t
                g0 = G_KV if t in B_K or t in B_V else G_N1 + KT
                pool.wait_ge(s_w[u % WSLOT], 16 * (u // WSLOT + 1))
                rows = w_raw[:, u % WSLOT].rearrange("p (k m) -> p k m", k=KT)
                nc.gpsimd.tensor_tensor(rows, rows, gain[:, g0:g0 + KT].unsqueeze(2).broadcast_to([P, KT, P]), ALU.mult).then_inc(s_wg, 1)
                pool.wait_ge(s_wg, t + 1)
                split(u % WSLOT, 16 * (u // WSLOT + 1), u + 1, u + 1 - WSLOT)
            with pool.Fori((U_KV + NB_IN) // WSLOT, NUNIT // WSLOT) as g:
                for s in range(WSLOT):
                    split(s, 16 * g + 16, WSLOT * g + (s + 1), WSLOT * g + (s + 1 - WSLOT))
            for u in range(NUNIT // WSLOT * WSLOT, NUNIT):
                split(u % WSLOT, 16 * (u // WSLOT + 1), u + 1, u + 1 - WSLOT)

        @block.tensor
        def _(pe):
            def product(out, parts, last=None):
                n = len(parts)
                for i, (wh, wl, xh, xl) in enumerate(parts):
                    pe.matmul(out, wh, xh, start=(i == 0), stop=False)
                    pe.matmul(out, wh, xl, start=False, stop=False)
                    mm = pe.matmul(out, wl, xh, start=False, stop=(i == n - 1))
                return mm

            def tile_parts(s, cols, nk=KT, base=0, row=0):
                def w(t, k):
                    return t[:, s, base + k * P:base + (k + 1) * P]
                return [(w(w_hi, k), w(w_lo, k), x_hi[:, row + k, cols], x_lo[:, row + k, cols]) for k in range(nk)]

            def norm_sum(n, nk, width):
                pe.wait_ge(s_fold, n + 1)
                if n >= 2:
                    pe.wait_ge(s_ln, n - 1)
                for k in range(nk):
                    src = sq[:, k, 0:width] if nk > 1 else sq[:, (n - 1) % NCH, 0:width]
                    mm = pe.matmul(banks[6 + n % 2][:, 0:width], ones, src, start=(k == 0), stop=(k == nk - 1))
                mm.then_inc(s_sum, 1)

            def head_sum(i, width):
                pe.wait_ge(s_hsq, i + 1)
                if i >= 1:
                    pe.wait_ge(s_hln, i)
                pe.matmul(banks[6][:, 0:width], head_ones, hsq[:, i % 2, 0:width], start=True, stop=True).then_inc(s_hsum, 1)

            def mem_tile(t):
                pe.wait_ge(s_wlo, U_MEM + t + 1)
                if t == 0:
                    pe.wait_ge(s_lo, 1)
                if t >= 6:
                    pe.wait_ge(s_ev, t - 5)
                li, c0 = t // 4, T - 2 * MEM
                mm = product(banks[t % 6][:, 0:MEM], tile_parts((U_MEM + t) % WSLOT, slice(c0 + li * MEM, c0 + (li + 1) * MEM)))
                mm.then_inc(s_wused, 1)

            pe.wait_ge(s_cst, 16)
            norm_sum(0, 2, MEM)
            for t in range(8):
                mem_tile(t)
                if t == 2:
                    norm_sum(NORM_A1, 2, CH)
                if t == 5:
                    norm_sum(NORM_A1 + 1, 2, CH)
            pe.wait_ge(s_ev, 8)
            for i in range(4):
                if i >= 2:
                    pe.wait_ge(s_mvt, i - 1)
                for t in range(2):
                    mm = pe.transpose(banks[3 + i % 2][:, t * P:(t + 1) * P], mv_raw[:, i // 2, t, (i % 2) * P:(i % 2 + 1) * P], ident)
                mm.then_inc(s_mvT, 1)

            halves_of = (slice(0, HD), slice(HD, P))

            def mem_attention(L, mq, n):
                if n in MEM_AT[L]:
                    i = MEM_AT[L].index(n)
                    a = NBLK * L + i
                    pe.wait_ge(s_hn, HN_B if L == 0 else HN_B + 3 * ((P * (i + 1) - 1) // CH) + 2)
                    if a >= 1:
                        pe.wait_ge(s_ptk, 2 * a)
                    if a == 0:
                        pe.wait_ge(s_mvt, 4)
                    for par in range(2):
                        for r in range(2):
                            mm = pe.matmul(banks[3 + par][:, r * MEM:(r + 1) * MEM], mq[halves_of[par], r, i * P:(i + 1) * P],
                                           mk_t[halves_of[par], L, r], start=True, stop=True)
                    mm.then_inc(s_sc, 1)
                if n - 2 in MEM_AT[L]:
                    a = NBLK * L + MEM_AT[L].index(n - 2)
                    pe.wait_ge(s_pn, a + 1)
                    for j in range(H):
                        for kt in range(2):
                            mm = pe.transpose(banks[3 + j // 2][:, (2 * (j % 2) + kt) * P:][:, 0:P], mem_pr[L][:, j, kt * P:(kt + 1) * P], ident)
                    mm.then_inc(s_pt, 1)
                if n - 4 in MEM_AT[L]:
                    i = MEM_AT[L].index(n - 4)
                    a = NBLK * L + i
                    pe.wait_ge(s_ptk, 2 * a + 2)
                    if a >= 1:
                        pe.wait_ge(s_pok, a)
                    for par in range(2):
                        for r in range(2):
                            j, head = 2 * par + r, 2 * r + par
                            for kt in range(2):
                                mm = pe.matmul(banks[5][halves_of[par], r * P:(r + 1) * P], mv_t[:, L, kt, head * HD:(head + 1) * HD],
                                               mem_pt[L][:, 2 * j + kt], start=(kt == 0), stop=(kt == 1))
                    mm.then_inc(s_po, 1)

            def step_product(u0, ev0, norm, n, t, c):
                if c == 0 or t < 3:
                    pe.wait_ge(s_wlo, u0 + t + 1)
                if n < 9:
                    pe.wait_ge(s_lo, norm + c + 1)
                if n >= 3:
                    pe.wait_ge(s_ev, ev0 + n - 2)
                mm = product(banks[n % 3][:, 0:CH], tile_parts((u0 + t) % WSLOT, chunk(c)))
                mm.then_inc(s_mm if c < NCH - 1 else s_wused, 1)

            for n, (t, c) in enumerate(STEPS_A):
                step_product(U_AIN, 8, NORM_A1, n, t, c)
                if n == 0:
                    norm_sum(NORM_A1 + 2, 2, CH)
                if 1 <= n <= len(HEAD_A):
                    if n == 1:
                        pe.wait_ge(s_ln, NORM_A1 + 2)
                    head_sum(HN_MK + n - 1, HEAD_A[n - 1][0].shape[1])
                i, b = divmod(n - 3 * (A_V[0] + 1), 3)
                if 0 <= i < 6:
                    pe.wait_ge(s_ev, 8 + 3 * (A_V[i] + 1))
                    m = 3 * i + b
                    pe.wait_ge(*((s_vt, m) if m else (s_ln, NORM_A1 + NCH)))
                    if b < 2:
                        for j in range(4):
                            blk = 4 * b + j
                            mm = pe.transpose(banks[7][:, j * P:(j + 1) * P], ring[:, i % 2, blk * P:(blk + 1) * P], ident)
                    else:
                        mm = pe.transpose(banks[7][0:NB, 0:P], ring[:, i % 2, SEQ:T], ident)
                    mm.then_inc(s_vT, 1)
                mem_attention(0, mq_a, n)

            def mem_samples(L, ev):
                pe.wait_ge(s_qb, 4 * L + 4)
                pe.wait_ge(s_cache, 32 * (L + 1))
                pe.wait_ge(s_ev, ev)
                pe.wait_ge(s_ptk, 2 * NBLK * (L + 1))
                for t in range(2):
                    for b in range(NB):
                        mm = pe.matmul(banks[0][0:32, 0:MEM], q_blk[:, t, b], ck[:, t, b], start=(t + b == 0), stop=(t == 1 and b == NB - 1))
                mm.then_inc(s_dsc, 1)
                pe.wait_ge(s_dpn, L + 1)
                for kt in range(2):
                    mm = pe.transpose(banks[2][:, kt * 32:(kt + 1) * 32], dp[:, kt * P:(kt + 1) * P], ident[0:32, 0:32])
                mm.then_inc(s_dpt, 1)
                pe.wait_ge(s_dptk, L + 1)
                for b in range(NB):
                    for t in range(2):
                        for kt in range(2):
                            c0 = (t * NB + b) * 2
                            mm = pe.matmul(banks[3][:, c0:c0 + 2], cv[:, kt, b, t * P:(t + 1) * P], dpt[:, kt, 4 * b + 2 * t:4 * b + 2 * t + 2],
                                           start=(kt == 0), stop=(kt == 1))
                mm.then_inc(s_dpo, 1)

            mem_samples(0, 8 + 3 * NA_IN)

            NSTEP = NLEV + 2
            for hh in range(H):
                par = hh % 2
                half = slice(HD * par, HD * par + HD)
                if hh == 0:
                    pe.wait_ge(s_gate2, 16)
                    pe.wait_ge(s_ptk, 2 * NBLK)
                    pe.wait_ge(s_pok, NBLK)
                    pe.wait_ge(s_dpok, 2)
                else:
                    pe.wait_ge(s_st, 8 * hh)
                for c in range(NCH):
                    pe.matmul(banks[4 + c][:, 0:CH], gate2[:, hh * P:(hh + 1) * P], glr[:, chunk(c)], start=True, stop=True).then_inc(s_z, 1)
                for l in range(NSTEP):
                    n = NSTEP * hh + l
                    pair = banks[2 * (n % 2)], banks[2 * (n % 2) + 1]
                    if l >= 2:
                        pe.wait_ge(s_cp, 8 * hh + l - 1)
                    elif hh >= 1:
                        pe.wait_ge(s_oe, 4 * hh)
                    if l < NLEV:
                        pe.wait_ge(s_mu, NSTEP * hh + l + 1)
                    elif l == NLEV + 1:
                        pe.wait_ge(s_mu, NSTEP * hh + l + 1)
                    for b in range(NBLK):
                        cols = slice(b * P, (b + 1) * P)
                        out = pair[b // 4][:, (b % 4) * P:(b % 4 + 1) * P]
                        if l < NLEV:
                            mm = pe.matmul(out, dqk[:, l % 2, cols], dqk[:, l % 2, cols], start=True, stop=True)
                        elif l == NLEV:
                            mm = pe.matmul(out, k_a[:, hh, cols], q_a[:, hh, cols], start=True, stop=True)
                        else:
                            mm = pe.transpose(out, dqk[:, 0, cols], ident)
                    mm.then_inc(s_ss, 1)
                pe.wait_ge(s_kt, 2 * hh + 2)
                pe.wait_ge(s_zb, 3 * hh + 3)
                for b in range(NBLK):
                    pe.matmul(banks[4 + b // 2][:, (b % 2) * DV:(b % 2 + 1) * DV], k_tok[:, b], v_tok[:, b, hh * DV:(hh + 1) * DV],
                              start=True, stop=True).then_inc(s_kv, 1)
                pe.wait_ge(s_cp, 8 * (hh + 1))
                for b in range(NBLK):
                    if b >= 1:
                        pe.wait_ge(s_st, 8 * hh + b)
                    cols = slice((b % 4) * P, (b % 4 + 1) * P)
                    for e0, e1, out in ((0, P, banks[b // 4][:, cols]), (P, DV, banks[2 + b // 4][half, cols])):
                        pe.matmul(out, v_tok[:, b, hh * DV + e0:hh * DV + e1], s_acc[:, b], start=True, stop=(b == 0))
                        if b >= 1:
                            mm = pe.matmul(out, st[:, b - 1, e0:e1], q_dec[:, b * P:(b + 1) * P], start=False, stop=True)
                mm.then_inc(s_go, 1)

            pe.wait_ge(s_st, 8 * H)
            for hh in range(H):
                mm = pe.transpose(banks[4][0:NB, hh * P:(hh + 1) * P], k_a[:, hh, SEQ:T], ident)
            mm.then_inc(s_skt, 1)

            def sample_updates(hh):
                pe.wait_ge(s_sk1, hh + 1)
                if hh == 0:
                    pe.wait_ge(s_oe, 4 * H)
                if hh >= 2:
                    pe.wait_ge(s_soe, 2 * (hh - 1))
                for b in range(NB):
                    mm = pe.matmul(banks[4 * (hh % 2) + b // 2][:, (b % 2) * DV:(b % 2 + 1) * DV], k_one[:, hh, b],
                                   vs_a[:, hh * DV:(hh + 1) * DV], start=True, stop=True)
                mm.then_inc(s_su, 1)

            def sample_outs(hh):
                half = slice(HD * (hh % 2), HD * (hh % 2) + HD)
                pe.wait_ge(s_sn, 8 * (hh + 1))
                for b in range(NB):
                    pe.matmul(banks[4 * (hh % 2)][:, b:b + 1], st_smp[:, hh, b, 0:P], q_a[:, hh, SEQ + b:SEQ + b + 1], start=True, stop=True)
                    mm = pe.matmul(banks[4 * (hh % 2) + 1][half, b:b + 1], st_smp[:, hh, b, P:DV], q_a[:, hh, SEQ + b:SEQ + b + 1],
                                   start=True, stop=True)
                mm.then_inc(s_so, 1)

            for hh in range(H + 1):
                if hh < H:
                    sample_updates(hh)
                if hh >= 1:
                    sample_outs(hh - 1)

            for c in range(NCH):
                pe.wait_ge(s_osq, c + 1)
                if c == 0:
                    pe.wait_ge(s_soe, 2 * H)
                else:
                    pe.wait_ge(s_oln, 6 * c)
                for r in range(6):
                    out = banks[r][:, 0:CH]
                    if r < H:
                        half = slice(HD * (r % 2), HD * (r % 2) + HD)
                        pe.matmul(out, ones, o_sq[:, r], start=True, stop=False)
                        pe.matmul(out, ones[half], o_sq[half, 4 + r // 2], start=False, stop=True).then_inc(s_osum, 1)
                    else:
                        pe.matmul(out, low_ones, o_sq[:, 2 * (r - 4)], start=True, stop=False)
                        pe.matmul(out, high_ones, o_sq[:, 2 * (r - 4) + 1], start=False, stop=False)
                        pe.matmul(out, head_ones, o_sq[:, r], start=False, stop=True).then_inc(s_osum, 1)

            def tiles_product(nt, u0, ready, free_sem, free0, nk=KT, per_unit=1):
                for t in range(nt):
                    u = u0 + t // per_unit
                    pe.wait_ge(s_wlo, u + 1)
                    for c in range(NCH):
                        n = 3 * t + c
                        if t == 0:
                            ready(c)
                        if n >= 6:
                            pe.wait_ge(free_sem, free0 + n - 5)
                        mm = product(banks[n % 6][:, 0:CH], tile_parts(u % WSLOT, chunk(c), nk, (t % per_unit) * nk * P))
                        last = c == NCH - 1 and t % per_unit == per_unit - 1
                        mm.then_inc(s_wused if last else s_mm, 1)

            def after_outs(c):
                pe.wait_ge(s_clo, 2 * (c + 1))
                pe.wait_ge(s_oln, 18)
            tiles_product(KT, U_AOUT, after_outs, s_res, 0)

            def swiglu(L, norm, u0, ev0, next_norm):
                for c in range(NCH):
                    norm_sum(norm + c, 1, CH)
                pe.wait_ge(*ev0)

                def step(j, first=False, last=False):
                    order = [(q, c) for q in range(4) for c in range(NCH)]
                    if first:
                        order = [(q, c) for c in range(NCH) for q in range(2)] + order[6:]
                    for q, c in order:
                        s = (u0 + q) % WSLOT
                        if c == 0 or first:
                            pe.wait_ge(s_wlo, u0 + q + 1 if first else 6 * j + (u0 + q + 1))
                        if first and q < 2:
                            pe.wait_ge(s_lo, norm + c + 1)
                        if q >= 2:
                            sem_, at_ = ((s_sil, s_hid)[q % 2], 6 * JFF * L + c + 1)
                            pe.wait_ge(sem_, at_ if first else 6 * j + at_)
                        elif not first:
                            pe.wait_ge(s_down, 24 * j + (24 * JFF * L - 6 + 3 * q + c + 1))
                        mm = product(banks[3 * (q % 2) + c][:, 0:CH], tile_parts(s, chunk(c)))
                        mm.then_inc(s_mm if c < NCH - 1 else s_wused, 1)
                    sd = [(u0 + 4) % WSLOT, (u0 + 5) % WSLOT]
                    pe.wait_ge(s_wlo, u0 + 6 if first else 6 * j + (u0 + 6))
                    for c in range(NCH):
                        at_ = 6 * JFF * L + 3 + c + 1
                        pe.wait_ge(s_hlo, at_ if first else 6 * j + at_)
                        for m in range(KT):
                            n = KT * c + m
                            if n < 6:
                                sem_, at_ = (s_sil if n < 3 else s_hid, 6 * JFF * L + 3 + n % 3 + 1)
                                pe.wait_ge(sem_, at_ if first else 6 * j + at_)
                            else:
                                at_ = 24 * JFF * L + n - 5
                                pe.wait_ge(s_down, at_ if first else 24 * j + at_)
                            cols = slice(m * P, (m + 1) * P)
                            mm = product(banks[n % 6][:, 0:CH], [(w_hi[:, sd[f], cols], w_lo[:, sd[f], cols], hid_hi[:, f, chunk(c)],
                                                                  hid_lo[:, f, chunk(c)]) for f in range(2)])
                            if n < 23:
                                mm.then_inc(s_mm, 1)
                            else:
                                mm.then_inc(s_wused, 2)
                        if last and next_norm and c >= 1:
                            norm_sum(next_norm + c - 1, 2, CH)

                step(0, first=True)
                with pe.Fori(1, JFF - 1) as j:
                    step(j)
                step(JFF - 1, last=True)

            swiglu(0, NORM_A2, U_FFA, (s_res, 24), NORM_KV)

            pe.wait_ge(s_down, 24 * JFF)
            for n, (t, c) in enumerate(STEPS_B):
                step_product(U_KV, EV_KV, NORM_KV, n, t, c)
                if n == 0:
                    norm_sum(NORM_KV + 2, 2, CH)
                if 1 <= n <= NB_NORM:
                    if n == 1:
                        pe.wait_ge(s_ln, NORM_KV + 2)
                    head_sum(HN_B + n - 1, CH)
                if n - 2 in ROPE_B:
                    i = ROPE_B.index(n - 2)
                    pe.wait_ge(s_hn, HN_B + n - 1)
                    pe.wait_ge(*((s_rok, i) if i else (s_ln, NORM_KV + NCH)))
                    pe.matmul(banks[7][:, 0:CH], swap, HEAD_B[n - 2][0], start=True, stop=True).then_inc(s_rsw, 1)
                mem_attention(1, mq_b, n)
            mem_samples(1, EV_END)

            for i in range(12):
                g, b = i // 4, i % 4
                if i == 0:
                    pe.wait_ge(s_dpok, 4)
                if i >= 4:
                    pe.wait_ge(s_v3, i - 3)
                for m in range(2):
                    for t in range(2):
                        c0 = (2 * m + t) * P
                        mm = pe.transpose(banks[i % 4][:, c0:c0 + P], tokens_of(v_b[:, t], g, 2 * b + m), ident)
                mm.then_inc(s_v3t, 1)

            pe.wait_ge(s_v3, 12)
            pe.wait_ge(s_tri, 1)
            pe.wait_ge(s_rok, len(ROPE_B))
            i = 0
            for hh in range(H):
                par = slice(HD * (hh % 2), HD * (hh % 2) + HD)
                for g in range(3):
                    per = 4 if g == 2 else 2
                    for b in range(NBLK // per):
                        bk = banks[i % 4]
                        if i >= 4:
                            pe.wait_ge(s_m1, i - 3)
                        if g < 2:
                            late = [blk for blk in range(2 * b, 2 * b + 2)]
                            for m, blk in enumerate(late):
                                kbs = key_blocks(g, blk)
                                if len(kbs) == 1:
                                    kbs = kbs * 2
                                for x, (kb, before) in enumerate(kbs):
                                    out = bk[:, (2 * m + x) * P:(2 * m + x + 1) * P]
                                    pe.matmul(out, tri[:, 0], tri[:, 1 if before else 2], start=True, stop=False)
                                    mm = pe.matmul(out, tokens_of(q_b[par, 2 * g + hh // 2], g, blk), tokens_of(k_b[par, hh // 2], g, kb),
                                                   start=False, stop=True)
                        else:
                            for m in range(4):
                                blk = 4 * b + m
                                out = bk[:, m * P:(m + 1) * P]
                                pe.matmul(out, tri[:, 0], tri[:, 4], start=True, stop=False)
                                mm = pe.matmul(out, tokens_of(q_b[par, 2 * g + hh // 2], g, blk), tokens_of(k_b[par, hh // 2], g, blk),
                                               start=False, stop=True)
                        mm.then_inc(s_w1, 1)
                        i += 1
            pe.wait_ge(s_m1, 40)
            for g in range(3):
                for b in range(2):
                    n = 2 * g + b
                    if n >= 4:
                        pe.wait_ge(s_mr, n - 3)
                    for m in range(4):
                        mm = pe.transpose(banks[n % 4][0:H, m * P:(m + 1) * P], m_col[:, g, :, 4 * b + m], ident)
                    mm.then_inc(s_mt, 1)
            pe.wait_ge(s_nm, 1)
            pe.wait_ge(s_sel, 1)

            def key_scores(hh, w):
                i = NW * hh + w
                g, qs, back, before = W_STEPS[w]
                par = slice(HD * (hh % 2), HD * (hh % 2) + HD)
                if i >= 4:
                    pe.wait_ge(s_we, i - 3)
                bk = banks[i % 4]
                n = len(qs)
                mask = tri[:, (2 if before else 1) if g < 2 else 3].unsqueeze(1).broadcast_to([P, n, P])
                pe.matmul(bk[:, 0:n * P], tri[:, 0], mask, start=True, stop=False, skip_group_check=True)
                at_ = tokens_of4(nm_row[:], g, qs[0] // 4)
                if n < 4:
                    at_ = at_[:, 4 - n:4]
                pe.matmul(bk[:, 0:n * P], sel[:, hh], at_, start=False, stop=False, skip_group_check=True)
                for m, blk in enumerate(qs):
                    mm = pe.matmul(bk[:, m * P:(m + 1) * P], tokens_of(k_b[par, hh // 2], g, blk - back),
                                   tokens_of(q_b[par, 2 * g + hh // 2], g, blk), start=False, stop=(m == n - 1), skip_group_check=True)
                mm.then_inc(s_w2, 1)

            def value_products(hh, w):
                i = NW * hh + w
                g, qs, back, before = W_STEPS[w]
                pe.wait_ge(s_we, i + 1)
                if w == 0 and hh >= 1:
                    pe.wait_ge(s_woc, 2 * hh)
                    pe.wait_ge(s_wok, 2 * hh)
                if w == 0 and hh == 0:
                    pe.wait_ge(s_rok, len(ROPE_B))
                for m, blk in enumerate(qs):
                    e0 = 192 * (hh // 2) + HD * (hh % 2)
                    lhs = v3[:, g, blk - back, e0:e0 + P]
                    rhs = pw[:, i % 2, m]
                    bk = banks[(6 if g == 2 else 4) + blk // 4]
                    if g == 1:
                        out = tokens_of(bk[:], 1, blk % 4)
                    else:
                        out = bk[:, (blk % 4) * P:(blk % 4 + 1) * P]
                    mm = pe.matmul(out, lhs, rhs, start=((w in (0, 1, 7, 8)) and m == 0), stop=False, skip_group_check=True)
                mm.then_inc(s_wo, 1)

            for i in range(NW * H + 2):
                if i < NW * H:
                    key_scores(i // NW, i % NW)
                if i >= 2:
                    value_products((i - 2) // NW, (i - 2) % NW)

            pe.wait_ge(s_wqb, 12)
            pe.wait_ge(s_wkn, 3)
            for g in range(3):
                for t in range(2):
                    for b in range(NB):
                        mm = pe.matmul(banks[0][0:32, g * NWIN:(g + 1) * NWIN], qw_blk[:, g, t, b], wk[:, t, g, b, 0:NWIN],
                                       start=(t + b == 0), stop=(t == 1 and b == NB - 1))
            mm.then_inc(s_d1, 1)
            pe.wait_ge(s_dp, 1)
            for g in range(3):
                mm = pe.transpose(banks[1][:, g * 32:(g + 1) * 32], pd[:, g, 0:P], ident[0:32, 0:32])
            mm.then_inc(s_dpt_, 1)
            pe.wait_ge(s_dn, 1)
            for t in range(2):
                mm = pe.matmul(banks[2][:, t * NB:(t + 1) * NB], smp_head[:, t], wst[:, 8:16], start=True, stop=True)
            mm.then_inc(s_dnb_, 1)
            pe.wait_ge(s_dptk_, 1)
            for b in range(NB):
                for t in range(2):
                    c0 = (t * NB + b) * 2
                    for g in range(3):
                        mm = pe.matmul(banks[3][:, c0:c0 + 2], wv[:, g, b, t * P:(t + 1) * P], pdt[:, g, 4 * b + 2 * t:4 * b + 2 * t + 2],
                                       start=(g == 0), stop=(g == 2))
            mm.then_inc(s_do, 1)

            def after_mix(c):
                if c == 0:
                    pe.wait_ge(s_dok, 2)
                    pe.wait_ge(s_wok, 2 * H)
                    pe.wait_ge(s_woc, 2 * H)
                pe.wait_ge(s_clo, 2 * NCH + 2 * (c + 1))
            tiles_product(KT, U_BOUT, after_mix, s_res, 24, nk=4, per_unit=2)
            swiglu(1, NORM_B2, U_FFB, (s_res, 48), None)

        @block.scalar
        def _(act):
            act.dma_start(cst[:], cst_d).then_inc(s_cst, 16)
            act.dma_start(mt[:], mem_d).then_inc(s_mem, 16)
            act.dma_start(gain[:], gain_d).then_inc(s_gain, 16)
            for c in range(NCH):
                act.dma_start(h[:, :, chunk(c)], x_d[:, :, chunk(c)]).then_inc(s_x[c], 16)
            nc.scalar.preload_act_table_set("natural_log_exp_and_others")

            def rstd_of(bank_, out, scale, log_sem, exp_sem, n):
                nc.scalar.activation(out, bank_, ACT.Ln, scale=scale, bias=EPS).then_inc(log_sem, 1)
                act.wait_ge(log_sem, n + 1)
                nc.scalar.activation(out, out, ACT.Exp, scale=-0.5).then_inc(exp_sem, 1)

            def square(i, n, src, width):
                if n >= 1:
                    act.wait_ge(s_sum, n)
                nc.scalar.activation(sq[:, :, 0:width], src, ACT.Square).then_inc(s_sq, 1)

            def norm_rstd(n, width, out):
                act.wait_ge(s_sum, n + 1)
                if n >= 1:
                    act.wait_ge(s_xt, max(n - 1, 1))
                rstd_of(banks[6 + n % 2][:, 0:width], out[:, n % 2, 0:width], 1.0 / D, s_ln, s_rs, n)

            def norm_hi(n, dst):
                act.wait_ge(s_xt, n + 1)
                nc.scalar.activation(dst, xt[:], ACT.Copy).then_inc(s_hi, 1)

            def head_square(i, src):
                if i >= 2:
                    act.wait_ge(s_hsum, i - 1)
                nc.scalar.activation(hsq[:, i % 2, 0:src.shape[1]], src, ACT.Square).then_inc(s_hsq, 1)

            def head_rstd(i, width):
                act.wait_ge(s_hsum, i + 1)
                if i >= 2:
                    act.wait_ge(s_hn, i - 1)
                rstd_of(banks[6][:, 0:width], rstd[:, i % 2, 0:width], 1.0 / HD, s_hln, s_hrs, i)

            act.wait_ge(s_mem, 16)
            square(0, 0, mt[:], MEM)
            norm_rstd(0, MEM, rstd)
            act.wait_ge(s_xt, 1)
            nc.scalar.activation(x_hi[:, :, T - 2 * MEM:T].rearrange("p k (l m) -> p l k m", l=2), mem_xt[:], ACT.Copy).then_inc(s_hi, 1)
            act.wait_ge(s_x[0], 16)
            square(SQ_A1, NORM_A1, h[:, :, chunk(0)], CH)
            for t in range(8):
                li, j = t // 4, t % 4
                dst = mk_raw[:, li, j] if j < 2 else mv_raw[:, li, j - 2]
                act.wait_ge(s_wused, U_MEM + t + 1)
                nc.scalar.activation(dst, banks[t % 6][:, 0:MEM], ACT.Copy).then_inc(s_ev, 1)
                if t == 2:
                    norm_rstd(NORM_A1, CH, rstd_b)
                    act.wait_ge(s_x[1], 16)
                    square(SQ_A1 + 1, NORM_A1 + 1, h[:, :, chunk(1)], CH)
                if t == 5:
                    norm_hi(NORM_A1, x_hi[:, :, chunk(0)])
            norm_rstd(NORM_A1 + 1, CH, rstd_b)
            act.wait_ge(s_x[2], 16)
            square(SQ_A1 + 2, NORM_A1 + 2, h[:, :, chunk(2)], CH)
            norm_hi(NORM_A1 + 1, x_hi[:, :, chunk(1)])
            act.wait_ge(s_ev, 8)
            act.dma_start(mv_d, mv_raw[:]).then_inc(s_out, 16)

            def mem_attention(L, n):
                if n in MEM_AT[L]:
                    a = NBLK * L + MEM_AT[L].index(n)
                    act.wait_ge(s_nb, a + 1)
                    if a >= 1:
                        act.wait_ge(s_pt, a)
                    for par in range(2):
                        for r in range(2):
                            j = 2 * par + r
                            op = nc.scalar.activation(mem_pr[L][:, j], banks[3 + par][:, r * MEM:(r + 1) * MEM], ACT.Exp,
                                                      scale=HD ** -0.5, bias=nbias[:, j:j + 1], accum_out=psums[:, j:j + 1])
                    op.then_inc(s_pe, 1)
                if n - 2 in MEM_AT[L]:
                    a = NBLK * L + MEM_AT[L].index(n - 2)
                    act.wait_ge(s_pt, a + 1)
                    if a >= 1:
                        act.wait_ge(s_po, a)
                    for b in range(2):
                        op = nc.scalar.activation(mem_pt[L][:, 4 * b:4 * b + 4], banks[3 + b][:].rearrange("p (j m) -> p j m", j=4), ACT.Copy)
                        op.then_inc(s_ptk, 1)

            def mem_samples(L):
                act.wait_ge(s_dnb, L + 1)
                nc.scalar.activation(dp[:], banks[0][0:32, 0:MEM], ACT.Exp, scale=HD ** -0.5, bias=dst4[:, 1:2], accum_out=dst4[:, 2:3]).then_inc(s_dpe, 1)
                act.wait_ge(s_dpt, L + 1)
                nc.scalar.activation(dpt[:], banks[2][:, 0:64].rearrange("p (k m) -> p k m", k=2), ACT.Copy).then_inc(s_dptk, 1)

            for n, (t, c) in enumerate(STEPS_A):
                rows, scale = P, 1.0
                if t in A_Q:
                    dst, scale = q_a[:, t - A_Q[0], chunk(c)], float(P) ** -0.5
                elif t in A_K:
                    dst = k_a[:, t - A_K[0], chunk(c)]
                elif t in A_V or t in A_G:
                    i = t - A_V[0]
                    dst = ring[:, i % 2, chunk(c)]
                    if c == 0 and 2 <= i < 8:
                        act.wait_ge(s_vT, 3 * (i - 1))
                    if c == 0 and i >= 8:
                        act.wait_ge(s_spill[i % 2], 16 * (i // 2 - 3))
                elif t in A_R:
                    dst, rows = glr[:, chunk(c)], 16
                else:
                    dst = mq_a[:, t - A_M[0], chunk(c)]
                if n == 9:
                    act.wait_ge(s_out, 32)
                    act.dma_start(gate2[:], gate2_d).then_inc(s_gate2, 16)
                tile_ready(act, MM_AIN, U_AIN, t, c)
                nc.scalar.activation(dst, banks[n % 3][0:rows, 0:CH], ACT.Copy, scale=scale).then_inc(s_ev, 1)
                if n < len(HEAD_A):
                    if HN_MK + n >= 4:
                        act.wait_ge(s_ev, 8 + n + 1)
                    head_square(HN_MK + n, HEAD_A[n][0])
                if n == 0:
                    norm_rstd(NORM_A1 + 2, CH, rstd_b)
                if 1 <= n <= len(HEAD_A):
                    head_rstd(HN_MK + n - 1, HEAD_A[n - 1][0].shape[1])
                if n == 1:
                    norm_hi(NORM_A1 + 2, x_hi[:, :, chunk(2)])
                if n == 5:
                    act.wait_ge(s_hn, HN_MK + 4)
                    act.dma_start(mk_d, mk_t[:]).then_inc(s_out, 16)
                mem_attention(0, n)
                if t in A_G and c == NCH - 1:
                    act.wait_ge(s_ev, 8 + 3 * (t + 1))
                    i = t - A_V[0]
                    act.dma_start(g_spill[:, t - A_G[0]], ring[:, i % 2]).then_inc(s_spill[i % 2], 16)
            act.wait_ge(s_wused, U_AIN + NA_IN)
            act.wait_ge(s_ev, 8 + 3 * NA_IN)
            act.dma_start(ck[:], cmk_d[0]).then_inc(s_cache, 16)
            act.dma_start(cv[:], cmv_d[0]).then_inc(s_cache, 16)
            act.wait_ge(s_pok, NBLK)
            act.dma_start(lvl_raw[:], lvl_d).then_inc(s_lvl_in, 16)
            mem_samples(0)

            for hh in range(H):
                half = slice(HD * (hh % 2), HD * (hh % 2) + HD)
                for c in range(NCH):
                    act.wait_ge(s_z, 3 * hh + c + 1)
                    if hh == 0 and c == 0:
                        act.wait_ge(s_spill[0], 48)
                        act.wait_ge(s_spill[1], 48)
                    elif c == 0:
                        act.wait_ge(s_bc, hh)
                        act.wait_ge(s_as, hh)
                    nc.scalar.activation(ring[:, 0, chunk(c)], banks[4 + c][:, 0:CH], ACT.Identity,
                                         bias=gain[:, G_BIAS + hh:G_BIAS + hh + 1]).then_inc(s_zb, 1)
                act.wait_ge(s_zb, 3 * hh + 3)
                nc.scalar.activation(ring[:, 1], ring[:, 0], ACT.Abs).then_inc(s_zt, 1)
                act.wait_ge(s_zt, 3 * hh + 1)
                nc.scalar.activation(ring[:, 1], ring[:, 1], ACT.Exp, scale=-1.0).then_inc(s_zt, 1)
                act.wait_ge(s_zt, 3 * hh + 2)
                nc.scalar.activation(ring[:, 1], ring[:, 1], ACT.Ln, bias=1.0).then_inc(s_zt, 1)
                act.wait_ge(s_la, hh + 1)
                nc.scalar.activation(a_smp[:, hh], ring[:, 0, SEQ:T], ACT.Exp, scale=1.0 / TAU).then_inc(s_as, 1)
                act.wait_ge(s_bc, hh + 1)
                if hh >= 1:
                    act.wait_ge(s_st, 8 * hh)
                nc.scalar.activation(b_end[:], b_cum[:, P - 1::P], ACT.Exp, scale=1.0 / TAU).then_inc(s_be, 1)
                for l in range(NLEV + 2):
                    n = (NLEV + 2) * hh + l
                    src = dec[:, l % 2]
                    if l == NLEV:
                        act.wait_ge(s_mu, n - 1)
                        src = b_cum[:]
                    else:
                        act.wait_ge(s_df, (NLEV + 1) * hh + min(l, NLEV) + 1)
                    nc.scalar.activation(dec[:, l % 2], src, ACT.Exp, scale=1.0 / TAU).then_inc(s_ex, 1)
                act.wait_ge(s_ss, (NLEV + 2) * (hh + 1))
                if hh >= 1:
                    act.wait_ge(s_kv, 8 * hh)
                n = (NLEV + 2) * hh + NLEV + 1
                for b in range(2):
                    nc.scalar.activation(k_tok[:, 4 * b:4 * b + 4], banks[2 * (n % 2) + b][:].rearrange("p (j m) -> p j m", j=4), ACT.Copy).then_inc(s_kt, 1)
                act.wait_ge(s_go, hh + 1)
                for b in range(2):
                    nc.scalar.activation(o_a[:, hh, b * 512:(b + 1) * 512], banks[b][:], ACT.Copy).then_inc(s_oe, 1)
                    nc.scalar.activation(o_a[half, 4 + hh // 2, b * 512:(b + 1) * 512], banks[2 + b][half], ACT.Copy).then_inc(s_oe, 1)
                act.wait_ge(s_st, 8 * (hh + 1))
                act.dma_start(gstate_d[hh], st[:, NBLK - 1]).then_inc(s_gst, 16)
            act.wait_ge(s_cp, 8 * H)
            act.dma_start(st_smp[:], state_d.rearrange("h p b e -> p h b e")).then_inc(s_sin, 16)
            act.wait_ge(s_spill[0], 48)
            act.wait_ge(s_spill[1], 48)
            act.dma_start(g_a[:], g_spill).then_inc(s_gland, 16)
            for hh in range(H):
                half = slice(HD * (hh % 2), HD * (hh % 2) + HD)
                act.wait_ge(s_sn, 8 * (hh + 1))
                act.dma_start(sstate_d[hh], st_smp[:, hh]).then_inc(s_sout, 16)
                act.wait_ge(s_so, hh + 1)
                nc.scalar.activation(o_a[:, hh, SEQ:T], banks[4 * (hh % 2)][:, 0:NB], ACT.Copy).then_inc(s_soe, 1)
                nc.scalar.activation(o_a[half, 4 + hh // 2, SEQ:T], banks[4 * (hh % 2) + 1][half, 0:NB], ACT.Copy).then_inc(s_soe, 1)
            act.wait_ge(s_gland, 16)
            nc.scalar.activation(g_a[:], g_a[:], ACT.Silu).then_inc(s_gsil, 1)
            act.wait_ge(s_sout, 16 * H)
            act.wait_ge(s_soe, 2 * H)
            for c in range(NCH):
                if c >= 1:
                    act.wait_ge(s_osum, 6 * c)
                nc.scalar.activation(o_sq[:], o_a[:, :, chunk(c)], ACT.Square).then_inc(s_osq, 1)
                if c >= 1:
                    act.wait_ge(s_onm, c)
                for r in range(6):
                    act.wait_ge(s_osum, 6 * c + r + 1)
                    nc.scalar.activation(o_rs[:, r], banks[r][:, 0:CH], ACT.Ln, scale=1.0 / DV, bias=EPS).then_inc(s_oln, 1)
                act.wait_ge(s_oln, 6 * (c + 1))
                nc.scalar.activation(o_rs[:], o_rs[:], ACT.Exp, scale=-0.5).then_inc(s_ors, 1)
            act.wait_ge(s_tok, NCH)
            for c in range(NCH):
                nc.scalar.activation(x_hi[:, 0:6, chunk(c)], tok_a[:, :, chunk(c)], ACT.Copy).then_inc(s_chi, 1)
                nc.scalar.activation(x_hi[:, 6:8, chunk(c)], mq_a[:, :, chunk(c)], ACT.Copy).then_inc(s_chi, 1)
            act.wait_ge(s_clo, 2 * NCH)
            act.dma_start(h[:], x_d).then_inc(s_h, 16)

            def residual_squares(L):
                for n in range(3 * KT):
                    t, c = n // 3, n % 3
                    act.wait_ge(s_res, 24 * L + n + 1)
                    if n >= 8:
                        act.wait_ge(s_tacc, 18 * L + n - 7)
                    nc.scalar.activation(sq[:, c] if t == 0 else sq[:, 3 + n % 5], h[:, t, chunk(c)], ACT.Square).then_inc(s_tsq, 1)

            residual_squares(0)

            def norm_after_residual(norm):
                norm_rstd(norm, CH, rstd)
                norm_rstd(norm + 1, CH, rstd)
                norm_hi(norm, x_hi[:, :, chunk(0)])
                norm_rstd(norm + 2, CH, rstd)
                norm_hi(norm + 1, x_hi[:, :, chunk(1)])
                norm_hi(norm + 2, x_hi[:, :, chunk(2)])

            def swiglu(L, norm, u0, mm0):
                norm_after_residual(norm)

                def step(j, first=False):
                    def at_(base, k):
                        return base if first else k * j + base
                    for f in range(2):
                        for c in range(NCH):
                            if c < NCH - 1:
                                act.wait_ge(s_mm, at_(mm0 + (2 * c + 1 if first and f == 0 else 4 * f + c + 1), MM_FF))
                            else:
                                act.wait_ge(s_wused, at_(u0 + 2 * f + 1, 6))
                            done = 6 * JFF * L + 3 * f + c - 2
                            if done > 0 or not first:
                                act.wait_ge(s_hid, at_(done, 6))
                            nc.scalar.activation(sil[:, c], banks[c][:, 0:CH], ACT.Silu).then_inc(s_sil, 1)
                        for c in range(NCH):
                            act.wait_ge(s_hid, at_(6 * JFF * L + 3 * f + c + 1, 6))
                            nc.scalar.activation(hid_hi[:, f, chunk(c)], hid[:, c], ACT.Copy).then_inc(s_hhi, 1)

                step(0, first=True)
                with act.Fori(1, JFF) as j:
                    step(j)

            swiglu(0, NORM_A2, U_FFA, MM_FFA)

            def norm_square(c):
                act.wait_ge(s_down, 24 * (JFF - 1) + KT * (c + 1))
                square(SQ_KV + c, NORM_KV + c, h[:, :, chunk(c)], CH)
            norm_square(0)
            norm_rstd(NORM_KV, CH, rstd_b)
            norm_square(1)
            norm_hi(NORM_KV, x_hi[:, :, chunk(0)])
            norm_rstd(NORM_KV + 1, CH, rstd_b)
            norm_square(2)
            norm_hi(NORM_KV + 1, x_hi[:, :, chunk(1)])
            act.dma_start(rope[:], rope_d).then_inc(s_rope, 16)

            for n, (t, c) in enumerate(STEPS_B):
                tile_ready(act, MM_KV, U_KV, t, c)
                nc.scalar.activation(dest_b(t)[0][:, chunk(c)], banks[n % 3][:, 0:CH], ACT.Copy).then_inc(s_ev, 1)
                if n < NB_NORM:
                    act.wait_ge(s_ev, EV_KV + n + 1)
                    head_square(HN_B + n, HEAD_B[n][0])
                if n == 0:
                    norm_rstd(NORM_KV + 2, CH, rstd_b)
                if 1 <= n <= NB_NORM:
                    head_rstd(HN_B + n - 1, CH)
                if n == 1:
                    norm_hi(NORM_KV + 2, x_hi[:, :, chunk(2)])
                mem_attention(1, n)
            act.wait_ge(s_wused, U_KV + NB_IN)
            act.wait_ge(s_ev, EV_END)
            act.dma_start(ck[:], cmk_d[1]).then_inc(s_cache, 16)
            act.dma_start(cv[:], cmv_d[1]).then_inc(s_cache, 16)
            act.dma_start(vwin_d, v_b[:]).then_inc(s_out, 16)
            mem_samples(1)

            act.wait_ge(s_rok, len(ROPE_B))
            act.dma_start(kwin_d, k_b[:]).then_inc(s_out, 16)
            act.dma_start(tri_raw[:], tri_d).then_inc(s_tri_in, 16)
            act.dma_start(sel_raw[:], sel_d).then_inc(s_sel_in, 16)
            for i in range(NW * H):
                hh, w = i // NW, i % NW
                act.wait_ge(s_w2, i + 1)
                if i >= 2:
                    act.wait_ge(s_wo, i - 1)
                n = len(W_STEPS[w][1])
                nc.scalar.activation(pw[:, i % 2, 0:n], banks[i % 4][:, 0:n * P].rearrange("p (n m) -> p n m", n=n), ACT.Exp,
                                     scale=HD ** -0.5).then_inc(s_we, 1)
                if w == 1 and hh >= 1 or i == NW * H - 1:
                    done = hh if w == 1 else hh + 1
                    act.wait_ge(s_wo, NW * done)
                    if done >= 2:
                        act.wait_ge(s_wod, done - 1)
                    for b in range(2):
                        nc.scalar.activation(o_sb[:, 512 * b:512 * b + 512], banks[4 + b][:], ACT.Copy).then_inc(s_woc, 1)
            act.wait_ge(s_wod, H)
            act.dma_start(wk[:, :, :, :, 0:P], wink_d).then_inc(s_wc, 16)
            act.dma_start(wv[:], winv_d).then_inc(s_wc, 16)
            act.wait_ge(s_db, 1)
            nc.scalar.activation(pd[:], banks[0][0:32, 0:3 * NWIN].rearrange("p (g m) -> p g m", g=3), ACT.Exp, scale=HD ** -0.5,
                                 bias=wst[:, 1:2], accum_out=wst[:, 2:3]).then_inc(s_de, 1)
            act.wait_ge(s_dpt_, 1)
            nc.scalar.activation(pdt[:], banks[1][:, 0:96].rearrange("p (g m) -> p g m", g=3), ACT.Copy).then_inc(s_dptk_, 1)
            act.wait_ge(s_dok, 2)
            for c in range(NCH):
                nc.scalar.activation(x_hi[:, 0:2, chunk(c)], tok_b[:, :, chunk(c)], ACT.Copy).then_inc(s_chi, 1)
                nc.scalar.activation(x_hi[:, 2:4, chunk(c)], mq_b[:, :, chunk(c)], ACT.Copy).then_inc(s_chi, 1)
            residual_squares(1)
            swiglu(1, NORM_B2, U_FFB, MM_FFB)
            for c in range(NCH):
                act.wait_ge(s_down, 48 * JFF - KT * (NCH - 1 - c))
                act.dma_start(y_d[:, :, chunk(c)], h[:, :, chunk(c)]).then_inc(s_out, 16)
            act.wait_ge(s_out, 16 * 7)

        @block.vector
        def _(dve):
            def fold(i, n, width):
                v = sq[:, :, 0:width]
                dve.wait_ge(s_sq, i + 1)
                nc.vector.tensor_tensor(v[:, 0:4], v[:, 0:4], v[:, 4:8], ALU.add).then_inc(s_f1, 1)
                dve.wait_ge(s_f1, i + 1)
                nc.vector.tensor_tensor(v[:, 0:2], v[:, 0:2], v[:, 2:4], ALU.add).then_inc(s_fold, 1)

            def norm_apply(n, src, g0, rs, dst=None, inc=True):
                w = src.shape[2]
                dve.wait_ge(s_rs, n + 1)
                for k in range(KT):
                    op = nc.vector.scalar_tensor_tensor(out=dst[:, k], in0=src[:, k], scalar=gain[:, g0 + k:g0 + k + 1],
                                                        in1=rs[:, n % 2, 0:w], op0=ALU.mult, op1=ALU.mult)
                if inc:
                    op.then_inc(s_xt, 1)

            def norm_lo(n, dst, hi, src):
                dve.wait_ge(s_hi, n + 1)
                nc.vector.tensor_tensor(dst, src, hi.bitcast(F32), ALU.subtract).then_inc(s_lo, 1)

            def apply_chunk(n, c, g0, rs):
                if n >= 1:
                    dve.wait_ge(s_lo, n)
                norm_apply(n, h[:, :, chunk(c)], g0, rs, xt)

            def lo_chunk(n, c):
                norm_lo(n, x_lo[:, :, chunk(c)], x_hi[:, :, chunk(c)], xt[:])

            def head_apply(i, src, g, dst):
                dve.wait_ge(s_hrs, i + 1)
                nc.vector.scalar_tensor_tensor(out=dst, in0=src, scalar=gain[:, g:g + 1], in1=rstd[:, i % 2, 0:src.shape[1]],
                                               op0=ALU.mult, op1=ALU.mult).then_inc(s_hn, 1)

            dve.wait_ge(s_gain, 16)
            dve.wait_ge(s_mem, 16)
            fold(0, 0, MEM)
            norm_apply(0, mt, G_MN, rstd, mem_xt[:, 0], inc=False)
            norm_apply(0, mt, G_MN + KT, rstd, mem_xt[:, 1])
            norm_lo(0, x_lo[:, :, T - 2 * MEM:T].rearrange("p k (l m) -> p l k m", l=2),
                    x_hi[:, :, T - 2 * MEM:T].rearrange("p k (l m) -> p l k m", l=2), mem_xt[:])
            for c in range(NCH):
                dve.wait_ge(s_x[c], 16)
            fold(SQ_A1, NORM_A1, CH)
            apply_chunk(NORM_A1, 0, G_N1, rstd_b)
            fold(SQ_A1 + 1, NORM_A1 + 1, CH)
            lo_chunk(NORM_A1, 0)
            apply_chunk(NORM_A1 + 1, 1, G_N1, rstd_b)
            fold(SQ_A1 + 2, NORM_A1 + 2, CH)
            lo_chunk(NORM_A1 + 1, 1)
            for i in range(4):
                dve.wait_ge(s_mvT, i + 1)
                nc.vector.tensor_copy(mv_t[:, i // 2, i % 2], banks[3 + i % 2][:, 0:MEM]).then_inc(s_mvt, 1)

            def mem_attention(L, mq, n):
                if n in MEM_AT[L]:
                    a = NBLK * L + MEM_AT[L].index(n)
                    dve.wait_ge(s_sc, a + 1)
                    if a >= 1:
                        dve.wait_ge(s_pe, a)
                        dve.wait_ge(s_nb, a)
                    for par in range(2):
                        nc.vector.tensor_reduce(nmax[:, 2 * par:2 * par + 2], banks[3 + par][:].rearrange("p (r m) -> p r m", r=2),
                                                AX.X, ALU.max, negate=True).then_inc(s_mx, 1)
                    dve.wait_ge(s_mx, 2 * a + 2)
                    nc.vector.tensor_scalar(nbias, nmax, HD ** -0.5, None, ALU.mult).then_inc(s_nb, 1)
                if n - 1 in MEM_AT[L]:
                    a = NBLK * L + MEM_AT[L].index(n - 1)
                    dve.wait_ge(s_pe, a + 1)
                    if a >= 1:
                        dve.wait_ge(s_pn, a)
                    nc.vector.reciprocal(rsums, psums).then_inc(s_ra, 1)
                    dve.wait_ge(s_ra, a + 1)
                    for j in range(H):
                        op = nc.vector.tensor_scalar(mem_pr[L][:, j], mem_pr[L][:, j], rsums[:, j:j + 1], None, ALU.mult)
                    op.then_inc(s_pn, 1)
                if n - 4 in MEM_AT[L]:
                    i = MEM_AT[L].index(n - 4)
                    dve.wait_ge(s_po, NBLK * L + i + 1)
                    nc.vector.tensor_copy(mq[:, :, i * P:(i + 1) * P], banks[5][:, 0:2 * P].rearrange("p (r m) -> p r m", r=2)).then_inc(s_pok, 1)

            for n in range(3 * NA_IN):
                if 1 <= n <= len(HEAD_A):
                    head_apply(HN_MK + n - 1, *HEAD_A[n - 1])
                if n == 0:
                    apply_chunk(NORM_A1 + 2, 2, G_N1, rstd_b)
                if n == 1:
                    lo_chunk(NORM_A1 + 2, 2)
                mem_attention(0, mq_a, n)
                i, b = divmod(n - 3 * (A_V[0] + 1), 3)
                if 0 <= i < 6:
                    dve.wait_ge(s_vT, 3 * i + b + 1)
                    if b < 2:
                        nc.vector.tensor_copy(v_tok[:, 4 * b:4 * b + 4, i * P:(i + 1) * P], banks[7][:].rearrange("p (j m) -> p j m", j=4)).then_inc(s_vt, 1)
                    else:
                        nc.vector.tensor_copy(vs_a[:, i * P:(i + 1) * P], banks[7][0:NB, 0:P]).then_inc(s_vt, 1)

            def mem_samples(L, mq, used):
                sel = (slice(0, HD), slice(HD, P))
                dve.wait_ge(s_wused, used)
                nc.vector.memset(q_blk[:], 0.0).then_inc(s_qz, 1)
                dve.wait_ge(s_qz, L + 1)
                for t in range(2):
                    for par in range(2):
                        diag = bass.AP(q_blk[sel[par], t].tensor, q_blk[sel[par], t].offset + 2 * t + par, [[2 * NB * 32, HD], [36, NB]])
                        nc.vector.tensor_copy(diag, mq[sel[par], t, SEQ:T]).then_inc(s_qb, 1)
                dve.wait_ge(s_dsc, L + 1)
                nc.vector.tensor_reduce(dst4[:, 0:1], banks[0][0:32, 0:MEM], AX.X, ALU.max, negate=True).then_inc(s_dmx, 1)
                dve.wait_ge(s_dmx, L + 1)
                nc.vector.tensor_scalar(dst4[:, 1:2], dst4[:, 0:1], HD ** -0.5, None, ALU.mult).then_inc(s_dnb, 1)
                dve.wait_ge(s_dpe, L + 1)
                nc.vector.reciprocal(dst4[:, 3:4], dst4[:, 2:3]).then_inc(s_dra, 1)
                dve.wait_ge(s_dra, L + 1)
                nc.vector.tensor_scalar(dp[:], dp[:], dst4[:, 3:4], None, ALU.mult).then_inc(s_dpn, 1)
                dve.wait_ge(s_dpo, L + 1)
                for par in range(2):
                    nc.vector.tensor_copy(mq[sel[par], :, SEQ:T],
                                          banks[3][sel[par], 0:32].rearrange("p (t b r) -> p t b r", t=2, b=NB)[:, :, :, par]).then_inc(s_dpok, 1)

            mem_samples(0, mq_a, U_AIN + NA_IN)

            dve.wait_ge(s_lvl_in, 16)
            nc.vector.tensor_copy(lvl[:], lvl_raw[:]).then_inc(s_lvl, 1)
            nc.vector.memset(reset[:], 1.0).then_inc(s_rst, 1)
            dve.wait_ge(s_rst, 1)
            nc.vector.memset(reset[:, 0::P], 0.0).then_inc(s_rst2, 1)
            dve.wait_ge(s_ptk, 2 * NBLK)
            dve.wait_ge(s_po, NBLK)
            dve.wait_ge(s_dpo, 1)
            nc.vector.memset(s_acc[:], 0.0).then_inc(s_sz, 1)
            for hh in range(H):
                dve.wait_ge(s_zt, 3 * hh + 3)
                nc.vector.scalar_tensor_tensor(out=ring[:, 0], in0=ring[:, 0], scalar=0.0, in1=ring[:, 1], op0=ALU.min, op1=ALU.subtract).then_inc(s_la, 1)
                dve.wait_ge(s_la, hh + 1)
                dve.wait_ge(s_rst2, 1)
                nc.vector.tensor_tensor_scan(b_cum[:], reset[:], ring[:, 0, 0:SEQ], 0.0, ALU.mult, ALU.add).then_inc(s_bc, 1)
                dve.wait_ge(s_bc, hh + 1)
                N9 = NLEV + 2

                def halves(t2d, s):
                    v = t2d.rearrange("p (n h s) -> p n h s", h=2, s=s)
                    return v[:, :, 0], v[:, :, 1]

                def exponents(l):
                    n = N9 * hh + l
                    if n >= 2:
                        dve.wait_ge(s_mu, n - 1)
                    if l < NLEV:
                        s = 2 ** l
                        lo_, hi_ = halves(b_cum[:], s)
                        dlo, dhi = halves(dec[:, l % 2], s)
                        ref = lo_[:, :, s - 1:s].broadcast_to(list(lo_.shape))
                        nc.vector.tensor_tensor(dlo, ref, lo_, ALU.subtract)
                        nc.vector.tensor_tensor(dhi, hi_, ref, ALU.subtract).then_inc(s_df, 1)
                    elif l == NLEV + 1:
                        v = b_cum[:].rearrange("p (n s) -> p n s", s=P)
                        nc.vector.tensor_tensor(dec[:, l % 2].rearrange("p (n s) -> p n s", s=P), v[:, :, P - 1:P].broadcast_to([P, NBLK, P]), v,
                                                ALU.subtract).then_inc(s_df, 1)

                def decayed(l):
                    n = N9 * hh + l
                    dve.wait_ge(s_ex, n + 1)
                    if l == NLEV:
                        if hh >= 1:
                            dve.wait_ge(s_go, hh)
                        nc.vector.tensor_tensor(q_dec[:], q_a[:, hh, 0:SEQ], dec[:, l % 2], ALU.mult).then_inc(s_mu, 1)
                        return
                    slot = 0 if l == NLEV + 1 else l % 2
                    if l == 0 and hh >= 1:
                        dve.wait_ge(s_ss, N9 * hh)
                    if l >= 2:
                        dve.wait_ge(s_ss, N9 * hh + min(l, NLEV) - 1)
                    if l == NLEV + 1:
                        dve.wait_ge(s_ss, N9 * hh + NLEV)
                        nc.vector.tensor_tensor(dqk[:, 0], k_a[:, hh, 0:SEQ], dec[:, l % 2], ALU.mult).then_inc(s_mu, 1)
                        return
                    s = 2 ** l
                    elo, ehi = halves(dec[:, l % 2], s)
                    xlo, xhi = halves(dqk[:, l % 2], s)
                    nc.vector.tensor_tensor(xlo, halves(k_a[:, hh, 0:SEQ], s)[0], elo, ALU.mult)
                    nc.vector.tensor_tensor(xhi, halves(q_a[:, hh, 0:SEQ], s)[1], ehi, ALU.mult).then_inc(s_mu, 1)

                def keep(l):
                    n = N9 * hh + l
                    dve.wait_ge(s_ss, n + 1)
                    if l == 0 and hh >= 1:
                        dve.wait_ge(s_go, hh)
                    if hh == 0 and l == 0:
                        dve.wait_ge(s_sz, 1)
                        dve.wait_ge(s_lvl, 1)
                    if 8 * hh + l >= 1:
                        dve.wait_ge(s_cp, 8 * hh + l)
                    for b in range(2):
                        op = nc.vector.copy_predicated(s_acc[:, 4 * b:4 * b + 4], lvl[:, l:l + 1].broadcast_to([P, 4, P]),
                                                       banks[2 * (n % 2) + b][:].rearrange("p (j m) -> p j m", j=4))
                    op.then_inc(s_cp, 1)

                exponents(0)
                for l in range(N9):
                    if l + 1 < N9:
                        exponents(l + 1)
                    decayed(l)
                    if 1 <= l <= NLEV:
                        keep(l - 1)
                keep(NLEV)
                dve.wait_ge(s_be, hh + 1)
                for b in range(NBLK):
                    dve.wait_ge(s_kv, 8 * hh + 2 * (b // 2) + 2)
                    up = banks[4 + b // 2][:, (b % 2) * DV:(b % 2 + 1) * DV]
                    if b == 0:
                        if hh >= 1:
                            dve.wait_ge(s_gst, 16 * hh)
                            dve.wait_ge(s_go, hh)
                        nc.vector.tensor_copy(st[:, 0], up).then_inc(s_st, 1)
                    else:
                        dve.wait_ge(s_st, 8 * hh + b)
                        nc.vector.scalar_tensor_tensor(out=st[:, b], in0=st[:, b - 1], scalar=b_end[:, b:b + 1], in1=up,
                                                       op0=ALU.mult, op1=ALU.add).then_inc(s_st, 1)

            dve.wait_ge(s_skt, 1)
            nc.vector.tensor_copy(k_smp[:], banks[4][0:NB, :].rearrange("p (h m) -> p h m", h=H)).then_inc(s_skk, 1)
            dve.wait_ge(s_skk, 1)
            dve.wait_ge(s_go, H)
            dve.wait_ge(s_gst, 16 * H)
            for hh in range(H):
                nc.vector.tensor_tensor(k_one[:, hh], k_smp[:, hh:hh + 1].broadcast_to([NB, NB, P]),
                                        ident[0:NB, 0:NB].unsqueeze(2).broadcast_to([NB, NB, P]), ALU.mult).then_inc(s_sk1, 1)
            dve.wait_ge(s_sin, 16)
            dve.wait_ge(s_as, H)
            for hh in range(H):
                dve.wait_ge(s_su, hh + 1)
                for b in range(NB):
                    nc.vector.scalar_tensor_tensor(out=st_smp[:, hh, b], in0=st_smp[:, hh, b], scalar=a_smp[:, hh, b:b + 1],
                                                   in1=banks[4 * (hh % 2) + b // 2][:, (b % 2) * DV:(b % 2 + 1) * DV],
                                                   op0=ALU.mult, op1=ALU.add).then_inc(s_sn, 1)

            for c in range(NCH):
                dve.wait_ge(s_ors, c + 1)
                if c >= 1:
                    dve.wait_ge(s_tok, c)
                for r in range(6):
                    g = G_ON if r < H else G_ON + 1
                    op = nc.vector.scalar_tensor_tensor(out=o_nm[:, r], in0=o_a[:, r, chunk(c)], scalar=gain[:, g:g + 1], in1=o_rs[:, r],
                                                        op0=ALU.mult, op1=ALU.mult)
                op.then_inc(s_onm, 1)
                dve.wait_ge(s_onm, c + 1)
                dve.wait_ge(s_gsil, 1)
                nc.vector.tensor_tensor(tok_a[:, :, chunk(c)], o_nm[:], g_a[:, :, chunk(c)], ALU.mult).then_inc(s_tok, 1)
            for c in range(NCH):
                dve.wait_ge(s_chi, 2 * c + 2)
                nc.vector.tensor_tensor(x_lo[:, 0:6, chunk(c)], tok_a[:, :, chunk(c)], x_hi[:, 0:6, chunk(c)].bitcast(F32), ALU.subtract).then_inc(s_clo, 1)
                nc.vector.tensor_tensor(x_lo[:, 6:8, chunk(c)], mq_a[:, :, chunk(c)], x_hi[:, 6:8, chunk(c)].bitcast(F32), ALU.subtract).then_inc(s_clo, 1)

            def add_residual(nt, mm0, u0, per_unit, n0):
                L = n0 // 24
                for n in range(3 * nt + 2):
                    t, c = n // 3, n % 3
                    if n < 3 * nt:
                        if c < NCH - 1 or t % per_unit < per_unit - 1:
                            dve.wait_ge(s_mm, mm0 + (3 * per_unit - 1) * (t // per_unit) + 3 * (t % per_unit) + c + 1)
                        else:
                            dve.wait_ge(s_wused, u0 + t // per_unit + 1)
                        nc.vector.tensor_tensor(h[:, t, chunk(c)], h[:, t, chunk(c)], banks[n % 6][:, 0:CH], ALU.add).then_inc(s_res, 1)
                    m = n - 2
                    if m >= 3:
                        a = m - 3
                        dve.wait_ge(s_tsq, n0 + m + 1)
                        if a >= 3:
                            dve.wait_ge(s_tacc, 18 * L + a - 2)
                        nc.vector.tensor_tensor(sq[:, m % 3], sq[:, m % 3], sq[:, 3 + m % 5], ALU.add).then_inc(s_tacc if a < 18 else s_fold, 1)

            dve.wait_ge(s_h, 16)
            add_residual(KT, MM_AOUT, U_AOUT, 1, 0)

            def swiglu(L, norm, g0, u0, mm0, last_norm):
                for c in range(NCH):
                    apply_chunk(norm + c, c, g0, rstd)
                    lo_chunk(norm + c, c)

                def step(j, first=False, last=False):
                    def at_(base, k):
                        return base if first else k * j + base
                    for f in range(2):
                        for c in range(NCH + 1):
                            if c < NCH:
                                i = 6 * JFF * L + 3 * f + c
                                dve.wait_ge(s_sil, at_(i + 1, 6))
                                if c < NCH - 1:
                                    dve.wait_ge(s_mm, at_(mm0 + (2 * c + 2 if first and f == 0 else 4 * f + 2 + c + 1), MM_FF))
                                else:
                                    dve.wait_ge(s_wused, at_(u0 + 2 * f + 2, 6))
                                if i >= 3 or not first:
                                    dve.wait_ge(s_hlo, at_(i - 2, 6))
                                nc.vector.tensor_tensor(hid[:, c], sil[:, c], banks[3 + c][:, 0:CH], ALU.mult).then_inc(s_hid, 1)
                            if c >= 1:
                                i = 6 * JFF * L + 3 * f + c - 1
                                dve.wait_ge(s_hhi, at_(i + 1, 6))
                                nc.vector.tensor_tensor(hid_lo[:, f, chunk(c - 1)], hid[:, c - 1], hid_hi[:, f, chunk(c - 1)].bitcast(F32),
                                                        ALU.subtract).then_inc(s_hlo, 1)
                    for c in range(NCH):
                        for m in range(KT):
                            n = KT * c + m
                            if n < 23:
                                dve.wait_ge(s_mm, at_(mm0 + 8 + n + 1, MM_FF))
                            else:
                                dve.wait_ge(s_wused, at_(u0 + 6, 6))
                            i = 24 * JFF * L + n
                            if not first:
                                dve.wait_ge(s_down, at_(i - 23, 24))
                            nc.vector.tensor_tensor(h[:, m, chunk(c)], h[:, m, chunk(c)], banks[n % 6][:, 0:CH], ALU.add).then_inc(s_down, 1)
                            if last:
                                last_norm(n)

                step(0, first=True)
                with dve.Fori(1, JFF - 1) as j:
                    step(j)
                step(JFF - 1, last=True)

            def wide_apply(n, c):
                dve.wait_ge(s_lo, n)
                dve.wait_ge(s_rs, n + 1)
                nc.vector.tensor_tensor(xt[:], h[:, :, chunk(c)], rstd_b[:, n % 2:n % 2 + 1].broadcast_to([P, KT, CH]), ALU.mult).then_inc(s_xt, 1)

            def norm_in_last_step(n):
                if n == KT + 3:
                    fold(SQ_KV, NORM_KV, CH)
                if n == 2 * KT + 1:
                    wide_apply(NORM_KV, 0)
                if n == 2 * KT + 5:
                    fold(SQ_KV + 1, NORM_KV + 1, CH)

            swiglu(0, NORM_A2, G_N2, U_FFA, MM_FFA, norm_in_last_step)
            lo_chunk(NORM_KV, 0)
            wide_apply(NORM_KV + 1, 1)
            fold(SQ_KV + 2, NORM_KV + 2, CH)
            lo_chunk(NORM_KV + 1, 1)
            dve.wait_ge(s_rope, 16)

            for n in range(3 * NB_IN):
                if n == 0:
                    wide_apply(NORM_KV + 2, 2)
                if n == 1:
                    lo_chunk(NORM_KV + 2, 2)
                if 1 <= n <= NB_NORM:
                    x, g, c = HEAD_B[n - 1]
                    head_apply(HN_B + n - 1, x, g, x)
                if n - 2 in ROPE_B:
                    x, g, c = HEAD_B[n - 2]
                    i = ROPE_B.index(n - 2)
                    turned = banks[7][:, 0:CH]
                    dve.wait_ge(s_rsw, i + 1)
                    nc.vector.tensor_tensor(x, x, rope[:, 0, chunk(c)], ALU.mult).then_inc(s_rc, 1)
                    nc.vector.tensor_tensor(turned, turned, rope[:, 1, chunk(c)], ALU.mult).then_inc(s_rs_, 1)
                    dve.wait_ge(s_rc, i + 1)
                    dve.wait_ge(s_rs_, i + 1)
                    nc.vector.tensor_tensor(x, x, turned, ALU.add).then_inc(s_rok, 1)
                mem_attention(1, mq_b, n)
            mem_samples(1, mq_b, U_KV + NB_IN)

            sel2 = (slice(0, HD), slice(HD, P))
            dve.wait_ge(s_dpo, 2)
            nc.vector.memset(v3[:].rearrange("p g n (t x e) -> p (g n t) x e", t=2, e=HD)[:, :, 1], 1.0).then_inc(s_ones3, 1)
            for i in range(12):
                g, b = i // 4, i % 4
                dve.wait_ge(s_v3t, i + 1)
                nc.vector.tensor_copy(v3[:, g, 2 * b:2 * b + 2].rearrange("p n (t x e) -> p (n t) x e", t=2, e=HD)[:, :, 0::2],
                                      banks[i % 4][:].rearrange("p (n x e) -> p n x e", n=4, e=HD)).then_inc(s_v3, 1)
            dve.wait_ge(s_tri_in, 16)
            nc.vector.tensor_copy(tri[:], tri_raw[:]).then_inc(s_tri, 1)
            dve.wait_ge(s_sel_in, 16)
            nc.vector.tensor_copy(sel[:], sel_raw[:]).then_inc(s_sel, 1)
            i = 0
            for hh in range(H):
                for g in range(3):
                    per = 4 if g == 2 else 2
                    for b in range(NBLK // per):
                        dve.wait_ge(s_w1, i + 1)
                        nc.vector.tensor_reduce(m_col[:, g, hh, per * b:per * (b + 1)], banks[i % 4][:].rearrange("p (n m) -> p n m", n=per),
                                                AX.X, ALU.max).then_inc(s_m1, 1)
                        i += 1
            for g in range(3):
                for b in range(2):
                    n = 2 * g + b
                    dve.wait_ge(s_mt, n + 1)
                    src = banks[n % 4][0:H, :]
                    if g == 0:
                        nc.vector.tensor_copy(m_row[:, 512 * b:512 * b + 512], src).then_inc(s_mr, 1)
                        continue
                    dve.wait_ge(s_mr, n if g == 1 else 4 + b)
                    src = src.rearrange("p (n m) -> p n m", n=4)
                    nc.vector.tensor_tensor(tokens_of4(m_row[:], g, b), tokens_of4(m_row[:], g, b), src, ALU.max).then_inc(s_mr, 1)
            dve.wait_ge(s_mr, 6)
            nc.vector.tensor_scalar(nm_row[:], m_row[:], -1.0, None, ALU.mult).then_inc(s_nm, 1)
            for hh in range(H):
                dve.wait_ge(s_wo, NW * (hh + 1))
                for b in range(2):
                    dve.wait_ge(s_woc, 2 * hh + 2)
                    if b:
                        dve.wait_ge(s_wok, 2 * hh + 1)
                    v = tokens_of4(o_sb[:], 2, b)
                    nc.vector.tensor_tensor(v, v, banks[6 + b][:].rearrange("p (n m) -> p n m", n=4), ALU.add).then_inc(s_wok, 1)
                dve.wait_ge(s_wok, 2 * hh + 2)
                if hh >= 1:
                    dve.wait_ge(s_wod, hh)
                own, sums = sel2[hh % 2], sel2[1 - hh % 2]
                nc.vector.reciprocal(o_rl[own], o_sb[sums]).then_inc(s_wor, 1)
                dve.wait_ge(s_wor, hh + 1)
                nc.vector.tensor_tensor(tok_b[own, hh // 2, 0:SEQ], o_sb[own], o_rl[own], ALU.mult).then_inc(s_wod, 1)
            dve.wait_ge(s_wod, H)
            nc.vector.memset(qw_blk[:], 0.0).then_inc(s_wqz, 1)
            dve.wait_ge(s_wqz, 1)
            for g in range(3):
                for t in range(2):
                    for par in range(2):
                        v = qw_blk[sel2[par], g, t]
                        diag = bass.AP(v.tensor, v.offset + 2 * t + par, [[3 * 2 * NB * 32, HD], [36, NB]])
                        nc.vector.tensor_copy(diag, q_b[sel2[par], 2 * g + t, SEQ:T]).then_inc(s_wqb, 1)
            dve.wait_ge(s_wc, 32)
            for g in range(3):
                nc.vector.tensor_copy(wk[:, :, g, :, P], k_b[:, :, SEQ:T]).then_inc(s_wkn, 1)
            dve.wait_ge(s_d1, 1)
            nc.vector.tensor_reduce(wst[:, 0:1], banks[0][0:32, 0:3 * NWIN], AX.X, ALU.max, negate=True).then_inc(s_dm, 1)
            dve.wait_ge(s_dm, 1)
            nc.vector.tensor_scalar(wst[:, 1:2], wst[:, 0:1], HD ** -0.5, None, ALU.mult).then_inc(s_db, 1)
            dve.wait_ge(s_de, 1)
            nc.vector.reciprocal(wst[:, 3:4], wst[:, 2:3]).then_inc(s_dr, 1)
            dve.wait_ge(s_dr, 1)
            nc.vector.tensor_scalar(pd[:], pd[:], wst[:, 3:4], None, ALU.mult).then_inc(s_dp, 1)
            dve.wait_ge(s_dp, 1)
            nc.vector.tensor_reduce(wst[:, 4:5], pd[:, :, P], AX.X, ALU.add).then_inc(s_dpn_, 1)
            dve.wait_ge(s_dpn_, 1)
            nc.vector.tensor_scalar(wst[:, 8:16], smp_col, wst[:, 4:5], None, ALU.mult).then_inc(s_dn, 1)
            dve.wait_ge(s_dnb_, 1)
            nc.vector.tensor_tensor(v_new[:], banks[2][:, 0:2 * NB].rearrange("p (t b) -> p t b", t=2), v_b[:, :, SEQ:T], ALU.mult).then_inc(s_dvn, 1)
            dve.wait_ge(s_dvn, 1)
            dve.wait_ge(s_do, 1)
            for par in range(2):
                nc.vector.tensor_tensor(tok_b[sel2[par], :, SEQ:T], banks[3][sel2[par], 0:32].rearrange("p (t b r) -> p t b r", t=2, b=NB)[:, :, :, par],
                                        v_new[sel2[par]], ALU.add).then_inc(s_dok, 1)
            for c in range(NCH):
                dve.wait_ge(s_chi, 2 * NCH + 2 * c + 2)
                nc.vector.tensor_tensor(x_lo[:, 0:2, chunk(c)], tok_b[:, :, chunk(c)], x_hi[:, 0:2, chunk(c)].bitcast(F32), ALU.subtract).then_inc(s_clo, 1)
                nc.vector.tensor_tensor(x_lo[:, 2:4, chunk(c)], mq_b[:, :, chunk(c)], x_hi[:, 2:4, chunk(c)].bitcast(F32), ALU.subtract).then_inc(s_clo, 1)
            add_residual(KT, MM_BOUT, U_BOUT, 2, 24)
            swiglu(1, NORM_B2, G_N2 + KT, U_FFB, MM_FFB, lambda n: None)



_OUTS = [("y", (P, KT, T)), ("gstate", (H, P, DV)), ("sstate", (H, P, NB, DV)), ("kwin", (P, 2, T)), ("vwin", (P, 2, T)),
         ("mk", (P, 2, 2, MEM)), ("mv", (P, 2, 2, MEM))]

_E_ORDER = np.concatenate([np.arange(hh * DV, hh * DV + P) for hh in range(H)]
                          + [np.arange(hh * DV + P, (hh + 1) * DV) for hh in range(H)])


def _constants():
    i = np.arange(P)
    half = i // 64
    ident = np.eye(P)
    head = (half[:, None] == half[None, :]) * 1.0
    low = np.tile((i[None, :] < 64) * 1.0, (P, 1))
    swap = (i[:, None] == (i[None, :] ^ 32)) * 1.0
    smp = (i[:, None] // H == np.arange(NB)[None, :]) * 1.0
    smp_head = (i[:, None, None] % H == 2 * np.arange(2)[None, :, None] + half[None, None, :]).reshape(P, 2 * P) * 1.0
    cst = np.concatenate([ident, np.ones((P, P)), head, low, 1.0 - low, swap, smp, smp_head], axis=1).astype(np.float32)
    lvl = []
    for s in (1, 2, 4, 8, 16, 32, 64):
        same = (i[:, None] // (2 * s)) == (i[None, :] // (2 * s))
        lvl.append(same & (i[:, None] % (2 * s) < s) & (i[None, :] % (2 * s) >= s))
    lvl.append(np.eye(P, dtype=bool))
    lvl = np.stack(lvl, 1).astype(np.float32)
    ge = i[None, :] >= i[:, None]
    no = -1e30
    turn = i[:, None] % 2 == i[None, :] % 2
    tri = np.stack([ident, np.where(ge, 0, no), np.where(ge.T, 0, no),
                    np.where(ge & turn, 0, no), np.where(ge.T & turn, 0, no)], 1).astype(np.float32)
    sel = np.zeros((H, H, P), np.float32)
    for hh in range(H):
        sel[hh, hh] = 1.0
    pos = np.concatenate([np.arange(SEQ), np.full(NB, 2048)]).astype(np.float32)
    half_n = HD // 2
    inv = (10000.0 ** (-np.arange(half_n) / half_n)).astype(np.float32)
    ang = (pos[None, :] * inv[:, None].astype(np.float32)).astype(np.float32)
    cos, sin = np.cos(ang), np.sin(ang)
    rope = np.stack([np.concatenate([cos] * 4), np.concatenate([-sin, sin] * 2)], 1).astype(np.float32)
    return cst, lvl, tri, sel, rope


def _tiles(w):
    k, n = w.shape
    if n % P:
        w = np.concatenate([w, np.zeros((k, P - n % P), w.dtype)], 1)
    return w.reshape(KT, P, -1, P).transpose(2, 1, 0, 3).reshape(-1, P, KT * P)


def _ffn_units(gu, down):
    g, u = _tiles(gu[:, :FF]), _tiles(gu[:, FF:])
    d = down.reshape(FF // P, P, D)
    order = [x for j in range(JFF) for x in (g[2 * j], u[2 * j], g[2 * j + 1], u[2 * j + 1], d[2 * j], d[2 * j + 1])]
    return np.stack(order)


def _rows(a):
    return a.T.reshape(-1, P, a.shape[0]).transpose(1, 0, 2)


def kernel(x_prompt, x_sample, state_gla, cache_win_k, cache_win_v, cache_mem_k, cache_mem_v, mem_prompt,
           norm1, norm2, a_w_in, a_w_gate2, a_b_gate, a_g_onorm, a_w_out, kv_norm, w_kv, g_k, b_w_in, b_g_q,
           b_w_out, mem_norm, w_mem_kv, g_mem_q, g_mem_k, w_ffn_gu, w_ffn_down):
    import concourse.bacc as bacc
    from concourse.bass_utils import run_bass_kernel_spmd

    f = np.ascontiguousarray
    a = lambda x: np.asarray(x)
    (x_prompt, x_sample, state_gla, cache_win_k, cache_win_v, cache_mem_k, cache_mem_v, mem_prompt,
     norm1, norm2, a_w_in, a_w_gate2, a_b_gate, a_g_onorm, a_w_out, kv_norm, w_kv, g_k, b_w_in, b_g_q,
     b_w_out, mem_norm, w_mem_kv, g_mem_q, g_mem_k, w_ffn_gu, w_ffn_down) = map(a, (
         x_prompt, x_sample, state_gla, cache_win_k, cache_win_v, cache_mem_k, cache_mem_v, mem_prompt,
         norm1, norm2, a_w_in, a_w_gate2, a_b_gate, a_g_onorm, a_w_out, kv_norm, w_kv, g_k, b_w_in, b_g_q,
         b_w_out, mem_norm, w_mem_kv, g_mem_q, g_mem_k, w_ffn_gu, w_ffn_down))
    cst, lvl, tri, sel, rope = _constants()
    x = _rows(np.concatenate([x_prompt[0], x_sample[:, 0]], 0))
    w = a_w_in[0]
    q, k, v, g, r, mq = np.split(w, [512, 1024, 1792, 2560, 2576], axis=1)
    w_in = np.concatenate([mq, r, np.zeros((D, 112), w.dtype), q, k, v, g[:, _E_ORDER]], 1)
    w_out = np.concatenate([a_w_out[0][:768][_E_ORDER], a_w_out[0][768:]], 0)
    w_b = np.concatenate([b_w_in[0][:, 768:], w_kv[:, :256], b_w_in[0][:, :768], w_kv[:, 256:]], 1)
    b_out = b_w_out[0].reshape(4, P, 4, 2, P).transpose(2, 1, 3, 0, 4).reshape(4, P, 1024)
    weights = np.concatenate([_tiles(w_mem_kv[0]), _tiles(w_mem_kv[1]), _tiles(w_in), _tiles(w_out),
                              _ffn_units(w_ffn_gu[0], w_ffn_down[0]), _tiles(w_b), b_out,
                              _ffn_units(w_ffn_gu[1], w_ffn_down[1])], 0)
    assert weights.shape == (NUNIT, P, 1024)
    col = lambda v: v.reshape(-1, P).T
    two = lambda v: np.tile(v, 2)[:, None]
    gains = np.concatenate([col(norm1.reshape(-1)), col(norm2.reshape(-1)), col(kv_norm), col(mem_norm.reshape(-1)),
                            two(g_mem_q[0]), two(g_mem_q[1]), two(g_mem_k[0]), two(g_mem_k[1]), two(b_g_q[0]), two(g_k),
                            a_g_onorm[0][:P, None], two(a_g_onorm[0][P:]), col(a_b_gate[0])], 1)
    ck = cache_mem_k.reshape(2, NB, MEM, 2, P).transpose(0, 4, 3, 1, 2)
    cv = cache_mem_v.reshape(2, NB, 2, P, 256).transpose(0, 3, 2, 1, 4)
    n_past = cache_win_k.shape[1]
    rows = [n_past - dil * np.arange(1, win // dil + 1) for win, dil in GROUPS]
    wk = np.stack([cache_win_k[:, ix] for ix in rows]).reshape(3, NB, P, 2, P).transpose(4, 3, 0, 1, 2)
    wv = np.stack([cache_win_v[:, ix] for ix in rows]).reshape(3, NB, P, 256).transpose(2, 0, 1, 3)
    arrays = dict(x=x, mem=_rows(mem_prompt[0]), w=weights, cst=cst, lvl=lvl, tri=tri, gain=gains, gate2=a_w_gate2[0],
                  sel=sel, rope=rope, state=state_gla[0].transpose(1, 2, 0, 3), cmk=ck, cmv=cv, wink=wk, winv=wv)
    arrays = {f"in_{n}": f(v) for n, v in arrays.items()}
    nc = bacc.Bacc("TRN2", target_bir_lowering=False, num_devices=1)
    args = [nc.dram_tensor(n, v.shape, mybir.dt.from_np(v.dtype), kind="ExternalInput").ap() for n, v in arrays.items()]
    args += [nc.dram_tensor(f"out_{n}", s, F32, kind="ExternalOutput").ap() for n, s in _OUTS]
    trunk_program(nc, *args)
    r = run_bass_kernel_spmd(nc, [arrays], core_ids=[0]).results[0]
    y = r["out_y"].transpose(2, 1, 0).reshape(T, D)
    rows_of = lambda name: r[name].transpose(2, 1, 0).reshape(T, H, HD)
    kw, vw = rows_of("out_kwin"), rows_of("out_vwin")
    mem_out = lambda name: r[name].transpose(1, 3, 2, 0).reshape(2, 1, MEM, H, HD)
    return (y[:SEQ].reshape(1, SEQ, D), y[SEQ:].reshape(NB, 1, D),
            r["out_gstate"].reshape(1, 1, H, P, DV), r["out_sstate"].transpose(2, 0, 1, 3).reshape(1, NB, H, P, DV),
            kw[:SEQ].reshape(1, SEQ, H, HD), vw[:SEQ].reshape(1, SEQ, H, HD),
            kw[SEQ:].reshape(NB, 1, H, HD), vw[SEQ:].reshape(NB, 1, H, HD),
            mem_out("out_mk"), mem_out("out_mv"))
```

```python
from contextlib import ExitStack

import numpy as np

import concourse.bass as bass
from concourse import mybir

F32 = mybir.dt.float32
F32R = mybir.dt.float32r
BF16 = mybir.dt.bfloat16
U8 = mybir.dt.uint8
ACT = mybir.ActivationFunctionType
ALU = mybir.AluOpType
AX = mybir.AxisListType

P = 128
D = 1024
KT = D // P
SEQ, NB = 1024, 8
T = SEQ + NB
CH = T // 3
NCH = 3
MEM = 256
HD = 64
H = 4
DV = 192
NBLK = SEQ // P
FF = 2816
JFF = FF // (2 * P)
EPS = 1e-6
WSLOT = 3
NWIN = 129
GROUPS = ((P, 1), (512, 4), (2048, 16))

A_M, A_R, A_Q, A_K, A_V, A_G = range(0, 2), (2,), range(3, 7), range(7, 11), range(11, 17), range(17, 23)
NA_IN = 23
B_M, B_K, B_Q, B_V = range(0, 2), range(2, 4), range(4, 10), range(10, 12)
NB_IN = 12
NB_NORM = 30

U_MEM = 0
U_AIN = U_MEM + 8
U_AOUT = U_AIN + NA_IN
U_FFA = U_AOUT + KT
U_KV = U_FFA + 6 * JFF
U_BOUT = U_KV + NB_IN
U_FFB = U_BOUT + 4
NUNIT = U_FFB + 6 * JFF

G_N1, G_N2, G_KV, G_MN = 0, 16, 32, 40
G_MQ, G_MK, G_Q, G_K, G_ON, G_BIAS = 56, 58, 60, 61, 62, 64
NG = 68


def chunk(c):
    return slice(c * CH, (c + 1) * CH)

NCST = 776


def steps_of(nt):
    return [(t, c) for c in range(NCH) for t in range(3)] + [(t, c) for t in range(3, nt) for c in range(NCH)]


def tokens_of(view, g, blk):
    if g == 0:
        return view[:, blk * P:(blk + 1) * P]
    if g == 1:
        r, nb = blk % 4, blk // 4
        return view[:, r + 512 * nb:r + 512 * nb + 509:4]
    return view[:, blk:blk + SEQ - 7:8]


def tokens_of4(view, g, b):
    if g == 0:
        return view[:, 512 * b:512 * b + 512].rearrange("p (n m) -> p n m", n=4)
    if g == 1:
        return view[:, 512 * b:512 * b + 512].rearrange("p (m r) -> p r m", r=4)
    return view[:, 0:SEQ].rearrange("p (m c) -> p c m", c=8)[:, 4 * b:4 * b + 4]


def key_blocks(g, blk):
    before = {0: blk - 1 if blk >= 1 else None, 1: blk - 4 if blk >= 4 else None, 2: None}[g]
    return ([(before, True)] if before is not None else []) + [(blk, False)]


W_STEPS = [(0, range(0, 4), 0, False), (0, range(4, 8), 0, False), (0, range(1, 4), 1, True), (0, range(4, 8), 1, True),
           (1, range(0, 4), 0, False), (1, range(4, 8), 0, False), (1, range(4, 8), 4, True),
           (2, range(0, 4), 0, False), (2, range(4, 8), 0, False)]
NW = len(W_STEPS)


def trunk_program(nc, x_d, mem_d, w_d, cst_d, lvl_d, tri_d, gain_d, gate2_d, sel_d, rope_d, state_d,
                  cmk_d, cmv_d, wink_d, winv_d,
                  y_d, gstate_d, sstate_d, kwin_d, vwin_d, mk_d, mv_d):
    ctx = ExitStack()
    with ctx:
        def at(name, shape, offset, dt=F32):
            return nc.alloc_sbuf_tensor_at(name, shape, dt, offset=offset)

        def bank(i):
            return ctx.enter_context(nc.psum_tensor(f"bank{i}", [P, 512], F32))

        def sem(name):
            return ctx.enter_context(nc.semaphore(name))

        ROW = T * 4
        O_W = 16512
        w_raw = at("w_raw", [P, WSLOT, 1024], O_W)
        w_hi = at("w_hi", [P, WSLOT, 1024], O_W + 12288, F32R)
        w_lo = at("w_lo", [P, WSLOT, 1024], O_W + 24576, F32R)
        O_X = O_W + 36864
        x_hi = at("x_hi", [P, KT, T], O_X, F32R)
        x_lo = at("x_lo", [P, KT, T], O_X + KT * ROW, F32R)
        O_H = O_X + 2 * KT * ROW
        h = at("h", [P, KT, T], O_H)
        O_C = O_H + KT * ROW
        cst = at("cst", [P, NCST], O_C)
        ident, ones, head_ones = cst[:, 0:128], cst[:, 128:256], cst[:, 256:384]
        swap = cst[:, 384:512]
        smp_col = cst[0:32, 512:520]
        smp_head = cst[0:32, 520:776].rearrange("p (t m) -> p t m", t=2)
        gain = at("gain", [P, NG], O_C + 4128)
        mk_t = at("mk_t", [P, 2, 2, MEM], O_C + 4416)
        mv_t = at("mv_t", [P, 2, 2, MEM], O_C + 8512)
        hsq = at("hsq", [P, 2, CH], O_C + 12608)
        rstd = at("rstd", [P, 2, CH], O_C + 15360)
        zero = at("zero", [P, 1], O_C + 18112)
        O_L = O_C + 18144
        sq = at("sq", [P, KT, CH], O_L)
        xt = at("xt", [P, KT, CH], O_L + 11008)
        mt = at("mt", [P, KT, MEM], O_L + 22016)
        mk_raw = at("mk_raw", [P, 2, 2, MEM], O_L + 30208)
        mv_raw = at("mv_raw", [P, 2, 2, MEM], O_L + 34304)
        mem_xt = at("mem_xt", [P, 2, KT, MEM], O_L + 38400)
        q_a = at("q_a", [P, H, T], O_L)
        k_a = at("k_a", [P, H, T], O_L + 4 * ROW)
        v_tok = at("v_tok", [P, NBLK, H * DV], O_L + 8 * ROW)
        tok_a = at("tok_a", [P, 6, T], O_L)
        g_a = at("g_a", [P, 6, T], O_L + 8 * ROW)
        mq_a = at("mq_a", [P, 2, T], O_H)
        glr = at("glr", [16, T], O_H + 2 * ROW)
        ring = at("ring", [P, 2, T], O_H + 3 * ROW)
        vs_a = at("vs_a", [NB, H * DV], O_H + 5 * ROW)
        gate2 = at("gate2", [16, 512], O_H + 5 * ROW + 3072)
        lvl = at("lvl", [P, 8, P], O_H + 5 * ROW + 9376, U8)
        lvl_raw = at("lvl_raw", [P, 8, P], O_X + 34816)
        q_b = at("q_b", [P, 6, T], O_L)
        mq_b = at("mq_b", [P, 2, T], O_L + 6 * ROW)
        tok_b = at("tok_b", [P, 2, T], O_L + 8 * ROW)
        k_b = at("k_b", [P, 2, T], O_L + 10 * ROW)
        v_b = at("v_b", [P, 2, T], O_L + 12 * ROW)
        v3 = at("v3", [P, 3, NBLK, 6 * HD], O_X)
        pw = at("pw", [P, 2, 4, P], O_C + 4416)
        m_col = at("m_col", [P, 3, H, NBLK], O_L + 14 * ROW + 64)
        m_row = at("m_row", [H, SEQ], O_C + 8512)
        nm_row = at("nm_row", [H, SEQ], O_X + 39296, F32R)
        sel_raw = at("sel_raw", [H, H, P], O_X + 43392)
        sel = at("sel", [H, H, P], O_X + 45440, F32R)
        o_sb = at("o_sb", [P, SEQ], O_X + 47488)
        o_rl = at("o_rl", [P, SEQ], O_X + 51584)
        tri_raw = at("tri_raw", [P, 5, P], O_C + 12608)
        tri = at("tri", [P, 5, P], O_C + 15168, BF16)
        rope = at("rope", [P, 2, T], O_L + 8 * ROW)
        rstd_b = at("rstd_b", [P, 2, CH], O_L + 22016)
        mem_pr = [at("pr_a", [P, H, MEM], O_H + 5 * ROW + 5120), at("pr_b", [P, H, MEM], O_L + 12 * ROW)]
        mem_pt = [at("pt_a", [P, 2 * H, P], O_C + 12608), at("pt_b", [P, 2 * H, P], O_L + 13 * ROW)]
        mem_st = at("mem_st", [P, 4, H], O_L + 14 * ROW)
        nmax, nbias, psums, rsums = (mem_st[:, i] for i in range(4))
        wk = at("wk", [P, 2, 3, NB, 130], O_X)
        wv = at("wv", [P, 3, NB, 256], O_X + 24960)
        qw_blk = at("qw_blk", [P, 3, 2, NB, 32], O_X + 49536)
        pd = at("pd", [32, 3, NWIN], O_X + 55680)
        pw_blk = at("pw_blk", [P, 3, NB, 32], O_X + 57248)
        wst = at("wst", [32, 16], O_X + 60320)
        v_new = at("v_new", [P, 2, NB], O_X + 60384)
        w_own = at("w_own", [32, 256], O_X + 60448)
        hid_hi = at("hid_hi", [P, 2, T], O_L + 22016, F32R)
        hid_lo = at("hid_lo", [P, 2, T], O_L + 22016 + 2 * ROW, F32R)
        sil = at("sil", [P, NCH, CH], O_L + 22016 + 4 * ROW)
        hid = at("hid", [P, NCH, CH], O_L + 22016 + 5 * ROW)

        k_smp = at("k_smp", [NB, H, P], O_H + 5 * ROW + 5120)
        a_smp = at("a_smp", [P, H, NB], O_H + 5 * ROW + 9216)
        b_end = at("b_end", [P, NBLK], O_H + 5 * ROW + 9344)
        o_a = at("o_a", [P, 6, T], O_X)
        O_G = O_X + 6 * ROW
        dec = at("dec", [P, 2, SEQ], O_G)
        dqk = at("dqk", [P, 2, SEQ], O_G + 8192)
        s_accs = [at("s_acc0", [P, NBLK, P], O_G + 16384), at("s_acc1", [P, NBLK, P], O_H + 5 * ROW + 5120)]
        q_dec = at("q_dec", [P, SEQ], O_G + 20480)
        k_tok = at("k_tok", [P, NBLK, P], O_G + 24576)
        st = at("st", [P, NBLK, DV], O_G + 28672)
        b_cums = [at("b_cum0", [P, SEQ], O_C + 12608), at("b_cum1", [P, SEQ], O_G + 34816)]
        gate_bufs = [(at("z_0", [P, T], O_H + 5 * ROW + 5120)[:], at("zt_0", [P, T], O_C + 12608)[:])] + [(ring[:, 0], ring[:, 1])] * 3
        st_smp = at("st_smp", [P, H, NB, DV], O_G)
        k_one = at("k_one", [NB, H, NB, P], O_G + 24576)
        o_sq = at("o_sq", [P, 6, CH], O_L + 6 * ROW)
        o_rs = at("o_rs", [P, H, CH], O_H + 3 * ROW)
        ck = at("ck", [P, 2, NB, MEM], O_X)
        cv = [at("cv0", [P, NB, MEM], O_X + 16384), at("cv1", [P, NB, MEM], O_G + 20480)]
        q_blk = at("q_blk", [P, 2, NB, 32], O_G + 28672)
        dp = at("dp", [32, MEM], O_G + 30720)
        p_blk = at("p_blk", [P, 2, NB, 32], O_G + 31744)
        dst4 = at("dst4", [32, 4], O_G + 33792)

        banks = [bank(i) for i in range(8)]
        g_spill = nc.dram_tensor("g_spill", [P, 6, T], F32, kind="Internal").ap()

        s_wg = sem("w_scaled")
        s_w = [sem(f"w_landed{i}") for i in range(WSLOT)]
        s_whi, s_wlo, s_wused = sem("w_hi_made"), sem("w_split"), sem("w_used")
        s_cst, s_gain, s_lvl_in, s_lvl, s_mem = sem("constants_landed"), sem("gains_landed"), sem("level_masks_landed"), sem("level_masks_cast"), sem("mem_landed")
        s_x = [sem(f"x_landed{c}") for c in range(NCH)]
        s_zero = sem("zero_set")
        s_sq, s_f1, s_fold, s_sum, s_ln, s_rs = sem("squares"), sem("squares_halved"), sem("squares_folded"), sem("square_sums"), sem("logs"), sem("rstds")
        s_xt, s_hi, s_lo = sem("normed"), sem("hi_made"), sem("split")
        s_mm = sem("products")
        s_ev = sem("evacuated")
        s_hsq, s_hsum, s_hln, s_hrs, s_hn = (sem("head_" + n) for n in ("squares", "sums", "logs", "rstds", "normed"))
        s_mx0, s_mh0, s_ml0 = (sem("mem0_" + n) for n in ("normed", "hi_made", "split"))
        s_mvT, s_mvt = sem("mem_v_turned"), sem("mem_v_kept")
        s_vT, s_vt = sem("v_turned"), sem("v_kept")
        s_out = sem("outputs_written")
        s_spill = [sem("gate_spilled0"), sem("gate_spilled1")]
        s_res = sem("residual_added")
        s_tsq, s_tacc = sem("tile_squares"), sem("tile_squares_added")
        s_sil, s_hid, s_hhi, s_hlo, s_down = (sem(n) for n in ("silu", "hidden", "hidden_hi", "hidden_split", "down_added"))
        s_gate2 = sem("gate2_landed")

        s_z, s_zb, s_zt, s_la, s_bc, s_as, s_be = (sem("gla_" + n) for n in (
            "gates", "gates_kept", "gate_terms", "log_decays", "cumulated", "sample_decays", "block_decays"))
        s_df, s_ex, s_mu, s_ss, s_cp, s_sz, s_kt, s_kv, s_st, s_go, s_oe = (sem("gla_" + n) for n in (
            "exponents", "decays", "decayed", "level_scores", "scores_kept", "scores_cleared", "keys_kept", "updates", "states", "outs", "outs_kept"))
        s_gst, s_sin, s_sout = sem("gla_state_written"), sem("sample_states_landed"), sem("sample_states_written")
        s_skt, s_skk, s_sk1, s_su, s_sn, s_so, s_soe = (sem("sample_" + n) for n in (
            "keys_turned", "keys_kept", "keys_apart", "updates", "states", "outs", "outs_kept"))
        s_gland, s_gsil, s_osq, s_osum, s_oln, s_ors, s_onm, s_tok, s_chi, s_clo = (sem(n) for n in (
            "gate_landed", "gate_silu", "out_squares", "out_sums", "out_logs", "out_rstds", "out_normed", "tokens_mixed", "mix_hi", "mix_split"))
        s_rope, s_rsw, s_rc, s_rs_, s_rok = (sem("rope_" + n) for n in ("landed", "swapped", "cos", "sin", "done"))
        s_tri_in, s_sel_in, s_tri, s_sel, s_ones3 = (sem(n) for n in (
            "masks_landed", "head_rows_landed", "masks_cast", "head_rows_cast", "ones_set"))
        s_v3t, s_v3 = sem("window_values_turned"), sem("window_values_kept")
        s_w1, s_m1, s_mt, s_mr, s_nm = (sem("window_" + n) for n in ("scores", "max", "max_turned", "max_rows", "max_negated"))
        s_w2, s_we, s_wo, s_woc, s_wok, s_wor, s_wod = (sem("window_" + n) for n in (
            "key_scores", "exps", "outs", "outs_copied", "outs_joined", "sums_inverted", "outs_scaled"))
        s_wc, s_wqz, s_wqb, s_wkn, s_d1, s_dm, s_db, s_de, s_dr, s_dp, s_dpn_, s_dpt_, s_dptk_, s_dn, s_dnb_, s_dvn, s_do, s_dok = (
            sem("step_window_" + n) for n in ("cache_landed", "cleared", "queries", "new_keys", "scores", "max", "bias", "exps", "sums_inverted",
                                              "probs", "new_probs", "probs_turned", "probs_kept", "new_apart", "new_spread", "new_values", "outs", "outs_kept"))
        s_h = sem("residual_landed")
        s_cache = sem("cache_landed")
        s_sc, s_mx, s_nb, s_pe, s_ra, s_pn, s_pt, s_ptk, s_po, s_pok = (sem("mem_" + n) for n in (
            "scores", "max", "bias", "exps", "sums_inverted", "probs", "probs_turned", "probs_kept", "outs", "outs_kept"))
        s_qz, s_qb, s_dsc, s_dmx, s_dnb, s_dpe, s_dra, s_dpn, s_dpt, s_dptk, s_dpo, s_dpok = (sem("step_mem_" + n) for n in (
            "cleared", "queries", "scores", "max", "bias", "exps", "sums_inverted", "probs", "probs_turned", "probs_kept", "outs", "outs_kept"))

        NORM_A1, NORM_A2, NORM_KV, NORM_B2 = (1 + 3 * i for i in range(4))
        SQ_A1, SQ_KV = 1, 4
        HN_MK, HN_MQA = 0, 4
        HEAD_A = ([(mk_raw[:, i // 2, i % 2], G_MK + i // 2, mk_t[:, i // 2, i % 2]) for i in range(4)]
                  + [(mq_a[:, i % 2, chunk(i // 2)], G_MQ, mq_a[:, i % 2, chunk(i // 2)]) for i in range(2 * NCH)])
        STEPS_A, STEPS_B, STEPS_AO = steps_of(NA_IN), steps_of(NB_IN), steps_of(KT)
        MEM_TURN = range(6, 10)
        STEPS_BO = [(t, c) for t in range(KT) for c in range(NCH)]

        def dest_b(t):
            if t in B_M:
                return mq_b[:, t - B_M[0]], G_MQ + 1
            if t in B_K:
                return k_b[:, t - B_K[0]], G_K
            if t in B_Q:
                return q_b[:, t - B_Q[0]], G_Q
            return v_b[:, t - B_V[0]], None
        HEAD_B = [(dest_b(t)[0][:, chunk(c)], dest_b(t)[1], c) for t, c in STEPS_B[:NB_NORM]]
        ROPE_B = [i for i, (t, c) in enumerate(STEPS_B[:NB_NORM]) if t not in B_M]
        HN_B = 10
        MEM_AT = ([12 + 3 * i for i in range(NBLK)], [6 + 3 * i for i in range(NBLK)])
        GATE_STEP = MEM_AT[0][-1] + 7

        MM_AIN = 0
        MM_AOUT = MM_AIN + 2 * NA_IN
        MM_FFA = MM_AOUT + 2 * KT
        MM_FF = 4 * 2 + 23
        MM_KV = MM_FFA + MM_FF * JFF
        MM_BOUT = MM_KV + 2 * NB_IN
        MM_FFB = MM_BOUT + 20
        EV_KV = 8 + 3 * NA_IN
        EV_END = EV_KV + 3 * NB_IN
        NLEV = 7
        MEM_SAMPLES_AT = [(0, 1), (0, 2), (1, 0), (1, 1)]

        def diagonal(blk, src_shape):
            n = src_shape[1]
            return bass.AP(blk[:].tensor, blk[:].offset, [[n * NB * 32, P], [NB * 32, n], [36, NB], [1, 4]])
        NSTEP = NLEV + 2
        TAU = 16.0

        def halves(t2d, s):
            v = t2d.rearrange("p (n h s) -> p n h s", h=2, s=s)
            return v[:, :, 0], v[:, :, 1]

        HK = KT // 2

        def norm_half(n, half):
            return 2 * n + half

        def tile_ready(eng, mm0, u0, t, c):
            if c < NCH - 1:
                eng.wait_ge(s_mm, mm0 + (3 * c + t if t < 3 else 2 * t + c) + 1)
            else:
                eng.wait_ge(s_wused, u0 + t + 1)

        block = ctx.enter_context(nc.Block())

        @block.sync
        def _(sp):
            for s in range(WSLOT):
                sp.dma_start(w_raw[:, s], w_d[s]).then_inc(s_w[s], 16)
            with sp.Fori(1, NUNIT // WSLOT) as g:
                for s in range(WSLOT):
                    sp.wait_ge(s_wlo, WSLOT * g + (s + 1 - WSLOT))
                    sp.dma_start(w_raw[:, s], w_d[bass.ds(WSLOT * g + s, 1)].rearrange("a p n -> p (a n)")).then_inc(s_w[s], 16)
            for u in range(NUNIT // WSLOT * WSLOT, NUNIT):
                sp.wait_ge(s_wlo, u + 1 - WSLOT)
                sp.dma_start(w_raw[:, u % WSLOT], w_d[u]).then_inc(s_w[u % WSLOT], 16)

        @block.gpsimd
        def _(pool):
            def split(s, landed, made, used):
                pool.wait_ge(s_w[s], landed)
                if used is not None:
                    pool.wait_ge(s_wused, used)
                nc.gpsimd.tensor_tensor(w_hi[:, s], w_raw[:, s], zero[:].broadcast_to([P, 1024]), ALU.add).then_inc(s_whi, 1)
                pool.wait_ge(s_whi, made)
                nc.gpsimd.tensor_tensor(w_lo[:, s], w_raw[:, s], w_hi[:, s].bitcast(F32), ALU.subtract).then_inc(s_wlo, 1)

            pool.wait_ge(s_gain, 16)
            nc.gpsimd.memset(zero[:], 0.0).then_inc(s_zero, 1)
            pool.wait_ge(s_zero, 1)
            for s in range(WSLOT):
                split(s, 16, s + 1, None)
            G_GLA = (U_AOUT + 2) // WSLOT
            with pool.Fori(1, G_GLA) as g:
                for s in range(WSLOT):
                    split(s, 16 * g + 16, WSLOT * g + (s + 1), WSLOT * g + (s + 1 - WSLOT))
            for hh in range(H):
                b_cum = b_cums[hh % 2]
                for l in range(NSTEP):
                    n = NSTEP * hh + l
                    if l == NLEV:
                        continue
                    if l == 0:
                        pool.wait_ge(s_bc, NBLK * (hh + 1))
                        if hh == 0:
                            pool.wait_ge(s_wused, U_AIN + NA_IN)
                    if n >= 2:
                        pool.wait_ge(s_mu, n - 1)
                    if l < NLEV:
                        s = 2 ** l
                        lo_, hi_ = halves(b_cum[:], s)
                        dlo, dhi = halves(dec[:, n % 2], s)
                        ref = lo_[:, :, s - 1:s].broadcast_to(list(lo_.shape))
                        nc.gpsimd.tensor_tensor(dlo, ref, lo_, ALU.subtract)
                        nc.gpsimd.tensor_tensor(dhi, hi_, ref, ALU.subtract).then_inc(s_df, 1)
                    else:
                        v = b_cum[:].rearrange("p (n s) -> p n s", s=P)
                        nc.gpsimd.tensor_tensor(dec[:, n % 2].rearrange("p (n s) -> p n s", s=P), v[:, :, P - 1:P].broadcast_to([P, NBLK, P]), v,
                                                ALU.subtract).then_inc(s_df, 1)
            with pool.Fori(G_GLA, U_KV // WSLOT) as g:
                for s in range(WSLOT):
                    split(s, 16 * g + 16, WSLOT * g + (s + 1), WSLOT * g + (s + 1 - WSLOT))
            for t in range(NB_IN):
                u = U_KV + t
                g0 = G_KV if t in B_K or t in B_V else G_N1 + KT
                pool.wait_ge(s_w[u % WSLOT], 16 * (u // WSLOT + 1))
                rows = w_raw[:, u % WSLOT].rearrange("p (k m) -> p k m", k=KT)
                nc.gpsimd.tensor_tensor(rows, rows, gain[:, g0:g0 + KT].unsqueeze(2).broadcast_to([P, KT, P]), ALU.mult).then_inc(s_wg, 1)
                pool.wait_ge(s_wg, t + 1)
                split(u % WSLOT, 16 * (u // WSLOT + 1), u + 1, u + 1 - WSLOT)
            with pool.Fori((U_KV + NB_IN) // WSLOT, NUNIT // WSLOT) as g:
                for s in range(WSLOT):
                    split(s, 16 * g + 16, WSLOT * g + (s + 1), WSLOT * g + (s + 1 - WSLOT))
            for u in range(NUNIT // WSLOT * WSLOT, NUNIT):
                split(u % WSLOT, 16 * (u // WSLOT + 1), u + 1, u + 1 - WSLOT)

        @block.tensor
        def _(pe):
            def product(out, parts, middle=None):
                n = len(parts)
                for i, (wh, wl, xh, xl) in enumerate(parts):
                    if middle and i == n // 2:
                        pe.wait_ge(*middle)
                    pe.matmul(out, wh, xh, start=(i == 0), stop=False)
                    pe.matmul(out, wh, xl, start=False, stop=False)
                    mm = pe.matmul(out, wl, xh, start=False, stop=(i == n - 1))
                return mm

            def tile_parts(s, cols, nk=KT, base=0, row=0):
                def w(t, k):
                    return t[:, s, base + k * P:base + (k + 1) * P]
                return [(w(w_hi, k), w(w_lo, k), x_hi[:, row + k, cols], x_lo[:, row + k, cols]) for k in range(nk)]

            def norm_sum(n, nk, width):
                pe.wait_ge(s_fold, n + 1)
                if n >= 2:
                    pe.wait_ge(s_ln, n - 1)
                for k in range(nk):
                    src = sq[:, k, 0:width] if nk > 1 else sq[:, (n - 1) % NCH, 0:width]
                    mm = pe.matmul(banks[6 + n % 2][:, 0:width], ones, src, start=(k == 0), stop=(k == nk - 1))
                mm.then_inc(s_sum, 1)

            def head_sum(i, width):
                pe.wait_ge(s_hsq, i + 1)
                if i >= 1:
                    pe.wait_ge(s_hln, i)
                pe.matmul(banks[6][:, 0:width], head_ones, hsq[:, i % 2, 0:width], start=True, stop=True).then_inc(s_hsum, 1)

            def mem_tile(t):
                pe.wait_ge(s_wlo, U_MEM + t + 1)
                if t == 0:
                    pe.wait_ge(s_ml0, 1)
                if t == 4:
                    pe.wait_ge(s_lo, 1)
                if t >= 6:
                    pe.wait_ge(s_ev, t - 5)
                li, c0 = t // 4, T - 2 * MEM
                mm = product(banks[t % 6][:, 0:MEM], tile_parts((U_MEM + t) % WSLOT, slice(c0 + li * MEM, c0 + (li + 1) * MEM)))
                mm.then_inc(s_wused, 1)

            pe.wait_ge(s_cst, 16)
            norm_sum(0, 2, MEM)
            for t in range(8):
                mem_tile(t)
                if t == 2:
                    norm_sum(NORM_A1, 2, CH)
                if t == 5:
                    norm_sum(NORM_A1 + 1, 2, CH)
            halves_of = (slice(0, HD), slice(HD, P))

            def mem_attention(L, mq, n):
                if n in MEM_AT[L]:
                    i = MEM_AT[L].index(n)
                    a = NBLK * L + i
                    pe.wait_ge(s_hn, HN_B if L == 0 else HN_B + 3 * ((P * (i + 1) - 1) // CH) + 2)
                    if a >= 1:
                        pe.wait_ge(s_ptk, 2 * a)
                    if a == 0:
                        pe.wait_ge(s_mvt, 4)
                    for r in range(2):
                        for par in range(2):
                            mm = pe.matmul(banks[3 + par][:, r * MEM:(r + 1) * MEM], mq[halves_of[par], r, i * P:(i + 1) * P],
                                           mk_t[halves_of[par], L, r], start=True, stop=True)
                    mm.then_inc(s_sc, 1)
                if n - 2 in MEM_AT[L]:
                    a = NBLK * L + MEM_AT[L].index(n - 2)
                    pe.wait_ge(s_pn, a + 1)
                    for j in range(H):
                        for kt in range(2):
                            mm = pe.transpose(banks[3 + j // 2][:, (2 * (j % 2) + kt) * P:][:, 0:P], mem_pr[L][:, j, kt * P:(kt + 1) * P], ident)
                    mm.then_inc(s_pt, 1)
                if n - 4 in MEM_AT[L]:
                    i = MEM_AT[L].index(n - 4)
                    a = NBLK * L + i
                    pe.wait_ge(s_ptk, 2 * a + 2)
                    if a >= 1:
                        pe.wait_ge(s_pok, a)
                    for r in range(2):
                        for kt in range(2):
                            for par in range(2):
                                j, head = 2 * par + r, 2 * r + par
                                mm = pe.matmul(banks[5][halves_of[par], r * P:(r + 1) * P], mv_t[:, L, kt, head * HD:(head + 1) * HD],
                                               mem_pt[L][:, 2 * j + kt], start=(kt == 0), stop=(kt == 1))
                    mm.then_inc(s_po, 1)

            def step_product(u0, ev0, norm, n, t, c):
                if c == 0 or t < 3:
                    pe.wait_ge(s_wlo, u0 + t + 1)
                middle = None
                if n < 9:
                    pe.wait_ge(s_lo, norm_half(norm + c, 0))
                    middle = s_lo, norm_half(norm + c, 1)
                pe.wait_ge(s_ev, ev0 + max(n - 2, 0))
                mm = product(banks[n % 3][:, 0:CH], tile_parts((u0 + t) % WSLOT, chunk(c)), middle)
                mm.then_inc(s_mm if c < NCH - 1 else s_wused, 1)

            def gate_products(hh):
                if hh == 0:
                    pe.wait_ge(s_gate2, 16)
                    pe.wait_ge(s_pok, NBLK)
                    pe.wait_ge(s_ptk, 2 * NBLK)
                elif hh == 1:
                    pe.wait_ge(s_zb, 3)
                else:
                    pe.wait_ge(s_oe, 4 * (hh - 1))
                for c in range(NCH):
                    pe.matmul(banks[(3 if hh == 0 else 4) + c][:, 0:CH], gate2[:, hh * P:(hh + 1) * P], glr[:, chunk(c)],
                              start=True, stop=True).then_inc(s_z, 1)

            for n, (t, c) in enumerate(STEPS_A):
                step_product(U_AIN, 8, NORM_A1, n, t, c)
                if n == 0:
                    norm_sum(NORM_A1 + 2, 2, CH)
                if 1 <= n <= len(HEAD_A):
                    if n == 1:
                        pe.wait_ge(s_ln, NORM_A1 + 2)
                    head_sum(HN_MK + n - 1, HEAD_A[n - 1][0].shape[1])
                if n in MEM_TURN:
                    i = MEM_TURN.index(n)
                    if i >= 2:
                        pe.wait_ge(s_mvt, i - 1)
                    for t2 in range(2):
                        mm = pe.transpose(banks[3 + i % 2][:, t2 * P:(t2 + 1) * P], mv_raw[:, i // 2, t2, (i % 2) * P:(i % 2 + 1) * P], ident)
                    mm.then_inc(s_mvT, 1)
                i, b = divmod(n - 3 * (A_V[0] + 1), 3)
                if 0 <= i < 6:
                    pe.wait_ge(s_ev, 8 + 3 * (A_V[i] + 1))
                    m = 3 * i + b
                    pe.wait_ge(*((s_vt, m) if m else (s_ln, NORM_A1 + NCH)))
                    if b < 2:
                        for j in range(4):
                            blk = 4 * b + j
                            mm = pe.transpose(banks[7][:, j * P:(j + 1) * P], ring[:, i % 2, blk * P:(blk + 1) * P], ident)
                    else:
                        mm = pe.transpose(banks[7][0:NB, 0:P], ring[:, i % 2, SEQ:T], ident)
                    mm.then_inc(s_vT, 1)
                mem_attention(0, mq_a, n)
                if n == GATE_STEP:
                    gate_products(0)

            def mem_samples(L, part):
                bk = banks[7]
                if part == 0:
                    pe.wait_ge(s_qb, 4 * L + 4)
                    pe.wait_ge(s_cache, 48 * (L + 1))
                    pe.wait_ge(s_vt, 18)
                    for t in range(2):
                        for b in range(NB):
                            mm = pe.matmul(bk[0:32, 0:MEM], q_blk[:, t, b], ck[:, t, b], start=(t + b == 0), stop=(t == 1 and b == NB - 1))
                    mm.then_inc(s_dsc, 1)
                if part == 1:
                    pe.wait_ge(s_dpn, 2 * L + 1)
                    for kt in range(2):
                        mm = pe.transpose(bk[:, MEM + kt * 32:MEM + (kt + 1) * 32], dp[:, kt * P:(kt + 1) * P], ident[0:32, 0:32])
                    mm.then_inc(s_dpt, 1)
                if part == 2:
                    pe.wait_ge(s_dptk, L + 1)
                    for b in range(NB):
                        for kt in range(2):
                            mm = pe.matmul(bk[0:32, 0:MEM], p_blk[:, kt, b], cv[kt][:, b], start=(b + kt == 0), stop=(b == NB - 1 and kt == 1))
                    mm.then_inc(s_dpo, 1)
                if part == 3:
                    pe.wait_ge(s_dpn, 2 * L + 2)
                    for t in range(2):
                        mm = pe.matmul(bk[:, MEM + 64 + t * NB:MEM + 64 + (t + 1) * NB], dp[:, t * P:(t + 1) * P], smp_col, start=True, stop=True)
                    mm.then_inc(s_dpo, 1)

            def level_scores(hh, l):
                n = NSTEP * hh + l
                pair = banks[2 * (n % 2)], banks[2 * (n % 2) + 1]
                if n >= 2:
                    h0, l0 = divmod(n - 2, NSTEP)
                    pe.wait_ge(*((s_cp, NBLK * h0 + l0 + 1) if l0 <= NLEV else (s_kt, 2 * (h0 + 1))))
                if l != NLEV:
                    pe.wait_ge(s_mu, n + 1)
                for b in range(NBLK):
                    cols = slice(b * P, (b + 1) * P)
                    out = pair[b // 4][:, (b % 4) * P:(b % 4 + 1) * P]
                    if l < NLEV:
                        mm = pe.matmul(out, dqk[:, n % 2, cols], dqk[:, n % 2, cols], start=True, stop=True)
                    elif l == NLEV:
                        mm = pe.matmul(out, k_a[:, hh, cols], q_a[:, hh, cols], start=True, stop=True)
                    else:
                        mm = pe.transpose(out, dqk[:, n % 2, cols], ident)
                mm.then_inc(s_ss, 1)

            def state_updates(hh):
                pe.wait_ge(s_kt, 2 * hh + 2)
                pe.wait_ge(s_zb, 3 * min(hh + 2, H))
                pe.wait_ge(s_dpok, 1)
                if hh >= 1:
                    pe.wait_ge(s_oe, 4 * hh)
                for b in range(NBLK):
                    pe.matmul(banks[4 + b // 2][:, (b % 2) * DV:(b % 2 + 1) * DV], k_tok[:, b], v_tok[:, b, hh * DV:(hh + 1) * DV],
                              start=True, stop=True).then_inc(s_kv, 1)

            def outs(hh):
                half = slice(HD * (hh % 2), HD * (hh % 2) + HD)
                pe.wait_ge(s_cp, NBLK * (hh + 1))
                pe.wait_ge(s_st, NBLK * (hh + 1))
                for b in range(NBLK):
                    cols = slice((b % 4) * P, (b % 4 + 1) * P)
                    for e0, e1, out in ((0, P, banks[4 + b // 4][:, cols]), (P, DV, banks[6 + b // 4][half, cols])):
                        mm = pe.matmul(out, v_tok[:, b, hh * DV + e0:hh * DV + e1], s_accs[hh % 2][:, b], start=True, stop=(b == 0))
                        if b >= 1:
                            mm = pe.matmul(out, st[:, b - 1, e0:e1], q_dec[:, b * P:(b + 1) * P], start=False, stop=True)
                mm.then_inc(s_go, 1)

            pe.wait_ge(s_ev, 8 + 3 * NA_IN)
            pe.wait_ge(s_zb, 3)
            for hh in range(H):
                for l in range(NSTEP):
                    level_scores(hh, l)
                    if l == 0 and hh >= 1:
                        state_updates(hh - 1)
                    if l == 1 and hh >= 1:
                        outs(hh - 1)
                    if hh == 0 and l in (2, 4, 6, 7):
                        mem_samples(0, (l - 1) // 2 if l < 7 else 3)
                    if l == 2 and hh + 1 < H:
                        gate_products(hh + 1)
            state_updates(H - 1)
            outs(H - 1)

            pe.wait_ge(s_oe, 4 * H)
            for hh in range(H):
                mm = pe.transpose(banks[4][0:NB, hh * P:(hh + 1) * P], k_a[:, hh, SEQ:T], ident)
            mm.then_inc(s_skt, 1)

            def out_sums(c):
                pe.wait_ge(s_osq, c + 1)
                if c == 1:
                    pe.wait_ge(s_soe, 2 * (H - 1))
                if c == 2:
                    pe.wait_ge(s_soe, 2 * H)
                if c >= 1:
                    pe.wait_ge(s_oln, H * c)
                for r in range(H):
                    half = slice(HD * (r % 2), HD * (r % 2) + HD)
                    bk = banks[r + 4 * (c // 2)]
                    pe.matmul(bk[:, 0:CH], ones, o_sq[:, r], start=True, stop=False)
                    pe.matmul(bk[:, 0:CH], ones[half], o_sq[half, 4 + r // 2], start=False, stop=True).then_inc(s_osum, 1)

            out_sums(0)

            def sample_updates(hh):
                pe.wait_ge(s_sk1, hh + 1)
                if hh == 0:
                    pe.wait_ge(s_oln, H)
                if hh == 1:
                    pe.wait_ge(s_skk, 1)
                if hh >= 2:
                    pe.wait_ge(s_soe, 2 * (hh - 1))
                for b in range(NB):
                    mm = pe.matmul(banks[4 * (hh % 2) + b // 2][:, (b % 2) * DV:(b % 2 + 1) * DV], k_one[:, hh, b],
                                   vs_a[:, hh * DV:(hh + 1) * DV], start=True, stop=True)
                mm.then_inc(s_su, 1)

            def sample_outs(hh):
                half = slice(HD * (hh % 2), HD * (hh % 2) + HD)
                pe.wait_ge(s_sn, 8 * (hh + 1))
                for b in range(NB):
                    pe.matmul(banks[4 * (hh % 2)][:, b:b + 1], st_smp[:, hh, b, 0:P], q_a[:, hh, SEQ + b:SEQ + b + 1], start=True, stop=True)
                    mm = pe.matmul(banks[4 * (hh % 2) + 1][half, b:b + 1], st_smp[:, hh, b, P:DV], q_a[:, hh, SEQ + b:SEQ + b + 1],
                                   start=True, stop=True)
                mm.then_inc(s_so, 1)

            for hh in range(H + 1):
                if hh < H:
                    sample_updates(hh)
                if hh == H:
                    out_sums(1)
                if hh >= 1:
                    sample_outs(hh - 1)

            def tiles_product(order, u0, ready, free_sem, free0, nk=KT, per_unit=1, between=None):
                for n, (t, c) in enumerate(order):
                    u = u0 + t // per_unit
                    pe.wait_ge(s_wlo, u + 1)
                    if t == 0:
                        ready(c)
                    if n >= 6:
                        pe.wait_ge(free_sem, free0 + n - 5)
                    mm = product(banks[n % 6][:, 0:CH], tile_parts(u % WSLOT, chunk(c), nk, (t % per_unit) * nk * P))
                    last = c == NCH - 1 and t % per_unit == per_unit - 1
                    mm.then_inc(s_wused if last else s_mm, 1)
                    if between:
                        between(n)

            def after_outs(c):
                pe.wait_ge(s_clo, 2 * (c + 1))
                pe.wait_ge(s_oln, 2 * H)

            def between_outs(n):
                if n == 0:
                    out_sums(2)
                if n == 3:
                    pe.wait_ge(s_oln, H * NCH)
            tiles_product(STEPS_AO, U_AOUT, after_outs, s_res, 0, between=between_outs)

            def swiglu(L, norm, u0, ev0, next_norm):
                for c in range(NCH):
                    norm_sum(norm + c, 1, CH)
                pe.wait_ge(*ev0)

                def step(j, first=False, last=False):
                    order = [(q, c) for q in range(4) for c in range(NCH)]
                    if first:
                        order = [(q, c) for c in range(NCH) for q in range(2)] + order[6:]
                    for q, c in order:
                        s = (u0 + q) % WSLOT
                        if c == 0 or first:
                            pe.wait_ge(s_wlo, u0 + q + 1 if first else 6 * j + (u0 + q + 1))
                        middle = None
                        if first and q < 2:
                            pe.wait_ge(s_lo, norm_half(norm + c, 0))
                            middle = s_lo, norm_half(norm + c, 1)
                        if q >= 2:
                            sem_, at_ = ((s_sil, s_hid)[q % 2], 6 * JFF * L + c + 1)
                            pe.wait_ge(sem_, at_ if first else 6 * j + at_)
                        elif not first:
                            pe.wait_ge(s_down, 24 * j + (24 * JFF * L - 6 + 3 * q + c + 1))
                        mm = product(banks[3 * (q % 2) + c][:, 0:CH], tile_parts(s, chunk(c)), middle)
                        mm.then_inc(s_mm if c < NCH - 1 else s_wused, 1)
                    sd = [(u0 + 4) % WSLOT, (u0 + 5) % WSLOT]
                    pe.wait_ge(s_wlo, u0 + 6 if first else 6 * j + (u0 + 6))
                    for c in range(NCH):
                        at_ = 6 * JFF * L + 3 + c + 1
                        pe.wait_ge(s_hlo, at_ if first else 6 * j + at_)
                        for m in range(KT):
                            n = KT * c + m
                            if n < 6:
                                sem_, at_ = (s_sil if n < 3 else s_hid, 6 * JFF * L + 3 + n % 3 + 1)
                                pe.wait_ge(sem_, at_ if first else 6 * j + at_)
                            else:
                                at_ = 24 * JFF * L + n - 5
                                pe.wait_ge(s_down, at_ if first else 24 * j + at_)
                            cols = slice(m * P, (m + 1) * P)
                            mm = product(banks[n % 6][:, 0:CH], [(w_hi[:, sd[f], cols], w_lo[:, sd[f], cols], hid_hi[:, f, chunk(c)],
                                                                  hid_lo[:, f, chunk(c)]) for f in range(2)])
                            if n < 23:
                                mm.then_inc(s_mm, 1)
                            else:
                                mm.then_inc(s_wused, 2)
                        if last and next_norm and c >= 1:
                            norm_sum(next_norm + c - 1, 2, CH)

                step(0, first=True)
                with pe.Fori(1, JFF - 1) as j:
                    step(j)
                step(JFF - 1, last=True)

            swiglu(0, NORM_A2, U_FFA, (s_res, 24), NORM_KV)

            pe.wait_ge(s_down, 24 * JFF)
            for n, (t, c) in enumerate(STEPS_B):
                step_product(U_KV, EV_KV, NORM_KV, n, t, c)
                if n == 0:
                    norm_sum(NORM_KV + 2, 2, CH)
                if 1 <= n <= NB_NORM:
                    if n == 1:
                        pe.wait_ge(s_ln, NORM_KV + 2)
                    head_sum(HN_B + n - 1, CH)
                if n - 2 in ROPE_B:
                    i = ROPE_B.index(n - 2)
                    pe.wait_ge(s_hn, HN_B + n - 1)
                    pe.wait_ge(*((s_rok, i) if i else (s_ln, NORM_KV + NCH)))
                    pe.matmul(banks[7][:, 0:CH], swap, HEAD_B[n - 2][0], start=True, stop=True).then_inc(s_rsw, 1)
                mem_attention(1, mq_b, n)
            pe.wait_ge(s_ev, EV_END)
            pe.wait_ge(s_tri, 1)
            pe.wait_ge(s_rok, len(ROPE_B))
            pe.wait_ge(s_ptk, 4 * NBLK)

            def maxima_scores(pair):
                i = 20 * pair
                for g in range(3):
                    per = 4 if g == 2 else 2
                    for b in range(NBLK // per):
                        if g == 2:
                            masks = [(0, tri[:, 4:5].broadcast_to([P, 4, P]))]
                            pairs = [(4 * b + m, 4 * b + m) for m in range(4)]
                        else:
                            pairs, masks = [], []
                            for m, blk in enumerate(range(2 * b, 2 * b + 2)):
                                kbs = [kb for kb, _ in key_blocks(g, blk)]
                                pairs += [(blk, kb) for kb in (kbs if len(kbs) == 2 else kbs * 2)]
                                masks.append((2 * m, tri[:, 1:3] if len(kbs) == 2 else tri[:, 2:3].broadcast_to([P, 2, P])))
                        for x in range(2):
                            if i + x >= 4:
                                pe.wait_ge(s_m1, i + x - 3)
                            for m, mask in masks:
                                pe.matmul(banks[(i + x) % 4][:, m * P:m * P + mask.shape[1] * P], tri[:, 0], mask, start=(m == 0), stop=False,
                                          skip_group_check=True)
                        for m, (blk, kb) in enumerate(pairs):
                            for x in range(2):
                                mm = pe.matmul(banks[(i + x) % 4][:, m * P:(m + 1) * P], tokens_of(q_b[halves_of[x], 2 * g + pair], g, blk),
                                               tokens_of(k_b[halves_of[x], pair], g, kb), start=False, stop=(m == 3), skip_group_check=True)
                                if m == 3:
                                    mm.then_inc(s_w1, 1)
                        i += 2
                    if (pair, g) in MEM_SAMPLES_AT:
                        mem_samples(1, MEM_SAMPLES_AT.index((pair, g)))

            maxima_scores(0)
            maxima_scores(1)

            pe.wait_ge(s_wqb, 12)
            pe.wait_ge(s_wkn, 3)
            for g in range(3):
                for t in range(2):
                    for b in range(NB):
                        mm = pe.matmul(banks[4][0:32, g * NWIN:(g + 1) * NWIN], qw_blk[:, g, t, b], wk[:, t, g, b, 0:NWIN],
                                       start=(t + b == 0), stop=(t == 1 and b == NB - 1))
            mm.then_inc(s_d1, 1)
            pe.wait_ge(s_m1, 40)
            for g in range(3):
                for b in range(2):
                    n = 2 * g + b
                    if n >= 4:
                        pe.wait_ge(s_mr, n - 3)
                    for m in range(4):
                        mm = pe.transpose(banks[n % 4][0:H, m * P:(m + 1) * P], m_col[:, g, :, 4 * b + m], ident)
                    mm.then_inc(s_mt, 1)
            pe.wait_ge(s_dp, 1)
            for g in range(3):
                mm = pe.transpose(banks[5][:, g * 32:(g + 1) * 32], pd[:, g, 0:P], ident[0:32, 0:32])
            mm.then_inc(s_dpt_, 1)
            pe.wait_ge(s_dn, 1)
            for t in range(2):
                mm = pe.matmul(banks[6][:, t * NB:(t + 1) * NB], smp_head[:, t], wst[:, 8:16], start=True, stop=True)
            mm.then_inc(s_dnb_, 1)
            pe.wait_ge(s_dptk_, 1)
            for b in range(NB):
                for g in range(3):
                    mm = pe.matmul(banks[7][0:32, 0:256], pw_blk[:, g, b], wv[:, g, b], start=(b + g == 0), stop=(b == NB - 1 and g == 2))
            mm.then_inc(s_do, 1)
            pe.wait_ge(s_dp, 2)
            for t in range(2):
                mm = pe.matmul(banks[7][:, 256 + t * NB:256 + (t + 1) * NB], w_own[:, t * P:(t + 1) * P], smp_col, start=True, stop=True)
            mm.then_inc(s_do, 1)

            pe.wait_ge(s_mr, 6)
            for i in range(12):
                g, b = i // 4, i % 4
                if i >= 4:
                    pe.wait_ge(s_v3, i - 3)
                for m in range(2):
                    for t in range(2):
                        c0 = (2 * m + t) * P
                        mm = pe.transpose(banks[i % 4][:, c0:c0 + P], tokens_of(v_b[:, t], g, 2 * b + m), ident)
                mm.then_inc(s_v3t, 1)
            pe.wait_ge(s_v3, 12)

            pe.wait_ge(s_nm, 1)
            pe.wait_ge(s_sel, 1)

            def key_scores(hh, w):
                i = NW * hh + w
                g, qs, back, before = W_STEPS[w]
                par = slice(HD * (hh % 2), HD * (hh % 2) + HD)
                if i >= 4:
                    pe.wait_ge(s_we, i - 3)
                bk = banks[i % 4]
                n = len(qs)
                mask = tri[:, (2 if before else 1) if g < 2 else 3].unsqueeze(1).broadcast_to([P, n, P])
                pe.matmul(bk[:, 0:n * P], tri[:, 0], mask, start=True, stop=False, skip_group_check=True)
                at_ = tokens_of4(nm_row[:], g, qs[0] // 4)
                if n < 4:
                    at_ = at_[:, 4 - n:4]
                pe.matmul(bk[:, 0:n * P], sel[:, hh], at_, start=False, stop=False, skip_group_check=True)
                for m, blk in enumerate(qs):
                    mm = pe.matmul(bk[:, m * P:(m + 1) * P], tokens_of(k_b[par, hh // 2], g, blk - back),
                                   tokens_of(q_b[par, 2 * g + hh // 2], g, blk), start=False, stop=(m == n - 1), skip_group_check=True)
                mm.then_inc(s_w2, 1)

            def value_products(hh, w):
                i = NW * hh + w
                g, qs, back, before = W_STEPS[w]
                pe.wait_ge(s_we, i + 1)
                if w == 0 and hh >= 1:
                    pe.wait_ge(s_woc, 2 * hh)
                    pe.wait_ge(s_wok, 2 * hh)
                if w == 0 and hh == 0:
                    pe.wait_ge(s_dok, 1)
                for m, blk in enumerate(qs):
                    e0 = 192 * (hh // 2) + HD * (hh % 2)
                    lhs = v3[:, g, blk - back, e0:e0 + P]
                    rhs = pw[:, i % 2, m]
                    bk = banks[(6 if g == 2 else 4) + blk // 4]
                    if g == 1:
                        out = tokens_of(bk[:], 1, blk % 4)
                    else:
                        out = bk[:, (blk % 4) * P:(blk % 4 + 1) * P]
                    mm = pe.matmul(out, lhs, rhs, start=((w in (0, 1, 7, 8)) and m == 0), stop=False, skip_group_check=True)
                mm.then_inc(s_wo, 1)

            for i in range(NW * H + 2):
                if i < NW * H:
                    key_scores(i // NW, i % NW)
                if i >= 2:
                    value_products((i - 2) // NW, (i - 2) % NW)

            def after_mix(c):
                if c == 0:
                    pe.wait_ge(s_wok, 2 * H)
                    pe.wait_ge(s_woc, 2 * H)
                pe.wait_ge(s_clo, 2 * NCH + 2 * (c + 1))
            tiles_product(STEPS_BO, U_BOUT, after_mix, s_res, 24, nk=4, per_unit=2)
            swiglu(1, NORM_B2, U_FFB, (s_res, 48), None)

        @block.scalar
        def _(act):
            act.dma_start(cst[:], cst_d).then_inc(s_cst, 16)
            act.dma_start(mt[:], mem_d).then_inc(s_mem, 16)
            act.dma_start(gain[:], gain_d).then_inc(s_gain, 16)
            for c in range(NCH):
                act.dma_start(h[:, :, chunk(c)], x_d[:, :, chunk(c)]).then_inc(s_x[c], 16)
            nc.scalar.preload_act_table_set("natural_log_exp_and_others")

            def rstd_of(bank_, out, scale, log_sem, exp_sem, n):
                nc.scalar.activation(out, bank_, ACT.Ln, scale=scale, bias=EPS).then_inc(log_sem, 1)
                act.wait_ge(log_sem, n + 1)
                nc.scalar.activation(out, out, ACT.Exp, scale=-0.5).then_inc(exp_sem, 1)

            def square(i, n, src, width):
                if n >= 1:
                    act.wait_ge(s_sum, n)
                nc.scalar.activation(sq[:, :, 0:width], src, ACT.Square).then_inc(s_sq, 1)

            def norm_rstd(n, width, out):
                act.wait_ge(s_sum, n + 1)
                if n >= 1:
                    act.wait_ge(s_xt, max(norm_half(n - 2, 1), 1))
                rstd_of(banks[6 + n % 2][:, 0:width], out[:, n % 2, 0:width], 1.0 / D, s_ln, s_rs, n)

            def norm_hi(n, dst):
                for half in range(2):
                    act.wait_ge(s_xt, norm_half(n, half))
                    k = slice(HK * half, HK * (half + 1))
                    nc.scalar.activation(dst[:, k], xt[:, k], ACT.Copy).then_inc(s_hi, 1)

            def head_square(i, src):
                if i >= 2:
                    act.wait_ge(s_hsum, i - 1)
                nc.scalar.activation(hsq[:, i % 2, 0:src.shape[1]], src, ACT.Square).then_inc(s_hsq, 1)

            def head_rstd(i, width):
                act.wait_ge(s_hsum, i + 1)
                if i >= 2:
                    act.wait_ge(s_hn, i - 1)
                rstd_of(banks[6][:, 0:width], rstd[:, i % 2, 0:width], 1.0 / HD, s_hln, s_hrs, i)

            act.wait_ge(s_mem, 16)
            square(0, 0, mt[:], MEM)
            norm_rstd(0, MEM, rstd)
            act.wait_ge(s_mx0, 1)
            nc.scalar.activation(x_hi[:, :, T - 2 * MEM:T - MEM], mem_xt[:, 0], ACT.Copy).then_inc(s_mh0, 1)
            act.wait_ge(s_xt, 1)
            nc.scalar.activation(x_hi[:, :, T - MEM:T], mem_xt[:, 1], ACT.Copy).then_inc(s_hi, 1)
            act.wait_ge(s_x[0], 16)
            square(SQ_A1, NORM_A1, h[:, :, chunk(0)], CH)
            for t in range(8):
                li, j = t // 4, t % 4
                dst = mk_raw[:, li, j] if j < 2 else mv_raw[:, li, j - 2]
                act.wait_ge(s_wused, U_MEM + t + 1)
                nc.scalar.activation(dst, banks[t % 6][:, 0:MEM], ACT.Copy).then_inc(s_ev, 1)
                if t == 2:
                    norm_rstd(NORM_A1, CH, rstd_b)
                    act.wait_ge(s_x[1], 16)
                    square(SQ_A1 + 1, NORM_A1 + 1, h[:, :, chunk(1)], CH)
                if t == 5:
                    norm_hi(NORM_A1, x_hi[:, :, chunk(0)])
            norm_rstd(NORM_A1 + 1, CH, rstd_b)
            act.wait_ge(s_x[2], 16)
            square(SQ_A1 + 2, NORM_A1 + 2, h[:, :, chunk(2)], CH)
            norm_hi(NORM_A1 + 1, x_hi[:, :, chunk(1)])
            act.wait_ge(s_ev, 8)
            act.dma_start(mv_d, mv_raw[:]).then_inc(s_out, 16)

            def mem_attention(L, n):
                if n in MEM_AT[L]:
                    a = NBLK * L + MEM_AT[L].index(n)
                    act.wait_ge(s_nb, a + 1)
                    if a >= 1:
                        act.wait_ge(s_pt, a)
                    for par in range(2):
                        for r in range(2):
                            j = 2 * par + r
                            op = nc.scalar.activation(mem_pr[L][:, j], banks[3 + par][:, r * MEM:(r + 1) * MEM], ACT.Exp,
                                                      scale=HD ** -0.5, bias=nbias[:, j:j + 1], accum_out=psums[:, j:j + 1])
                    op.then_inc(s_pe, 1)
                if n - 2 in MEM_AT[L]:
                    a = NBLK * L + MEM_AT[L].index(n - 2)
                    act.wait_ge(s_pt, a + 1)
                    if a >= 1:
                        act.wait_ge(s_po, a)
                    for b in range(2):
                        op = nc.scalar.activation(mem_pt[L][:, 4 * b:4 * b + 4], banks[3 + b][:].rearrange("p (j m) -> p j m", j=4), ACT.Copy)
                        op.then_inc(s_ptk, 1)

            def mem_samples(L, part):
                if part == 0:
                    act.wait_ge(s_dnb, L + 1)
                    nc.scalar.activation(dp[:], banks[7][0:32, 0:MEM], ACT.Exp, scale=HD ** -0.5, bias=dst4[:, 1:2],
                                         accum_out=dst4[:, 2:3]).then_inc(s_dpe, 1)
                if part == 1:
                    act.wait_ge(s_dpt, L + 1)
                    nc.scalar.activation(diagonal(p_blk, [P, 2]), banks[7][:, MEM:MEM + 64].rearrange("p (k b m) -> p k b m", k=2, b=NB), ACT.Copy).then_inc(s_dptk, 1)

            def gates(hh, part):
                z, temp = gate_bufs[hh]
                for c in range(NCH if part == 0 else 0):
                    act.wait_ge(s_z, 3 * hh + c + 1)
                    if hh == 0 and c == 0:
                        act.wait_ge(s_pt, NBLK)
                        act.wait_ge(s_po, NBLK)
                    elif hh == 1 and c == 0:
                        act.wait_ge(s_spill[0], 48)
                        act.wait_ge(s_spill[1], 48)
                    elif c == 0:
                        act.wait_ge(s_bc, NBLK * hh)
                        act.wait_ge(s_as, hh)
                    nc.scalar.activation(z[:, chunk(c)], banks[(3 if hh == 0 else 4) + c][:, 0:CH], ACT.Identity,
                                         bias=gain[:, G_BIAS + hh:G_BIAS + hh + 1]).then_inc(s_zb, 1)
                if part == 1:
                    act.wait_ge(s_zb, 3 * hh + 3)
                    nc.scalar.activation(temp, z, ACT.Abs).then_inc(s_zt, 1)
                    act.wait_ge(s_zt, 3 * hh + 1)
                    nc.scalar.activation(temp, temp, ACT.Exp, scale=-1.0).then_inc(s_zt, 1)
                if part == 2:
                    act.wait_ge(s_zt, 3 * hh + 2)
                    nc.scalar.activation(temp, temp, ACT.Ln, bias=1.0).then_inc(s_zt, 1)

            def sample_decay(hh):
                act.wait_ge(s_la, hh + 1)
                nc.scalar.activation(a_smp[:, hh], gate_bufs[hh][0][:, SEQ:T], ACT.Exp, scale=1.0 / TAU).then_inc(s_as, 1)

            for n, (t, c) in enumerate(STEPS_A):
                rows, scale = P, 1.0
                if t in A_Q:
                    dst, scale = q_a[:, t - A_Q[0], chunk(c)], float(P) ** -0.5
                elif t in A_K:
                    dst = k_a[:, t - A_K[0], chunk(c)]
                elif t in A_V or t in A_G:
                    i = t - A_V[0]
                    dst = ring[:, i % 2, chunk(c)]
                    if c == 0 and 2 <= i < 8:
                        act.wait_ge(s_vT, 3 * (i - 1))
                    if c == 0 and i >= 8:
                        act.wait_ge(s_spill[i % 2], 16 * (i // 2 - 3))
                elif t in A_R:
                    dst, rows = glr[:, chunk(c)], 16
                else:
                    dst = mq_a[:, t - A_M[0], chunk(c)]
                if n == 9:
                    act.wait_ge(s_out, 32)
                    act.dma_start(gate2[:], gate2_d).then_inc(s_gate2, 16)
                tile_ready(act, MM_AIN, U_AIN, t, c)
                nc.scalar.activation(dst, banks[n % 3][0:rows, 0:CH], ACT.Copy, scale=scale).then_inc(s_ev, 1)
                if n < len(HEAD_A):
                    if HN_MK + n >= 4:
                        act.wait_ge(s_ev, 8 + n + 1)
                    head_square(HN_MK + n, HEAD_A[n][0])
                if n == 0:
                    norm_rstd(NORM_A1 + 2, CH, rstd_b)
                if 1 <= n <= len(HEAD_A):
                    head_rstd(HN_MK + n - 1, HEAD_A[n - 1][0].shape[1])
                if n == 1:
                    norm_hi(NORM_A1 + 2, x_hi[:, :, chunk(2)])
                if n == 5:
                    act.wait_ge(s_hn, HN_MK + 4)
                    act.dma_start(mk_d, mk_t[:]).then_inc(s_out, 16)
                mem_attention(0, n)
                if 1 <= n - GATE_STEP <= 3:
                    gates(0, n - GATE_STEP - 1)
                if n == GATE_STEP + 6:
                    sample_decay(0)
                if t in A_G and c == NCH - 1:
                    act.wait_ge(s_ev, 8 + 3 * (t + 1))
                    i = t - A_V[0]
                    act.dma_start(g_spill[:, t - A_G[0]], ring[:, i % 2]).then_inc(s_spill[i % 2], 16)
            act.wait_ge(s_wused, U_AIN + NA_IN)
            act.wait_ge(s_ev, 8 + 3 * NA_IN)
            act.dma_start(lvl_raw[:], lvl_d).then_inc(s_lvl_in, 16)
            act.dma_start(ck[:], cmk_d[0]).then_inc(s_cache, 16)
            for kt in range(2):
                act.dma_start(cv[kt][:], cmv_d[0, :, kt]).then_inc(s_cache, 16)

            def keys_kept(hh):
                act.wait_ge(s_ss, NSTEP * (hh + 1))
                if hh >= 1:
                    act.wait_ge(s_kv, NBLK * hh)
                n = NSTEP * hh + NLEV + 1
                for b in range(2):
                    nc.scalar.activation(k_tok[:, 4 * b:4 * b + 4], banks[2 * (n % 2) + b][:].rearrange("p (j m) -> p j m", j=4), ACT.Copy).then_inc(s_kt, 1)

            def outs_kept(hh):
                half = slice(HD * (hh % 2), HD * (hh % 2) + HD)
                act.wait_ge(s_go, hh + 1)
                for b in range(2):
                    nc.scalar.activation(o_a[:, hh, b * 512:(b + 1) * 512], banks[4 + b][:], ACT.Copy).then_inc(s_oe, 1)
                    nc.scalar.activation(o_a[half, 4 + hh // 2, b * 512:(b + 1) * 512], banks[6 + b][half], ACT.Copy).then_inc(s_oe, 1)

            for hh in range(H):
                for l in range(NSTEP):
                    n = NSTEP * hh + l
                    src = dec[:, n % 2]
                    if l == NLEV:
                        act.wait_ge(s_mu, n - 1)
                        src = b_cums[hh % 2][:]
                    else:
                        act.wait_ge(s_df, (NSTEP - 1) * hh + min(l, NLEV) + 1)
                    nc.scalar.activation(dec[:, n % 2], src, ACT.Exp, scale=1.0 / TAU).then_inc(s_ex, 1)
                    if l == 0 and hh >= 1:
                        keys_kept(hh - 1)
                    if l == 1:
                        if hh >= 1:
                            act.wait_ge(s_st, NBLK * hh)
                        nc.scalar.activation(b_end[:], b_cums[hh % 2][:, P - 1::P], ACT.Exp, scale=1.0 / TAU).then_inc(s_be, 1)
                        if hh >= 1:
                            act.dma_start(gstate_d[hh - 1], st[:, NBLK - 1]).then_inc(s_gst, 16)
                    if l == 2 and hh >= 1:
                        outs_kept(hh - 1)
                    if hh == 0 and l in (3, 5):
                        mem_samples(0, l // 2 - 1)
                    if 3 <= l <= 5 and hh + 1 < H:
                        gates(hh + 1, l - 3)
                    if l == 7 and hh + 1 < H:
                        sample_decay(hh + 1)
            keys_kept(H - 1)
            act.wait_ge(s_st, NBLK * H)
            act.dma_start(gstate_d[H - 1], st[:, NBLK - 1]).then_inc(s_gst, 16)
            outs_kept(H - 1)
            act.wait_ge(s_cp, NBLK * H)
            act.wait_ge(s_go, H)
            act.wait_ge(s_gst, 16 * H)
            act.dma_start(st_smp[:], state_d.rearrange("h p b e -> p h b e")).then_inc(s_sin, 16)
            act.dma_start(g_a[:], g_spill).then_inc(s_gland, 16)

            def out_norm(c):
                if c >= 1:
                    act.wait_ge(s_osum, H * c)
                nc.scalar.activation(o_sq[:], o_a[:, :, chunk(c)], ACT.Square).then_inc(s_osq, 1)
                if c >= 1:
                    act.wait_ge(s_onm, c)
                for r in range(H):
                    act.wait_ge(s_osum, H * c + r + 1)
                    nc.scalar.activation(o_rs[:, r], banks[r + 4 * (c // 2)][:, 0:CH], ACT.Ln, scale=1.0 / DV, bias=EPS).then_inc(s_oln, 1)
                act.wait_ge(s_oln, H * (c + 1))
                nc.scalar.activation(o_rs[:], o_rs[:], ACT.Exp, scale=-0.5).then_inc(s_ors, 1)

            act.wait_ge(s_oe, 4 * H)
            act.wait_ge(s_skt, 1)
            act.wait_ge(s_as, H)
            out_norm(0)
            for hh in range(H):
                half = slice(HD * (hh % 2), HD * (hh % 2) + HD)
                act.wait_ge(s_sn, 8 * (hh + 1))
                act.dma_start(sstate_d[hh], st_smp[:, hh]).then_inc(s_sout, 16)
                act.wait_ge(s_so, hh + 1)
                nc.scalar.activation(o_a[:, hh, SEQ:T], banks[4 * (hh % 2)][:, 0:NB], ACT.Copy).then_inc(s_soe, 1)
                nc.scalar.activation(o_a[half, 4 + hh // 2, SEQ:T], banks[4 * (hh % 2) + 1][half, 0:NB], ACT.Copy).then_inc(s_soe, 1)
                if hh == 1:
                    act.wait_ge(s_gland, 16)
                    nc.scalar.activation(g_a[:], g_a[:], ACT.Silu).then_inc(s_gsil, 1)
                    nc.scalar.preload_act_table_set("natural_log_exp_and_others")
                if hh == 2:
                    out_norm(1)
            def mix_hi(c):
                act.wait_ge(s_tok, c + 1)
                nc.scalar.activation(x_hi[:, 0:6, chunk(c)], tok_a[:, :, chunk(c)], ACT.Copy).then_inc(s_chi, 1)
                nc.scalar.activation(x_hi[:, 6:8, chunk(c)], mq_a[:, :, chunk(c)], ACT.Copy).then_inc(s_chi, 1)

            act.wait_ge(s_soe, 2 * H)
            act.wait_ge(s_sout, 16 * H)
            mix_hi(0)
            out_norm(2)
            mix_hi(1)
            act.wait_ge(s_onm, NCH)
            act.dma_start(h[:, 2:KT], x_d[:, 2:KT]).then_inc(s_h, 16)
            mix_hi(2)
            act.wait_ge(s_clo, 2 * NCH)
            act.dma_start(h[:, 0:2], x_d[:, 0:2]).then_inc(s_h, 16)

            def residual_squares(L, order):
                for n, (t, c) in enumerate(order):
                    act.wait_ge(s_res, 24 * L + n + 1)
                    a = sum(1 for t0, _ in order[:max(n - 4, 0)] if t0 > 0)
                    if a:
                        act.wait_ge(s_tacc, 18 * L + a)
                    nc.scalar.activation(sq[:, c] if t == 0 else sq[:, 3 + n % 5], h[:, t, chunk(c)], ACT.Square).then_inc(s_tsq, 1)

            residual_squares(0, STEPS_AO)

            def norm_after_residual(norm):
                norm_rstd(norm, CH, rstd)
                norm_rstd(norm + 1, CH, rstd)
                norm_hi(norm, x_hi[:, :, chunk(0)])
                norm_rstd(norm + 2, CH, rstd)
                norm_hi(norm + 1, x_hi[:, :, chunk(1)])
                norm_hi(norm + 2, x_hi[:, :, chunk(2)])

            def swiglu(L, norm, u0, mm0):
                norm_after_residual(norm)

                def step(j, first=False):
                    def at_(base, k):
                        return base if first else k * j + base
                    for f in range(2):
                        for c in range(NCH):
                            if c < NCH - 1:
                                act.wait_ge(s_mm, at_(mm0 + (2 * c + 1 if first and f == 0 else 4 * f + c + 1), MM_FF))
                            else:
                                act.wait_ge(s_wused, at_(u0 + 2 * f + 1, 6))
                            done = 6 * JFF * L + 3 * f + c - 2
                            if done > 0 or not first:
                                act.wait_ge(s_hid, at_(done, 6))
                            nc.scalar.activation(sil[:, c], banks[c][:, 0:CH], ACT.Silu).then_inc(s_sil, 1)
                        for c in range(NCH):
                            act.wait_ge(s_hid, at_(6 * JFF * L + 3 * f + c + 1, 6))
                            nc.scalar.activation(hid_hi[:, f, chunk(c)], hid[:, c], ACT.Copy).then_inc(s_hhi, 1)

                step(0, first=True)
                with act.Fori(1, JFF) as j:
                    step(j)

            swiglu(0, NORM_A2, U_FFA, MM_FFA)
            nc.scalar.preload_act_table_set("natural_log_exp_and_others")

            def norm_square(c):
                act.wait_ge(s_down, 24 * (JFF - 1) + KT * (c + 1))
                square(SQ_KV + c, NORM_KV + c, h[:, :, chunk(c)], CH)
            norm_square(0)
            norm_rstd(NORM_KV, CH, rstd_b)
            norm_square(1)
            norm_hi(NORM_KV, x_hi[:, :, chunk(0)])
            norm_rstd(NORM_KV + 1, CH, rstd_b)
            norm_square(2)
            norm_hi(NORM_KV + 1, x_hi[:, :, chunk(1)])
            act.dma_start(rope[:], rope_d).then_inc(s_rope, 16)

            for n, (t, c) in enumerate(STEPS_B):
                tile_ready(act, MM_KV, U_KV, t, c)
                nc.scalar.activation(dest_b(t)[0][:, chunk(c)], banks[n % 3][:, 0:CH], ACT.Copy).then_inc(s_ev, 1)
                if n < NB_NORM:
                    act.wait_ge(s_ev, EV_KV + n + 1)
                    head_square(HN_B + n, HEAD_B[n][0])
                if n == 0:
                    norm_rstd(NORM_KV + 2, CH, rstd_b)
                if 1 <= n <= NB_NORM:
                    head_rstd(HN_B + n - 1, CH)
                if n == 1:
                    norm_hi(NORM_KV + 2, x_hi[:, :, chunk(2)])
                mem_attention(1, n)
                if n == NB_NORM + 2:
                    act.wait_ge(s_hn, HN_B + NB_NORM)
                    act.dma_start(tri_raw[:], tri_d).then_inc(s_tri_in, 16)
            act.wait_ge(s_wused, U_KV + NB_IN)
            act.wait_ge(s_ev, EV_END)
            act.dma_start(ck[:], cmk_d[1]).then_inc(s_cache, 16)
            for kt in range(2):
                act.dma_start(cv[kt][:], cmv_d[1, :, kt]).then_inc(s_cache, 16)
            act.dma_start(vwin_d, v_b[:]).then_inc(s_out, 16)
            act.wait_ge(s_rok, len(ROPE_B))
            act.dma_start(kwin_d, k_b[:]).then_inc(s_out, 16)
            for part in range(2):
                mem_samples(1, part)
            act.wait_ge(s_dpo, 3)
            act.dma_start(wk[:, :, :, :, 0:P], wink_d).then_inc(s_wc, 16)
            act.dma_start(wv[:], winv_d).then_inc(s_wc, 16)
            act.wait_ge(s_db, 1)
            nc.scalar.activation(pd[:], banks[4][0:32, 0:3 * NWIN].rearrange("p (g m) -> p g m", g=3), ACT.Exp, scale=HD ** -0.5,
                                 bias=wst[:, 1:2], accum_out=wst[:, 2:3]).then_inc(s_de, 1)
            act.wait_ge(s_dpt_, 1)
            nc.scalar.activation(diagonal(pw_blk, [P, 3]), banks[5][:, 0:96].rearrange("p (g b m) -> p g b m", g=3, b=NB), ACT.Copy).then_inc(s_dptk_, 1)
            act.wait_ge(s_do, 2)
            act.dma_start(sel_raw[:], sel_d).then_inc(s_sel_in, 16)

            for i in range(NW * H):
                hh, w = i // NW, i % NW
                act.wait_ge(s_w2, i + 1)
                if i >= 2:
                    act.wait_ge(s_wo, i - 1)
                n = len(W_STEPS[w][1])
                nc.scalar.activation(pw[:, i % 2, 0:n], banks[i % 4][:, 0:n * P].rearrange("p (n m) -> p n m", n=n), ACT.Exp,
                                     scale=HD ** -0.5).then_inc(s_we, 1)
                if w == 1 and hh >= 1 or i == NW * H - 1:
                    done = hh if w == 1 else hh + 1
                    act.wait_ge(s_wo, NW * done)
                    if done >= 2:
                        act.wait_ge(s_wod, NCH * (done - 1))
                    for b in range(2):
                        nc.scalar.activation(o_sb[:, 512 * b:512 * b + 512], banks[4 + b][:], ACT.Copy).then_inc(s_woc, 1)
            for c in range(NCH):
                act.wait_ge(s_wod, NCH * (H - 1) + c + 1)
                nc.scalar.activation(x_hi[:, 0:2, chunk(c)], tok_b[:, :, chunk(c)], ACT.Copy).then_inc(s_chi, 1)
                nc.scalar.activation(x_hi[:, 2:4, chunk(c)], mq_b[:, :, chunk(c)], ACT.Copy).then_inc(s_chi, 1)
            residual_squares(1, STEPS_BO)
            swiglu(1, NORM_B2, U_FFB, MM_FFB)
            for c in range(NCH):
                act.wait_ge(s_down, 48 * JFF - KT * (NCH - 1 - c))
                act.dma_start(y_d[:, :, chunk(c)], h[:, :, chunk(c)]).then_inc(s_out, 16)
            act.wait_ge(s_out, 16 * 7)

        @block.vector
        def _(dve):
            def fold(i, n, width):
                v = sq[:, :, 0:width]
                dve.wait_ge(s_sq, i + 1)
                nc.vector.tensor_tensor(v[:, 0:4], v[:, 0:4], v[:, 4:8], ALU.add).then_inc(s_f1, 1)
                dve.wait_ge(s_f1, i + 1)
                nc.vector.tensor_tensor(v[:, 0:2], v[:, 0:2], v[:, 2:4], ALU.add).then_inc(s_fold, 1)

            def norm_apply(n, src, g0, rs, dst, done=s_xt):
                w = src.shape[2]
                dve.wait_ge(s_rs, n + 1)
                for k in range(KT):
                    op = nc.vector.scalar_tensor_tensor(out=dst[:, k], in0=src[:, k], scalar=gain[:, g0 + k:g0 + k + 1],
                                                        in1=rs[:, n % 2, 0:w], op0=ALU.mult, op1=ALU.mult)
                    if n and k == HK - 1:
                        op.then_inc(done, 1)
                op.then_inc(done, 1)

            def norm_lo(n, dst, hi, src):
                for half in range(2 if n else 1):
                    k = slice(HK * half, HK * (half + 1)) if n else slice(0, KT)
                    dve.wait_ge(s_hi, norm_half(n, half) if n else 1)
                    nc.vector.tensor_tensor(dst[:, k], src[:, k], hi[:, k].bitcast(F32), ALU.subtract).then_inc(s_lo, 1)

            def apply_chunk(n, c, g0, rs):
                if n >= 1:
                    dve.wait_ge(s_lo, norm_half(n - 1, 1))
                norm_apply(n, h[:, :, chunk(c)], g0, rs, xt)

            def lo_chunk(n, c):
                norm_lo(n, x_lo[:, :, chunk(c)], x_hi[:, :, chunk(c)], xt[:])

            def head_apply(i, src, g, dst):
                dve.wait_ge(s_hrs, i + 1)
                nc.vector.scalar_tensor_tensor(out=dst, in0=src, scalar=gain[:, g:g + 1], in1=rstd[:, i % 2, 0:src.shape[1]],
                                               op0=ALU.mult, op1=ALU.mult).then_inc(s_hn, 1)

            dve.wait_ge(s_gain, 16)
            dve.wait_ge(s_mem, 16)
            fold(0, 0, MEM)
            norm_apply(0, mt, G_MN, rstd, mem_xt[:, 0], s_mx0)
            norm_apply(0, mt, G_MN + KT, rstd, mem_xt[:, 1])
            first, second = slice(T - 2 * MEM, T - MEM), slice(T - MEM, T)
            dve.wait_ge(s_mh0, 1)
            nc.vector.tensor_tensor(x_lo[:, :, first], mem_xt[:, 0], x_hi[:, :, first].bitcast(F32), ALU.subtract).then_inc(s_ml0, 1)
            norm_lo(0, x_lo[:, :, second], x_hi[:, :, second], mem_xt[:, 1])
            for c in range(NCH):
                dve.wait_ge(s_x[c], 16)
            fold(SQ_A1, NORM_A1, CH)
            apply_chunk(NORM_A1, 0, G_N1, rstd_b)
            fold(SQ_A1 + 1, NORM_A1 + 1, CH)
            lo_chunk(NORM_A1, 0)
            apply_chunk(NORM_A1 + 1, 1, G_N1, rstd_b)
            fold(SQ_A1 + 2, NORM_A1 + 2, CH)
            lo_chunk(NORM_A1 + 1, 1)

            def mem_attention(L, mq, n):
                if n in MEM_AT[L]:
                    a = NBLK * L + MEM_AT[L].index(n)
                    dve.wait_ge(s_sc, a + 1)
                    if a >= 1:
                        dve.wait_ge(s_pe, a)
                        dve.wait_ge(s_nb, a)
                    for par in range(2):
                        nc.vector.tensor_reduce(nmax[:, 2 * par:2 * par + 2], banks[3 + par][:].rearrange("p (r m) -> p r m", r=2),
                                                AX.X, ALU.max, negate=True).then_inc(s_mx, 1)
                    dve.wait_ge(s_mx, 2 * a + 2)
                    nc.vector.tensor_scalar(nbias, nmax, HD ** -0.5, None, ALU.mult).then_inc(s_nb, 1)
                if n - 1 in MEM_AT[L]:
                    a = NBLK * L + MEM_AT[L].index(n - 1)
                    dve.wait_ge(s_pe, a + 1)
                    if a >= 1:
                        dve.wait_ge(s_pn, a)
                    nc.vector.reciprocal(rsums, psums).then_inc(s_ra, 1)
                    dve.wait_ge(s_ra, a + 1)
                    for j in range(H):
                        op = nc.vector.tensor_scalar(mem_pr[L][:, j], mem_pr[L][:, j], rsums[:, j:j + 1], None, ALU.mult)
                    op.then_inc(s_pn, 1)
                if n - 4 in MEM_AT[L]:
                    i = MEM_AT[L].index(n - 4)
                    dve.wait_ge(s_po, NBLK * L + i + 1)
                    nc.vector.tensor_copy(mq[:, :, i * P:(i + 1) * P], banks[5][:, 0:2 * P].rearrange("p (r m) -> p r m", r=2)).then_inc(s_pok, 1)

            def cumulate(hh):
                z, temp = gate_bufs[hh]
                dve.wait_ge(s_zt, 3 * hh + 3)
                nc.vector.scalar_tensor_tensor(out=z, in0=z, scalar=0.0, in1=temp, op0=ALU.min, op1=ALU.subtract).then_inc(s_la, 1)
                dve.wait_ge(s_la, hh + 1)
                if hh == 1:
                    dve.wait_ge(s_lvl, 1)
                for b in range(NBLK):
                    cols = slice(b * P, (b + 1) * P)
                    nc.vector.tensor_tensor_scan(b_cums[hh % 2][:, cols], ones, z[:, cols], 0.0, ALU.mult, ALU.add).then_inc(s_bc, 1)

            for n in range(3 * NA_IN):
                if 1 <= n <= len(HEAD_A):
                    head_apply(HN_MK + n - 1, *HEAD_A[n - 1])
                if n == 0:
                    apply_chunk(NORM_A1 + 2, 2, G_N1, rstd_b)
                if n == 1:
                    lo_chunk(NORM_A1 + 2, 2)
                if n in MEM_TURN:
                    i = MEM_TURN.index(n)
                    dve.wait_ge(s_mvT, i + 1)
                    nc.vector.tensor_copy(mv_t[:, i // 2, i % 2], banks[3 + i % 2][:, 0:MEM]).then_inc(s_mvt, 1)
                mem_attention(0, mq_a, n)
                if n == GATE_STEP + 4:
                    cumulate(0)
                i, b = divmod(n - 3 * (A_V[0] + 1), 3)
                if 0 <= i < 6:
                    dve.wait_ge(s_vT, 3 * i + b + 1)
                    if b < 2:
                        nc.vector.tensor_copy(v_tok[:, 4 * b:4 * b + 4, i * P:(i + 1) * P], banks[7][:].rearrange("p (j m) -> p j m", j=4)).then_inc(s_vt, 1)
                    else:
                        nc.vector.tensor_copy(vs_a[:, i * P:(i + 1) * P], banks[7][0:NB, 0:P]).then_inc(s_vt, 1)

            def mem_samples(L, mq, used, part):
                sel = (slice(0, HD), slice(HD, P))
                if part == 0:
                    dve.wait_ge(s_wused, used)
                    nc.vector.memset(q_blk[:], 0.0).then_inc(s_qz, 1)
                    nc.vector.memset(p_blk[:], 0.0).then_inc(s_qz, 1)
                    dve.wait_ge(s_qz, 2 * L + 2)
                    for t in range(2):
                        for par in range(2):
                            diag = bass.AP(q_blk[sel[par], t].tensor, q_blk[sel[par], t].offset + 2 * t + par, [[2 * NB * 32, HD], [36, NB]])
                            nc.vector.tensor_copy(diag, mq[sel[par], t, SEQ:T]).then_inc(s_qb, 1)
                if part == 1:
                    dve.wait_ge(s_dsc, L + 1)
                    nc.vector.tensor_reduce(dst4[:, 0:1], banks[7][0:32, 0:MEM], AX.X, ALU.max, negate=True).then_inc(s_dmx, 1)
                    dve.wait_ge(s_dmx, L + 1)
                    nc.vector.tensor_scalar(dst4[:, 1:2], dst4[:, 0:1], HD ** -0.5, None, ALU.mult).then_inc(s_dnb, 1)
                if part == 2:
                    dve.wait_ge(s_dpe, L + 1)
                    nc.vector.reciprocal(dst4[:, 3:4], dst4[:, 2:3]).then_inc(s_dra, 1)
                    dve.wait_ge(s_dra, L + 1)
                    nc.vector.tensor_scalar(dp[:], dp[:], dst4[:, 3:4], None, ALU.mult).then_inc(s_dpn, 1)
                if part == 3:
                    dve.wait_ge(s_dpo, 2 * L + 1)
                    nc.vector.tensor_tensor(dp[:], banks[7][0:32, 0:MEM], smp_head.rearrange("p t m -> p (t m)"), ALU.mult).then_inc(s_dpn, 1)
                if part == 4:
                    dve.wait_ge(s_dpo, 2 * L + 2)
                    nc.vector.tensor_copy(mq[:, :, SEQ:T], banks[7][:, MEM + 64:MEM + 80].rearrange("p (t b) -> p t b", t=2)).then_inc(s_dpok, 1)

            dve.wait_ge(s_lvl_in, 16)
            nc.vector.tensor_copy(lvl[:], lvl_raw[:]).then_inc(s_lvl, 1)
            dve.wait_ge(s_wused, U_AIN + NA_IN)
            for hh in range(2):
                nc.vector.memset(s_accs[hh][:], 0.0).then_inc(s_sz, 1)

            def decayed(hh, l):
                n = NSTEP * hh + l
                dve.wait_ge(s_ex, n + 1)
                if l == NLEV:
                    dve.wait_ge(*((s_go, hh) if hh >= 1 else (s_dpo, 1)))
                    nc.vector.tensor_tensor(q_dec[:], q_a[:, hh, 0:SEQ], dec[:, n % 2], ALU.mult).then_inc(s_mu, 1)
                    return
                if n >= 2:
                    dve.wait_ge(s_ss, n - 1)
                if l == NLEV + 1:
                    nc.vector.tensor_tensor(dqk[:, n % 2], k_a[:, hh, 0:SEQ], dec[:, n % 2], ALU.mult).then_inc(s_mu, 1)
                    return
                s = 2 ** l
                elo, ehi = halves(dec[:, n % 2], s)
                xlo, xhi = halves(dqk[:, n % 2], s)
                nc.vector.tensor_tensor(xlo, halves(k_a[:, hh, 0:SEQ], s)[0], elo, ALU.mult)
                nc.vector.tensor_tensor(xhi, halves(q_a[:, hh, 0:SEQ], s)[1], ehi, ALU.mult).then_inc(s_mu, 1)

            def keep(hh, l):
                n = NSTEP * hh + l
                dve.wait_ge(s_ss, n + 1)
                if l == 0 and hh >= 2:
                    dve.wait_ge(s_go, hh - 1)
                if l == 0:
                    dve.wait_ge(s_sz, 2)
                    dve.wait_ge(s_lvl, 1)
                if NBLK * hh + l >= 1:
                    dve.wait_ge(s_cp, NBLK * hh + l)
                if l < NLEV:
                    s = 2 ** l
                    for b in range(2):
                        into = s_accs[hh % 2][:, 4 * b:4 * b + 4].rearrange("p b (n h s) -> p b n h s", h=2, s=s)[:, :, :, 1]
                        mask = halves(lvl[:, l], s)[1].unsqueeze(1).broadcast_to(list(into.shape))
                        scores = banks[2 * (n % 2) + b][:].rearrange("p (b n h s) -> p b n h s", b=4, h=2, s=s)[:, :, :, 1]
                        op = nc.vector.copy_predicated(into, mask, scores)
                    op.then_inc(s_cp, 1)
                    return
                for b in range(2):
                    op = nc.vector.copy_predicated(s_accs[hh % 2][:, 4 * b:4 * b + 4], lvl[:, l:l + 1].broadcast_to([P, 4, P]),
                                                   banks[2 * (n % 2) + b][:].rearrange("p (j m) -> p j m", j=4))
                op.then_inc(s_cp, 1)

            def states(hh):
                for b in range(NBLK):
                    dve.wait_ge(s_kv, NBLK * hh + 2 * (b // 2) + 2)
                    up = banks[4 + b // 2][:, (b % 2) * DV:(b % 2 + 1) * DV]
                    if b == 0:
                        if hh >= 1:
                            dve.wait_ge(s_gst, 16 * hh)
                            dve.wait_ge(s_go, hh)
                        nc.vector.tensor_copy(st[:, 0], up).then_inc(s_st, 1)
                        dve.wait_ge(s_be, hh + 1)
                    else:
                        dve.wait_ge(s_st, NBLK * hh + b)
                        nc.vector.scalar_tensor_tensor(out=st[:, b], in0=st[:, b - 1], scalar=b_end[:, b:b + 1], in1=up,
                                                       op0=ALU.mult, op1=ALU.add).then_inc(s_st, 1)

            mem_samples(0, mq_a, U_AIN + NA_IN, 0)
            for hh in range(H):
                for l in range(NSTEP):
                    decayed(hh, l)
                    if l == 6 and hh + 1 < H:
                        cumulate(hh + 1)
                    if hh == 0 and l in (3, 4, 7, 8):
                        mem_samples(0, mq_a, U_AIN + NA_IN, {3: 1, 4: 2, 7: 3, 8: 4}[l])
                    if 1 <= l:
                        keep(hh, l - 1)
                    if l == 1 and hh >= 1:
                        states(hh - 1)
            states(H - 1)

            def out_apply(c):
                dve.wait_ge(s_ors, c + 1)
                for r in range(H):
                    nc.vector.scalar_tensor_tensor(out=o_a[:, r, chunk(c)], in0=o_a[:, r, chunk(c)], scalar=gain[:, G_ON:G_ON + 1],
                                                   in1=o_rs[:, r], op0=ALU.mult, op1=ALU.mult)
                for r in range(H):
                    half = slice(HD * (r % 2), HD * (r % 2) + HD)
                    x = o_a[half, 4 + r // 2, chunk(c)]
                    op = nc.vector.scalar_tensor_tensor(out=x, in0=x, scalar=gain[half, G_ON + 1:G_ON + 2],
                                                        in1=o_rs[half, r], op0=ALU.mult, op1=ALU.mult)
                op.then_inc(s_onm, 1)

            dve.wait_ge(s_skt, 1)
            nc.vector.tensor_copy(k_smp[:], banks[4][0:NB, :].rearrange("p (h m) -> p h m", h=H)).then_inc(s_skk, 1)
            dve.wait_ge(s_skk, 1)
            dve.wait_ge(s_go, H)
            dve.wait_ge(s_gst, 16 * H)
            for hh in range(H):
                nc.vector.tensor_tensor(k_one[:, hh], k_smp[:, hh:hh + 1].broadcast_to([NB, NB, P]),
                                        ident[0:NB, 0:NB].unsqueeze(2).broadcast_to([NB, NB, P]), ALU.mult).then_inc(s_sk1, 1)
            out_apply(0)
            dve.wait_ge(s_sin, 16)
            dve.wait_ge(s_as, H)
            for hh in range(H):
                dve.wait_ge(s_su, hh + 1)
                for b in range(NB):
                    nc.vector.scalar_tensor_tensor(out=st_smp[:, hh, b], in0=st_smp[:, hh, b], scalar=a_smp[:, hh, b:b + 1],
                                                   in1=banks[4 * (hh % 2) + b // 2][:, (b % 2) * DV:(b % 2 + 1) * DV],
                                                   op0=ALU.mult, op1=ALU.add).then_inc(s_sn, 1)

            dve.wait_ge(s_gsil, 1)
            for c in range(NCH + 1):
                if 1 <= c < NCH:
                    out_apply(c)
                if c < NCH:
                    dve.wait_ge(s_onm, c + 1)
                    nc.vector.tensor_tensor(tok_a[:, :, chunk(c)], o_a[:, :, chunk(c)], g_a[:, :, chunk(c)], ALU.mult).then_inc(s_tok, 1)
                if c < 1:
                    continue
                c -= 1
                dve.wait_ge(s_chi, 2 * c + 2)
                nc.vector.tensor_tensor(x_lo[:, 0:6, chunk(c)], tok_a[:, :, chunk(c)], x_hi[:, 0:6, chunk(c)].bitcast(F32), ALU.subtract).then_inc(s_clo, 1)
                nc.vector.tensor_tensor(x_lo[:, 6:8, chunk(c)], mq_a[:, :, chunk(c)], x_hi[:, 6:8, chunk(c)].bitcast(F32), ALU.subtract).then_inc(s_clo, 1)

            def add_residual(order, mm0, u0, per_unit, n0):
                L = n0 // 24
                mm = a = 0
                for n in range(len(order) + 2):
                    if n < len(order):
                        t, c = order[n]
                        if c < NCH - 1 or t % per_unit < per_unit - 1:
                            mm += 1
                            dve.wait_ge(s_mm, mm0 + mm)
                        else:
                            dve.wait_ge(s_wused, u0 + t // per_unit + 1)
                        nc.vector.tensor_tensor(h[:, t, chunk(c)], h[:, t, chunk(c)], banks[n % 6][:, 0:CH], ALU.add).then_inc(s_res, 1)
                    m = n - 2
                    if m >= 0 and order[m][0] > 0:
                        acc = sq[:, order[m][1]]
                        dve.wait_ge(s_tsq, n0 + m + 1)
                        if a >= 1:
                            dve.wait_ge(s_tacc, 18 * L + min(a, 18))
                        nc.vector.tensor_tensor(acc, acc, sq[:, 3 + m % 5], ALU.add).then_inc(s_tacc if a < 18 else s_fold, 1)
                        a += 1

            dve.wait_ge(s_h, 32)
            add_residual(STEPS_AO, MM_AOUT, U_AOUT, 1, 0)

            def swiglu(L, norm, g0, u0, mm0, last_norm):
                for c in range(NCH):
                    apply_chunk(norm + c, c, g0, rstd)
                    lo_chunk(norm + c, c)

                def step(j, first=False, last=False):
                    def at_(base, k):
                        return base if first else k * j + base
                    for f in range(2):
                        for c in range(NCH + 1):
                            if c < NCH:
                                i = 6 * JFF * L + 3 * f + c
                                dve.wait_ge(s_sil, at_(i + 1, 6))
                                if c < NCH - 1:
                                    dve.wait_ge(s_mm, at_(mm0 + (2 * c + 2 if first and f == 0 else 4 * f + 2 + c + 1), MM_FF))
                                else:
                                    dve.wait_ge(s_wused, at_(u0 + 2 * f + 2, 6))
                                if i >= 3 or not first:
                                    dve.wait_ge(s_hlo, at_(i - 2, 6))
                                nc.vector.tensor_tensor(hid[:, c], sil[:, c], banks[3 + c][:, 0:CH], ALU.mult).then_inc(s_hid, 1)
                            if c >= 1:
                                i = 6 * JFF * L + 3 * f + c - 1
                                dve.wait_ge(s_hhi, at_(i + 1, 6))
                                nc.vector.tensor_tensor(hid_lo[:, f, chunk(c - 1)], hid[:, c - 1], hid_hi[:, f, chunk(c - 1)].bitcast(F32),
                                                        ALU.subtract).then_inc(s_hlo, 1)
                    for c in range(NCH):
                        for m in range(KT):
                            n = KT * c + m
                            if n < 23:
                                dve.wait_ge(s_mm, at_(mm0 + 8 + n + 1, MM_FF))
                            else:
                                dve.wait_ge(s_wused, at_(u0 + 6, 6))
                            i = 24 * JFF * L + n
                            if not first:
                                dve.wait_ge(s_down, at_(i - 23, 24))
                            nc.vector.tensor_tensor(h[:, m, chunk(c)], h[:, m, chunk(c)], banks[n % 6][:, 0:CH], ALU.add).then_inc(s_down, 1)
                            if last:
                                last_norm(n)

                step(0, first=True)
                with dve.Fori(1, JFF - 1) as j:
                    step(j)
                step(JFF - 1, last=True)

            def wide_apply(n, c):
                dve.wait_ge(s_lo, norm_half(n - 1, 1))
                dve.wait_ge(s_rs, n + 1)
                for half in range(2):
                    k = slice(HK * half, HK * (half + 1))
                    nc.vector.tensor_tensor(xt[:, k], h[:, k, chunk(c)], rstd_b[:, n % 2:n % 2 + 1].broadcast_to([P, HK, CH]), ALU.mult).then_inc(s_xt, 1)

            def norm_in_last_step(n):
                if n == KT + 3:
                    fold(SQ_KV, NORM_KV, CH)
                if n == 2 * KT + 1:
                    wide_apply(NORM_KV, 0)
                if n == 2 * KT + 5:
                    fold(SQ_KV + 1, NORM_KV + 1, CH)

            swiglu(0, NORM_A2, G_N2, U_FFA, MM_FFA, norm_in_last_step)
            lo_chunk(NORM_KV, 0)
            wide_apply(NORM_KV + 1, 1)
            fold(SQ_KV + 2, NORM_KV + 2, CH)
            lo_chunk(NORM_KV + 1, 1)
            dve.wait_ge(s_rope, 16)

            for n in range(3 * NB_IN):
                if n == 0:
                    wide_apply(NORM_KV + 2, 2)
                if n == 1:
                    lo_chunk(NORM_KV + 2, 2)
                if 1 <= n <= NB_NORM:
                    x, g, c = HEAD_B[n - 1]
                    head_apply(HN_B + n - 1, x, g, x)
                if n - 2 in ROPE_B:
                    x, g, c = HEAD_B[n - 2]
                    i = ROPE_B.index(n - 2)
                    turned = banks[7][:, 0:CH]
                    dve.wait_ge(s_rsw, i + 1)
                    nc.vector.tensor_tensor(x, x, rope[:, 0, chunk(c)], ALU.mult).then_inc(s_rc, 1)
                    nc.vector.tensor_tensor(turned, turned, rope[:, 1, chunk(c)], ALU.mult).then_inc(s_rs_, 1)
                    dve.wait_ge(s_rc, i + 1)
                    dve.wait_ge(s_rs_, i + 1)
                    nc.vector.tensor_tensor(x, x, turned, ALU.add).then_inc(s_rok, 1)
                mem_attention(1, mq_b, n)
            sel2 = (slice(0, HD), slice(HD, P))
            dve.wait_ge(s_tri_in, 16)
            nc.vector.tensor_copy(tri[:], tri_raw[:]).then_inc(s_tri, 1)

            def maxima(pair):
                i = 20 * pair
                for g in range(3):
                    per = 4 if g == 2 else 2
                    for b in range(NBLK // per):
                        for hh in (2 * pair, 2 * pair + 1):
                            dve.wait_ge(s_w1, i + 1)
                            nc.vector.tensor_reduce(m_col[:, g, hh, per * b:per * (b + 1)], banks[i % 4][:].rearrange("p (n m) -> p n m", n=per),
                                                    AX.X, ALU.max).then_inc(s_m1, 1)
                            i += 1
                    if (pair, g) in MEM_SAMPLES_AT:
                        mem_samples(1, mq_b, U_KV + NB_IN, 1 + MEM_SAMPLES_AT.index((pair, g)))
            mem_samples(1, mq_b, U_KV + NB_IN, 0)
            maxima(0)
            maxima(1)
            dve.wait_ge(s_dpok, 2)
            nc.vector.memset(qw_blk[:], 0.0).then_inc(s_wqz, 1)
            nc.vector.memset(pw_blk[:], 0.0).then_inc(s_wqz, 1)
            dve.wait_ge(s_wqz, 2)
            for g in range(3):
                for t in range(2):
                    for par in range(2):
                        v = qw_blk[sel2[par], g, t]
                        diag = bass.AP(v.tensor, v.offset + 2 * t + par, [[3 * 2 * NB * 32, HD], [36, NB]])
                        nc.vector.tensor_copy(diag, q_b[sel2[par], 2 * g + t, SEQ:T]).then_inc(s_wqb, 1)
            dve.wait_ge(s_wc, 32)
            for g in range(3):
                nc.vector.tensor_copy(wk[:, :, g, :, P], k_b[:, :, SEQ:T]).then_inc(s_wkn, 1)
            for g in range(3):
                for b in range(2):
                    n = 2 * g + b
                    dve.wait_ge(s_mt, n + 1)
                    src = banks[n % 4][0:H, :]
                    if g == 0:
                        nc.vector.tensor_copy(m_row[:, 512 * b:512 * b + 512], src).then_inc(s_mr, 1)
                        continue
                    dve.wait_ge(s_mr, n if g == 1 else 4 + b)
                    src = src.rearrange("p (n m) -> p n m", n=4)
                    nc.vector.tensor_tensor(tokens_of4(m_row[:], g, b), tokens_of4(m_row[:], g, b), src, ALU.max).then_inc(s_mr, 1)
            dve.wait_ge(s_d1, 1)
            nc.vector.tensor_reduce(wst[:, 0:1], banks[4][0:32, 0:3 * NWIN], AX.X, ALU.max, negate=True).then_inc(s_dm, 1)
            dve.wait_ge(s_dm, 1)
            nc.vector.tensor_scalar(wst[:, 1:2], wst[:, 0:1], HD ** -0.5, None, ALU.mult).then_inc(s_db, 1)
            dve.wait_ge(s_de, 1)
            nc.vector.reciprocal(wst[:, 3:4], wst[:, 2:3]).then_inc(s_dr, 1)
            dve.wait_ge(s_dr, 1)
            nc.vector.tensor_scalar(pd[:], pd[:], wst[:, 3:4], None, ALU.mult).then_inc(s_dp, 1)
            dve.wait_ge(s_dp, 1)
            nc.vector.tensor_reduce(wst[:, 4:5], pd[:, :, P], AX.X, ALU.add).then_inc(s_dpn_, 1)
            dve.wait_ge(s_dpn_, 1)
            nc.vector.tensor_scalar(wst[:, 8:16], smp_col, wst[:, 4:5], None, ALU.mult).then_inc(s_dn, 1)
            dve.wait_ge(s_dnb_, 1)
            nc.vector.tensor_tensor(v_new[:], banks[6][:, 0:2 * NB].rearrange("p (t b) -> p t b", t=2), v_b[:, :, SEQ:T], ALU.mult).then_inc(s_dvn, 1)
            dve.wait_ge(s_do, 1)
            nc.vector.tensor_tensor(w_own[:], banks[7][0:32, 0:256], smp_head.rearrange("p t m -> p (t m)"), ALU.mult).then_inc(s_dp, 1)
            dve.wait_ge(s_dvn, 1)
            dve.wait_ge(s_do, 2)
            nc.vector.tensor_tensor(tok_b[:, :, SEQ:T], banks[7][:, 256:256 + 2 * NB].rearrange("p (t b) -> p t b", t=2), v_new[:], ALU.add).then_inc(s_dok, 1)
            dve.wait_ge(s_mr, 6)
            nc.vector.tensor_scalar(nm_row[:], m_row[:], -1.0, None, ALU.mult).then_inc(s_nm, 1)
            nc.vector.memset(v3[:].rearrange("p g n (t x e) -> p (g n t) x e", t=2, e=HD)[:, :, 1], 1.0).then_inc(s_ones3, 1)
            for i in range(12):
                g, b = i // 4, i % 4
                dve.wait_ge(s_v3t, i + 1)
                nc.vector.tensor_copy(v3[:, g, 2 * b:2 * b + 2].rearrange("p n (t x e) -> p (n t) x e", t=2, e=HD)[:, :, 0::2],
                                      banks[i % 4][:].rearrange("p (n x e) -> p n x e", n=4, e=HD)).then_inc(s_v3, 1)
            dve.wait_ge(s_sel_in, 16)
            nc.vector.tensor_copy(sel[:], sel_raw[:]).then_inc(s_sel, 1)
            def mix_split(c):
                dve.wait_ge(s_chi, 2 * NCH + 2 * c + 2)
                nc.vector.tensor_tensor(x_lo[:, 0:2, chunk(c)], tok_b[:, :, chunk(c)], x_hi[:, 0:2, chunk(c)].bitcast(F32), ALU.subtract).then_inc(s_clo, 1)
                nc.vector.tensor_tensor(x_lo[:, 2:4, chunk(c)], mq_b[:, :, chunk(c)], x_hi[:, 2:4, chunk(c)].bitcast(F32), ALU.subtract).then_inc(s_clo, 1)

            for hh in range(H):
                dve.wait_ge(s_wo, NW * (hh + 1))
                for b in range(2):
                    dve.wait_ge(s_woc, 2 * hh + 2)
                    if b:
                        dve.wait_ge(s_wok, 2 * hh + 1)
                    v = tokens_of4(o_sb[:], 2, b)
                    nc.vector.tensor_tensor(v, v, banks[6 + b][:].rearrange("p (n m) -> p n m", n=4), ALU.add).then_inc(s_wok, 1)
                dve.wait_ge(s_wok, 2 * hh + 2)
                own, sums = sel2[hh % 2], sel2[1 - hh % 2]
                for c in range(NCH):
                    cols = slice(c * CH, min((c + 1) * CH, SEQ))
                    if hh >= 1:
                        dve.wait_ge(s_wod, NCH * (hh - 1) + c + 1)
                    nc.vector.reciprocal(o_rl[own, cols], o_sb[sums, cols]).then_inc(s_wor, 1)
                    dve.wait_ge(s_wor, NCH * hh + c + 1)
                    nc.vector.tensor_tensor(tok_b[own, hh // 2, cols], o_sb[own, cols], o_rl[own, cols], ALU.mult).then_inc(s_wod, 1)
                    if hh == H - 1 and c >= 1:
                        mix_split(c - 1)
            mix_split(NCH - 1)

            add_residual(STEPS_BO, MM_BOUT, U_BOUT, 2, 24)
            swiglu(1, NORM_B2, G_N2 + KT, U_FFB, MM_FFB, lambda n: None)



_OUTS = [("y", (P, KT, T)), ("gstate", (H, P, DV)), ("sstate", (H, P, NB, DV)), ("kwin", (P, 2, T)), ("vwin", (P, 2, T)),
         ("mk", (P, 2, 2, MEM)), ("mv", (P, 2, 2, MEM))]

_E_ORDER = np.concatenate([np.arange(hh * DV, hh * DV + P) for hh in range(H)]
                          + [np.arange(hh * DV + P, (hh + 1) * DV) for hh in range(H)])


def _constants():
    i = np.arange(P)
    half = i // 64
    ident = np.eye(P)
    head = (half[:, None] == half[None, :]) * 1.0
    swap = (i[:, None] == (i[None, :] ^ 32)) * 1.0
    smp = (i[:, None] // H == np.arange(NB)[None, :]) * 1.0
    smp_head = (i[:, None, None] % H == 2 * np.arange(2)[None, :, None] + half[None, None, :]).reshape(P, 2 * P) * 1.0
    cst = np.concatenate([ident, np.ones((P, P)), head, swap, smp, smp_head], axis=1).astype(np.float32)
    lvl = []
    for s in (1, 2, 4, 8, 16, 32, 64):
        same = (i[:, None] // (2 * s)) == (i[None, :] // (2 * s))
        lvl.append(same & (i[:, None] % (2 * s) < s) & (i[None, :] % (2 * s) >= s))
    lvl.append(np.eye(P, dtype=bool))
    lvl = np.stack(lvl, 1).astype(np.float32)
    ge = i[None, :] >= i[:, None]
    no = -1e30
    turn = i[:, None] % 2 == i[None, :] % 2
    tri = np.stack([ident, np.where(ge, 0, no), np.where(ge.T, 0, no),
                    np.where(ge & turn, 0, no), np.where(ge.T & turn, 0, no)], 1).astype(np.float32)
    sel = np.zeros((H, H, P), np.float32)
    for hh in range(H):
        sel[hh, hh] = 1.0
    pos = np.concatenate([np.arange(SEQ), np.full(NB, 2048)]).astype(np.float32)
    half_n = HD // 2
    inv = (10000.0 ** (-np.arange(half_n) / half_n)).astype(np.float32)
    ang = (pos[None, :] * inv[:, None].astype(np.float32)).astype(np.float32)
    cos, sin = np.cos(ang), np.sin(ang)
    rope = np.stack([np.concatenate([cos] * 4), np.concatenate([-sin, sin] * 2)], 1).astype(np.float32)
    return cst, lvl, tri, sel, rope


def _tiles(w):
    k, n = w.shape
    if n % P:
        w = np.concatenate([w, np.zeros((k, P - n % P), w.dtype)], 1)
    return w.reshape(KT, P, -1, P).transpose(2, 1, 0, 3).reshape(-1, P, KT * P)


def _ffn_units(gu, down):
    g, u = _tiles(gu[:, :FF]), _tiles(gu[:, FF:])
    d = down.reshape(FF // P, P, D)
    order = [x for j in range(JFF) for x in (g[2 * j], u[2 * j], g[2 * j + 1], u[2 * j + 1], d[2 * j], d[2 * j + 1])]
    return np.stack(order)


def _rows(a):
    return a.T.reshape(-1, P, a.shape[0]).transpose(1, 0, 2)


def kernel(x_prompt, x_sample, state_gla, cache_win_k, cache_win_v, cache_mem_k, cache_mem_v, mem_prompt,
           norm1, norm2, a_w_in, a_w_gate2, a_b_gate, a_g_onorm, a_w_out, kv_norm, w_kv, g_k, b_w_in, b_g_q,
           b_w_out, mem_norm, w_mem_kv, g_mem_q, g_mem_k, w_ffn_gu, w_ffn_down):
    import concourse.bacc as bacc
    from concourse.bass_utils import run_bass_kernel_spmd

    f = np.ascontiguousarray
    a = lambda x: np.asarray(x)
    (x_prompt, x_sample, state_gla, cache_win_k, cache_win_v, cache_mem_k, cache_mem_v, mem_prompt,
     norm1, norm2, a_w_in, a_w_gate2, a_b_gate, a_g_onorm, a_w_out, kv_norm, w_kv, g_k, b_w_in, b_g_q,
     b_w_out, mem_norm, w_mem_kv, g_mem_q, g_mem_k, w_ffn_gu, w_ffn_down) = map(a, (
         x_prompt, x_sample, state_gla, cache_win_k, cache_win_v, cache_mem_k, cache_mem_v, mem_prompt,
         norm1, norm2, a_w_in, a_w_gate2, a_b_gate, a_g_onorm, a_w_out, kv_norm, w_kv, g_k, b_w_in, b_g_q,
         b_w_out, mem_norm, w_mem_kv, g_mem_q, g_mem_k, w_ffn_gu, w_ffn_down))
    cst, lvl, tri, sel, rope = _constants()
    x = _rows(np.concatenate([x_prompt[0], x_sample[:, 0]], 0))
    w = a_w_in[0]
    q, k, v, g, r, mq = np.split(w, [512, 1024, 1792, 2560, 2576], axis=1)
    w_in = np.concatenate([mq, r, np.zeros((D, 112), w.dtype), q, k, v, g[:, _E_ORDER]], 1)
    w_out = np.concatenate([a_w_out[0][:768][_E_ORDER], a_w_out[0][768:]], 0)
    w_b = np.concatenate([b_w_in[0][:, 768:], w_kv[:, :256], b_w_in[0][:, :768], w_kv[:, 256:]], 1)
    b_out = b_w_out[0].reshape(4, P, 4, 2, P).transpose(2, 1, 3, 0, 4).reshape(4, P, 1024)
    weights = np.concatenate([_tiles(w_mem_kv[0]), _tiles(w_mem_kv[1]), _tiles(w_in), _tiles(w_out),
                              _ffn_units(w_ffn_gu[0], w_ffn_down[0]), _tiles(w_b), b_out,
                              _ffn_units(w_ffn_gu[1], w_ffn_down[1])], 0)
    assert weights.shape == (NUNIT, P, 1024)
    col = lambda v: v.reshape(-1, P).T
    two = lambda v: np.tile(v, 2)[:, None]
    gains = np.concatenate([col(norm1.reshape(-1)), col(norm2.reshape(-1)), col(kv_norm), col(mem_norm.reshape(-1)),
                            two(g_mem_q[0]), two(g_mem_q[1]), two(g_mem_k[0]), two(g_mem_k[1]), two(b_g_q[0]), two(g_k),
                            a_g_onorm[0][:P, None], two(a_g_onorm[0][P:]), col(a_b_gate[0])], 1)
    ck = cache_mem_k.reshape(2, NB, MEM, 2, P).transpose(0, 4, 3, 1, 2)
    cv = cache_mem_v.reshape(2, NB, 2, P, 256).transpose(0, 3, 2, 1, 4)
    n_past = cache_win_k.shape[1]
    rows = [n_past - dil * np.arange(1, win // dil + 1) for win, dil in GROUPS]
    wk = np.stack([cache_win_k[:, ix] for ix in rows]).reshape(3, NB, P, 2, P).transpose(4, 3, 0, 1, 2)
    wv = np.stack([cache_win_v[:, ix] for ix in rows]).reshape(3, NB, P, 256).transpose(2, 0, 1, 3)
    arrays = dict(x=x, mem=_rows(mem_prompt[0]), w=weights, cst=cst, lvl=lvl, tri=tri, gain=gains, gate2=a_w_gate2[0],
                  sel=sel, rope=rope, state=state_gla[0].transpose(1, 2, 0, 3), cmk=ck, cmv=cv, wink=wk, winv=wv)
    arrays = {f"in_{n}": f(v) for n, v in arrays.items()}
    nc = bacc.Bacc("TRN2", target_bir_lowering=False, num_devices=1)
    args = [nc.dram_tensor(n, v.shape, mybir.dt.from_np(v.dtype), kind="ExternalInput").ap() for n, v in arrays.items()]
    args += [nc.dram_tensor(f"out_{n}", s, F32, kind="ExternalOutput").ap() for n, s in _OUTS]
    trunk_program(nc, *args)
    r = run_bass_kernel_spmd(nc, [arrays], core_ids=[0]).results[0]
    y = r["out_y"].transpose(2, 1, 0).reshape(T, D)
    rows_of = lambda name: r[name].transpose(2, 1, 0).reshape(T, H, HD)
    kw, vw = rows_of("out_kwin"), rows_of("out_vwin")
    mem_out = lambda name: r[name].transpose(1, 3, 2, 0).reshape(2, 1, MEM, H, HD)
    return (y[:SEQ].reshape(1, SEQ, D), y[SEQ:].reshape(NB, 1, D),
            r["out_gstate"].reshape(1, 1, H, P, DV), r["out_sstate"].transpose(2, 0, 1, 3).reshape(1, NB, H, P, DV),
            kw[:SEQ].reshape(1, SEQ, H, HD), vw[:SEQ].reshape(1, SEQ, H, HD),
            kw[SEQ:].reshape(NB, 1, H, HD), vw[SEQ:].reshape(NB, 1, H, HD),
            mem_out("out_mk"), mem_out("out_mv"))
```
